# Optimizing a Trainium2 kernel written in Bass

```python
import jax, jax.numpy as jnp
from jax import lax
import numpy as np

D_MODEL = 1024
BATCH = 1
SEQ = 256
DEPTH = 2

HEAD_DIM = 64
SWA_Q_HEADS = 8
SWA_KV_HEADS = 2
SWA_WINDOW = 128
MOBA_HEADS = 8
MOBA_BLOCK = 256
MOBA_TOPK = 3
MOBA_Q_CHUNK = 32
D_FF = 4 * D_MODEL
ROPE_THETA = 10000.0
NORM_EPS = 1e-6
NEG_INF = -1e30

SWA_Q_W = SWA_Q_HEADS * HEAD_DIM
SWA_KV_W = SWA_KV_HEADS * HEAD_DIM
MOBA_W = MOBA_HEADS * HEAD_DIM
IN_SPLITS = [SWA_Q_W, SWA_KV_W, SWA_KV_W, MOBA_W, MOBA_W, MOBA_W, D_MODEL, D_MODEL]
IN_W = int(sum(IN_SPLITS))
IN_OFFSETS = [int(o) for o in np.cumsum(IN_SPLITS)[:-1]]


def rms_norm(x, gain):
    xf = x.astype(jnp.float32)
    y = xf * lax.rsqrt(jnp.mean(xf * xf, axis=-1, keepdims=True) + NORM_EPS)
    return (y * gain.astype(jnp.float32)).astype(x.dtype)

def rope(x, positions):
    half = HEAD_DIM // 2
    inv_freq = ROPE_THETA ** (-jnp.arange(half, dtype=jnp.float32) / half)
    ang = positions.astype(jnp.float32)[..., None] * inv_freq
    cos = jnp.cos(ang)[:, :, None, :]
    sin = jnp.sin(ang)[:, :, None, :]
    xf = x.astype(jnp.float32)
    x1, x2 = xf[..., :half], xf[..., half:]
    out = jnp.concatenate([x1 * cos - x2 * sin, x2 * cos + x1 * sin], axis=-1)
    return out.astype(x.dtype)

def swa_attention(q, k, v, sinks):
    B, S = q.shape[:2]
    W = SWA_WINDOW
    nb = S // W
    G = SWA_Q_HEADS // SWA_KV_HEADS
    qb = q.reshape(B, nb, W, SWA_KV_HEADS, G, HEAD_DIM)

    def band(t):
        tb = t.reshape(B, nb, W, SWA_KV_HEADS, HEAD_DIM)
        prev = jnp.pad(tb[:, :-1], ((0, 0), (1, 0), (0, 0), (0, 0), (0, 0)))
        return jnp.concatenate([prev, tb], axis=2)

    kb, vb = band(k), band(v)
    s = jnp.einsum('bnqhgd,bnkhd->bnhgqk', qb, kb,
                   preferred_element_type=jnp.float32) * (HEAD_DIM ** -0.5)
    qi = jnp.arange(W)[:, None]
    kj = jnp.arange(2 * W)[None, :]
    diff = qi + W - kj
    blk = jnp.arange(nb)[:, None, None]
    valid = (diff >= 0) & (diff < W) & (blk * W - W + kj >= 0)
    s = jnp.where(valid[None, :, None, None], s, NEG_INF)
    sink = sinks.astype(jnp.float32).reshape(SWA_KV_HEADS, G)[None, None, :, :, None, None]
    sink = jnp.broadcast_to(sink, s.shape[:-1] + (1,))
    p = jax.nn.softmax(jnp.concatenate([s, sink], axis=-1), axis=-1)[..., :-1]
    o = jnp.einsum('bnhgqk,bnkhd->bnqhgd', p.astype(v.dtype), vb)
    return o.reshape(B, S, SWA_Q_W)

def _take_blocks(blocks, idx):
    return blocks[idx]

_gather_bh = jax.vmap(jax.vmap(_take_blocks))

def moba_attention(q, k, v):
    B, S = q.shape[:2]
    L = MOBA_BLOCK
    nblk = -(-S // L)
    s_pad = nblk * L
    pad = ((0, 0), (0, s_pad - S), (0, 0), (0, 0))
    kb = jnp.pad(k, pad).reshape(B, nblk, L, MOBA_HEADS, HEAD_DIM).transpose(0, 3, 1, 2, 4)
    vb = jnp.pad(v, pad).reshape(B, nblk, L, MOBA_HEADS, HEAD_DIM).transpose(0, 3, 1, 2, 4)
    k_mean = jnp.mean(kb.astype(jnp.float32), axis=3)
    qh = q.transpose(0, 2, 1, 3)
    gate = jnp.einsum('bhsd,bhnd->bhsn', qh.astype(jnp.float32), k_mean)
    qblk = jnp.arange(S) // L
    past = jnp.arange(nblk)[None, :] < qblk[:, None]
    gate = jnp.where(past[None, None], gate, NEG_INF)
    topk = min(MOBA_TOPK, nblk)
    _, sel = lax.top_k(gate, topk)
    sel_valid = sel < qblk[None, None, :, None]
    scale = HEAD_DIM ** -0.5
    QC = MOBA_Q_CHUNK
    n_chunks = S // QC

    def chunk(ci):
        start = ci * QC
        qc = lax.dynamic_slice_in_dim(qh, start, QC, axis=2)
        selc = lax.dynamic_slice_in_dim(sel, start, QC, axis=2)
        validc = lax.dynamic_slice_in_dim(sel_valid, start, QC, axis=2)
        kg = _gather_bh(kb, selc)
        vg = _gather_bh(vb, selc)
        s_sel = jnp.einsum('bhqd,bhqtld->bhqtl', qc, kg,
                           preferred_element_type=jnp.float32) * scale
        s_sel = jnp.where(validc[..., None], s_sel, NEG_INF).reshape(B, MOBA_HEADS, QC, topk * L)
        own = start // L
        k_own = lax.dynamic_index_in_dim(kb, own, axis=2, keepdims=False)
        v_own = lax.dynamic_index_in_dim(vb, own, axis=2, keepdims=False)
        s_own = jnp.einsum('bhqd,bhld->bhql', qc, k_own,
                           preferred_element_type=jnp.float32) * scale
        qpos = start + jnp.arange(QC)
        kpos = own * L + jnp.arange(L)
        s_own = jnp.where(kpos[None, :] <= qpos[:, None], s_own, NEG_INF)
        p = jax.nn.softmax(jnp.concatenate([s_sel, s_own], axis=-1), axis=-1).astype(v.dtype)
        p_sel = p[..., :topk * L].reshape(B, MOBA_HEADS, QC, topk, L)
        p_own = p[..., topk * L:]
        return (jnp.einsum('bhqtl,bhqtld->bhqd', p_sel, vg)
                + jnp.einsum('bhql,bhld->bhqd', p_own, v_own))

    out = lax.map(chunk, jnp.arange(n_chunks))
    return out.transpose(1, 0, 3, 2, 4).reshape(B, S, MOBA_W)

def adaln(h, shift, scale):
    return h * (1 + scale[:, None, :]) + shift[:, None, :]

def hybrid_layer(x, c, positions, g_mix, g_mlp, w_ada, b_ada, w_in, qn_swa, kn_swa,
                 qn_moba, kn_moba, sinks, w_o_swa, w_o_moba, w_out, w_up, w_down):
    B, S, _ = x.shape
    mod = jax.nn.silu(c) @ w_ada + b_ada
    sh1, sc1, gt1, sh2, sc2, gt2 = jnp.split(mod, 6, axis=-1)

    h = adaln(rms_norm(x, g_mix), sh1, sc1)
    proj = h @ w_in
    q_a, k_a, v_a, q_b, k_b, v_b, gate_a, gate_b = jnp.split(proj, IN_OFFSETS, axis=-1)
    q_a = rope(rms_norm(q_a.reshape(B, S, SWA_Q_HEADS, HEAD_DIM), qn_swa), positions)
    k_a = rope(rms_norm(k_a.reshape(B, S, SWA_KV_HEADS, HEAD_DIM), kn_swa), positions)
    v_a = v_a.reshape(B, S, SWA_KV_HEADS, HEAD_DIM)
    q_b = rope(rms_norm(q_b.reshape(B, S, MOBA_HEADS, HEAD_DIM), qn_moba), positions)
    k_b = rope(rms_norm(k_b.reshape(B, S, MOBA_HEADS, HEAD_DIM), kn_moba), positions)
    v_b = v_b.reshape(B, S, MOBA_HEADS, HEAD_DIM)
    y_a = swa_attention(q_a, k_a, v_a, sinks) @ w_o_swa
    y_b = moba_attention(q_b, k_b, v_b) @ w_o_moba
    mixed = jax.nn.sigmoid(gate_a) * y_a + jax.nn.sigmoid(gate_b) * y_b
    x = x + gt1[:, None, :] * (mixed @ w_out)

    h = adaln(rms_norm(x, g_mlp), sh2, sc2)
    u = jnp.square(jax.nn.relu(h @ w_up))
    x = x + gt2[:, None, :] * (u @ w_down)
    return x

def first_inputs(seed: int = 0) -> dict:
    key = jax.random.key(seed)
    ks = jax.random.split(key, 20)
    f32 = jnp.float32

    def nrm(k, shape, scale):
        return jax.random.normal(k, shape, f32) * scale

    x = jax.random.normal(ks[0], (BATCH, SEQ, D_MODEL), f32)
    c = jax.random.normal(ks[1], (BATCH, D_MODEL), f32)
    offs = jax.random.randint(ks[2], (BATCH, 1), 0, 1024, dtype=jnp.int32)
    positions = (jnp.arange(SEQ, dtype=jnp.int32)[None, :] + offs).astype(jnp.int32)
    return {
        "x": x,
        "c": c,
        "positions": positions,
        "rms_mix": 1.0 + nrm(ks[3], (DEPTH, D_MODEL), 0.05),
        "rms_mlp": 1.0 + nrm(ks[4], (DEPTH, D_MODEL), 0.05),
        "w_ada": nrm(ks[5], (DEPTH, D_MODEL, 6 * D_MODEL), 0.5 * D_MODEL ** -0.5),
        "b_ada": nrm(ks[6], (DEPTH, 6 * D_MODEL), 0.02),
        "w_in": nrm(ks[7], (DEPTH, D_MODEL, IN_W), D_MODEL ** -0.5),
        "q_norm_swa": 1.0 + nrm(ks[8], (DEPTH, HEAD_DIM), 0.05),
        "k_norm_swa": 1.0 + nrm(ks[9], (DEPTH, HEAD_DIM), 0.05),
        "q_norm_moba": 1.0 + nrm(ks[10], (DEPTH, HEAD_DIM), 0.05),
        "k_norm_moba": 1.0 + nrm(ks[11], (DEPTH, HEAD_DIM), 0.05),
        "swa_sinks": nrm(ks[12], (DEPTH, SWA_Q_HEADS), 0.5),
        "w_o_swa": nrm(ks[13], (DEPTH, SWA_Q_W, D_MODEL), SWA_Q_W ** -0.5),
        "w_o_moba": nrm(ks[14], (DEPTH, MOBA_W, D_MODEL), MOBA_W ** -0.5),
        "w_out": nrm(ks[15], (DEPTH, D_MODEL, D_MODEL), D_MODEL ** -0.5),
        "w_up": nrm(ks[16], (DEPTH, D_MODEL, D_FF), D_MODEL ** -0.5),
        "w_down": nrm(ks[17], (DEPTH, D_FF, D_MODEL), D_FF ** -0.5),
    }

def first_block(x, c, positions, rms_mix, rms_mlp, w_ada, b_ada, w_in, q_norm_swa, k_norm_swa,
              q_norm_moba, k_norm_moba, swa_sinks, w_o_swa, w_o_moba, w_out, w_up, w_down):
    for l in range(DEPTH):
        x = hybrid_layer(x, c, positions, rms_mix[l], rms_mlp[l], w_ada[l], b_ada[l], w_in[l],
                         q_norm_swa[l], k_norm_swa[l], q_norm_moba[l], k_norm_moba[l],
                         swa_sinks[l], w_o_swa[l], w_o_moba[l], w_out[l], w_up[l], w_down[l])
    return x


GRID_W = 64
CTX_LEN = 256
EPS = 1e-6

N_MIXERS = 3
POOL_SLOT, ATTN_SLOT, SGU_SLOT = 0, 1, 2
N_POOL_LAYERS = len(range(POOL_SLOT, DEPTH, N_MIXERS))
N_ATTN_LAYERS = len(range(ATTN_SLOT, DEPTH, N_MIXERS))
N_SGU_LAYERS = len(range(SGU_SLOT, DEPTH, N_MIXERS))
CTX_LAST_READER = max([i for i in range(DEPTH) if i % N_MIXERS == ATTN_SLOT], default=-1)

POOL_WINDOWS = (2, 4, 8, 16)
POOL_GROUPS = len(POOL_WINDOWS)
POOL_CH = D_MODEL // POOL_GROUPS

N_Q_HEADS = D_MODEL // HEAD_DIM
N_KV_HEADS = 4
Q_PER_KV = N_Q_HEADS // N_KV_HEADS
Q_DIM = N_Q_HEADS * HEAD_DIM
KV_DIM = N_KV_HEADS * HEAD_DIM
QKV_DIM = Q_DIM + 2 * KV_DIM
ROPE_AXIS_DIM = HEAD_DIM // 2
Q_BLOCK = 128

CHUNK = 128
SGU_WIDTH = D_MODEL
SGU_CH = 128
SGU_GROUPS = SGU_WIDTH // SGU_CH

N_EXPERT_GROUPS = 4
EXPERTS_PER_GROUP = 4
N_EXPERTS = N_EXPERT_GROUPS * EXPERTS_PER_GROUP
TOPK_IN_GROUP = 2
D_EXPERT = 256


def rmsnorm(x, g):
    xf = x.astype(jnp.float32)
    y = xf * lax.rsqrt(jnp.mean(xf * xf, axis=-1, keepdims=True) + EPS)
    return (y * g.astype(jnp.float32)).astype(x.dtype)

def layernorm(x, g, b):
    xf = x.astype(jnp.float32)
    mu = jnp.mean(xf, axis=-1, keepdims=True)
    xc = xf - mu
    var = jnp.mean(xc * xc, axis=-1, keepdims=True)
    return (xc * lax.rsqrt(var + EPS) * g.astype(jnp.float32) + b.astype(jnp.float32)).astype(x.dtype)

def adaln_2(cvec, w_mod, b_mod):
    m = jax.nn.silu(cvec) @ w_mod + b_mod
    m = m.reshape(cvec.shape[:-1] + (6, 1, D_MODEL))
    return tuple(m[..., k, :, :] for k in range(6))

def modulate(x, g, shift, scale):
    return rmsnorm(x, g) * (1.0 + scale) + shift

def rope_tables(rows):
    row = jnp.repeat(jnp.arange(rows), GRID_W)
    col = jnp.tile(jnp.arange(GRID_W), rows)
    inv = ROPE_THETA ** (-jnp.arange(0, ROPE_AXIS_DIM, 2, dtype=jnp.float32) / ROPE_AXIS_DIM)
    ang = jnp.stack([row, col], axis=-1).astype(jnp.float32)[..., None] * inv
    return jnp.cos(ang), jnp.sin(ang)

def apply_rope(x, cos, sin):
    B, n, H, _ = x.shape
    xr = x.astype(jnp.float32).reshape(B, n, H, 2, 2, ROPE_AXIS_DIM // 2)
    x1, x2 = xr[..., 0, :], xr[..., 1, :]
    c, s = cos[:, None], sin[:, None]
    out = jnp.stack([x1 * c - x2 * s, x2 * c + x1 * s], axis=-2)
    return out.reshape(x.shape).astype(x.dtype)

def pool_mixer(h, w_pool, b_pool, ls):
    B, n, _ = h.shape
    t = jnp.arange(n)
    hf = h.astype(jnp.float32)
    outs = []
    for g, w in enumerate(POOL_WINDOWS):
        xg = hf[..., g * POOL_CH:(g + 1) * POOL_CH]
        cs = jnp.concatenate([jnp.zeros_like(xg[:, :1]), jnp.cumsum(xg, axis=1)], axis=1)
        lo = jnp.clip(t - w // 2, 0, n)
        hi = jnp.clip(t + w // 2, 0, n)
        mean = (cs[:, hi] - cs[:, lo]) / (hi - lo).astype(jnp.float32)[:, None]
        outs.append(mean - xg)
    p = jnp.stack(outs, axis=2).astype(h.dtype)
    y = jnp.einsum('bngc,gcd->bngd', p, w_pool) + b_pool
    return y.reshape(h.shape) * ls

def attn_mixer(h_lat, h_ctx, w_qkv, q_g, k_g, w_o, cos, sin, ctx_out):
    B, S, _ = h_lat.shape
    L = h_ctx.shape[1]
    scale = HEAD_DIM ** -0.5
    qkv = h_lat @ w_qkv
    q = rmsnorm(qkv[..., :Q_DIM].reshape(B, S, N_Q_HEADS, HEAD_DIM), q_g)
    k = rmsnorm(qkv[..., Q_DIM:Q_DIM + KV_DIM].reshape(B, S, N_KV_HEADS, HEAD_DIM), k_g)
    v = qkv[..., Q_DIM + KV_DIM:].reshape(B, S, N_KV_HEADS, HEAD_DIM)
    q = apply_rope(q, cos, sin)
    k = apply_rope(k, cos, sin)
    kv_c = h_ctx @ w_qkv[:, Q_DIM:]
    k_c = rmsnorm(kv_c[..., :KV_DIM].reshape(B, L, N_KV_HEADS, HEAD_DIM), k_g)
    v_c = kv_c[..., KV_DIM:].reshape(B, L, N_KV_HEADS, HEAD_DIM)
    k_all = jnp.concatenate([k_c, k], axis=1)
    v_all = jnp.concatenate([v_c, v], axis=1)
    qb = (q * scale).reshape(B, S // Q_BLOCK, Q_BLOCK, N_KV_HEADS, Q_PER_KV, HEAD_DIM)
    qb = jnp.moveaxis(qb, 1, 0)

    def block(q_blk):
        s = jnp.einsum('bqhgd,bkhd->bhgqk', q_blk, k_all).astype(jnp.float32)
        p = jax.nn.softmax(s, axis=-1).astype(v_all.dtype)
        return jnp.einsum('bhgqk,bkhd->bqhgd', p, v_all)

    o = jnp.moveaxis(lax.map(block, qb), 0, 1).reshape(B, S, Q_DIM)
    y_lat = o @ w_o
    y_ctx = None
    if ctx_out:
        q_c = rmsnorm((h_ctx @ w_qkv[:, :Q_DIM]).reshape(B, L, N_Q_HEADS, HEAD_DIM), q_g)
        q_c = (q_c * scale).reshape(B, L, N_KV_HEADS, Q_PER_KV, HEAD_DIM)
        s_c = jnp.einsum('bqhgd,bkhd->bhgqk', q_c, k_c).astype(jnp.float32)
        p_c = jax.nn.softmax(s_c, axis=-1).astype(v_c.dtype)
        y_ctx = jnp.einsum('bhgqk,bkhd->bqhgd', p_c, v_c).reshape(B, L, Q_DIM) @ w_o
    return y_lat, y_ctx

def sgu_mixer(h, w_in, b_in, ln_g, ln_b, w_s, b_s, w_out):
    B, n, _ = h.shape
    z = jax.nn.gelu(h @ w_in + b_in)
    u, v = z[..., :SGU_WIDTH], z[..., SGU_WIDTH:]
    v = layernorm(v, ln_g, ln_b)
    vc = v.reshape(B, n // CHUNK, CHUNK, SGU_GROUPS, SGU_CH)
    sv = jnp.einsum('gpq,bcqgk->bcpgk', w_s, vc) + b_s.T[:, :, None]
    return (u * sv.reshape(B, n, SGU_WIDTH)) @ w_out

def hier_moe(h, w_rg, b_rg, w_re, b_re, w_gate, w_up, w_down):
    shp = h.shape
    hf = h.reshape(-1, D_MODEL)
    n = hf.shape[0]
    g_logits = (hf @ w_rg).astype(jnp.float32) + b_rg
    g_prob = jax.nn.softmax(g_logits, axis=-1)
    g_sel = jnp.argmax(g_logits, axis=-1)
    g_w = jnp.take_along_axis(g_prob, g_sel[:, None], axis=-1)
    e_logits = ((hf @ w_re).astype(jnp.float32) + b_re).reshape(n, N_EXPERT_GROUPS, EXPERTS_PER_GROUP)
    e_in = jnp.take_along_axis(e_logits, g_sel[:, None, None], axis=1)[:, 0]
    top_v, top_i = lax.top_k(e_in, TOPK_IN_GROUP)
    e_w = jax.nn.softmax(top_v, axis=-1) * g_w
    expert_id = g_sel[:, None] * EXPERTS_PER_GROUP + top_i
    gates = jnp.sum(jax.nn.one_hot(expert_id, N_EXPERTS, dtype=jnp.float32) * e_w[..., None], axis=1)
    a = jnp.einsum('nd,edf->nef', hf, w_gate)
    b = jnp.einsum('nd,edf->nef', hf, w_up)
    hid = jax.nn.silu(a) * b * gates.astype(h.dtype)[..., None]
    return jnp.einsum('nef,efd->nd', hid, w_down).reshape(shp)

def second_inputs(seed: int = 0) -> dict:
    key = jax.random.key(seed)
    ks = iter(jax.random.split(key, 40))
    D = D_MODEL

    def nrm(shape, scale):
        return jax.random.normal(next(ks), shape, jnp.float32) * scale

    return {
        "x": nrm((BATCH, SEQ, D), 1.0),
        "c": nrm((BATCH, D), 1.0),
        "ctx": nrm((BATCH, CTX_LEN, D), 1.0),
        "c_ctx": nrm((D,), 1.0),
        "w_mod": nrm((DEPTH, D, 6 * D), 0.5 * D ** -0.5),
        "b_mod": nrm((DEPTH, 6 * D), 0.02),
        "norm1_g": 1.0 + nrm((DEPTH, D), 0.02),
        "norm2_g": 1.0 + nrm((DEPTH, D), 0.02),
        "pool_w": nrm((N_POOL_LAYERS, POOL_GROUPS, POOL_CH, POOL_CH), POOL_CH ** -0.5),
        "pool_b": nrm((N_POOL_LAYERS, POOL_GROUPS, POOL_CH), 0.02),
        "pool_ls": 1.0 + nrm((N_POOL_LAYERS, D), 0.02),
        "attn_wqkv": nrm((N_ATTN_LAYERS, D, QKV_DIM), D ** -0.5),
        "attn_qg": 1.0 + nrm((N_ATTN_LAYERS, HEAD_DIM), 0.02),
        "attn_kg": 1.0 + nrm((N_ATTN_LAYERS, HEAD_DIM), 0.02),
        "attn_wo": nrm((N_ATTN_LAYERS, Q_DIM, D), Q_DIM ** -0.5),
        "sgu_win": nrm((N_SGU_LAYERS, D, 2 * SGU_WIDTH), D ** -0.5),
        "sgu_bin": nrm((N_SGU_LAYERS, 2 * SGU_WIDTH), 0.02),
        "sgu_lng": 1.0 + nrm((N_SGU_LAYERS, SGU_WIDTH), 0.02),
        "sgu_lnb": nrm((N_SGU_LAYERS, SGU_WIDTH), 0.02),
        "sgu_ws": nrm((N_SGU_LAYERS, SGU_GROUPS, CHUNK, CHUNK), CHUNK ** -0.5),
        "sgu_bs": 1.0 + nrm((N_SGU_LAYERS, SGU_GROUPS, CHUNK), 0.02),
        "sgu_wout": nrm((N_SGU_LAYERS, SGU_WIDTH, D), SGU_WIDTH ** -0.5),
        "moe_wrg": nrm((DEPTH, D, N_EXPERT_GROUPS), D ** -0.5),
        "moe_brg": nrm((DEPTH, N_EXPERT_GROUPS), 0.01),
        "moe_wre": nrm((DEPTH, D, N_EXPERTS), D ** -0.5),
        "moe_bre": nrm((DEPTH, N_EXPERTS), 0.01),
        "moe_wg": nrm((DEPTH, N_EXPERTS, D, D_EXPERT), D ** -0.5),
        "moe_wu": nrm((DEPTH, N_EXPERTS, D, D_EXPERT), D ** -0.5),
        "moe_wd": nrm((DEPTH, N_EXPERTS, D_EXPERT, D), D_EXPERT ** -0.5),
    }

def second_block(x, c, ctx, c_ctx, w_mod, b_mod, norm1_g, norm2_g, pool_w, pool_b, pool_ls,
              attn_wqkv, attn_qg, attn_kg, attn_wo, sgu_win, sgu_bin, sgu_lng, sgu_lnb, sgu_ws, sgu_bs,
              sgu_wout, moe_wrg, moe_brg, moe_wre, moe_bre, moe_wg, moe_wu, moe_wd):
    rows = x.shape[1] // GRID_W
    cos, sin = rope_tables(rows)
    s = ctx
    for i in range(DEPTH):
        kind = i % N_MIXERS
        j = i // N_MIXERS
        ctx_in = i <= CTX_LAST_READER
        ctx_upd = i < CTX_LAST_READER
        sh1, sc1, g1, sh2, sc2, g2 = adaln_2(c, w_mod[i], b_mod[i])
        a_lat = modulate(x, norm1_g[i], sh1, sc1)
        if ctx_in:
            csh1, csc1, cg1, csh2, csc2, cg2 = adaln_2(c_ctx, w_mod[i], b_mod[i])
            a_ctx = modulate(s, norm1_g[i], csh1, csc1)
        if kind == POOL_SLOT:
            y_lat = pool_mixer(a_lat, pool_w[j], pool_b[j], pool_ls[j])
            if ctx_upd:
                y_ctx = pool_mixer(a_ctx, pool_w[j], pool_b[j], pool_ls[j])
        elif kind == ATTN_SLOT:
            y_lat, y_ctx = attn_mixer(a_lat, a_ctx, attn_wqkv[j], attn_qg[j], attn_kg[j], attn_wo[j],
                                      cos, sin, ctx_upd)
        else:
            y_lat = sgu_mixer(a_lat, sgu_win[j], sgu_bin[j], sgu_lng[j], sgu_lnb[j], sgu_ws[j], sgu_bs[j],
                              sgu_wout[j])
            if ctx_upd:
                y_ctx = sgu_mixer(a_ctx, sgu_win[j], sgu_bin[j], sgu_lng[j], sgu_lnb[j], sgu_ws[j],
                                  sgu_bs[j], sgu_wout[j])
        x = x + g1 * y_lat
        x = x + g2 * hier_moe(modulate(x, norm2_g[i], sh2, sc2), moe_wrg[i], moe_brg[i], moe_wre[i],
                              moe_bre[i], moe_wg[i], moe_wu[i], moe_wd[i])
        if ctx_upd:
            s = s + cg1 * y_ctx
            s = s + cg2 * hier_moe(modulate(s, norm2_g[i], csh2, csc2), moe_wrg[i], moe_brg[i],
                                   moe_wre[i], moe_bre[i], moe_wg[i], moe_wu[i], moe_wd[i])
    return x


def setup_inputs(seed=0):
    out = dict(first_inputs(seed))
    for name, value in second_inputs(seed + 1).items():
        if name != "x":
            out[name + "_2"] = value
    return out


def reference(
    x, c, positions, rms_mix, rms_mlp, w_ada, b_ada, w_in, q_norm_swa, k_norm_swa, q_norm_moba,
    k_norm_moba, swa_sinks, w_o_swa, w_o_moba, w_out, w_up, w_down, c_2, ctx_2, c_ctx_2,
    w_mod_2, b_mod_2, norm1_g_2, norm2_g_2, pool_w_2, pool_b_2, pool_ls_2, attn_wqkv_2,
    attn_qg_2, attn_kg_2, attn_wo_2, sgu_win_2, sgu_bin_2, sgu_lng_2, sgu_lnb_2, sgu_ws_2,
    sgu_bs_2, sgu_wout_2, moe_wrg_2, moe_brg_2, moe_wre_2, moe_bre_2, moe_wg_2, moe_wu_2,
    moe_wd_2,
):
    x = first_block(
        x, c, positions, rms_mix, rms_mlp, w_ada, b_ada, w_in, q_norm_swa, k_norm_swa,
        q_norm_moba, k_norm_moba, swa_sinks, w_o_swa, w_o_moba, w_out, w_up, w_down,
    )
    return second_block(
        x, c_2, ctx_2, c_ctx_2, w_mod_2, b_mod_2, norm1_g_2, norm2_g_2, pool_w_2, pool_b_2,
        pool_ls_2, attn_wqkv_2, attn_qg_2, attn_kg_2, attn_wo_2, sgu_win_2, sgu_bin_2,
        sgu_lng_2, sgu_lnb_2, sgu_ws_2, sgu_bs_2, sgu_wout_2, moe_wrg_2, moe_brg_2, moe_wre_2,
        moe_bre_2, moe_wg_2, moe_wu_2, moe_wd_2,
    )


_drawn_inputs = setup_inputs


def setup_inputs(seed=0):
    import zlib

    import numpy as np

    out = dict(_drawn_inputs(seed))
    spreads = {}
    factors = {'rms_mix': 7.011,
     'q_norm_swa': 8.0,
     'k_norm_swa': 8.0,
     'q_norm_moba': 8.0,
     'k_norm_moba': 8.0,
     'swa_sinks': 8.0,
     'ctx_2': 3.568,
     'norm1_g_2': 8.0,
     'norm2_g_2': 5.165,
     'pool_b_2': 7.707,
     'pool_ls_2': 8.0,
     'attn_qg_2': 8.0,
     'attn_kg_2': 8.0,
     'moe_brg_2': 21.959,
     'moe_bre_2': 8.0}
    for name, (base, spread) in spreads.items():
        noise = np.random.default_rng([zlib.crc32(name.encode()), seed]).standard_normal(out[name].shape)
        drawn = base * np.exp(spread * noise) if base else spread * noise
        out[name] = __import__('jax').numpy.asarray(drawn.astype(out[name].dtype))
    for name, factor in factors.items():
        out[name] = (out[name] * factor).astype(out[name].dtype)
    return out
```

```python
from contextlib import ExitStack

import numpy as np
import concourse.bass as bass
from concourse import mybir

F32 = mybir.dt.float32
F32R = mybir.dt.float32r
I32 = mybir.dt.int32
ALU = mybir.AluOpType
ACT = mybir.ActivationFunctionType
AX = mybir.AxisListType

P = 128
D = 1024
DT = D // P
S = 256
S2 = 512
HD = 64
UC = 256
UNIT = DT * UC
RAW_SLOTS = 4
SPLIT_SLOTS = 3
NEG = -1e30
EPS = 1e-6
SCALE = HD ** -0.5
N_EXP = 16
WINDOW = 128
GRID_W = 64
THETA = 10000.0

C_IDENT, C_ROT1, C_ROT2, C_DUP0, C_DUP1, C_HEADMEAN, C_MEAN = (P * i for i in range(7))
C_MISC = 7 * P
C_IOTA = C_MISC + 2
C_FIXED = C_IOTA + N_EXP
C_CAUSAL = C_FIXED
C_SWA = C_CAUSAL + 512
C_COS2 = C_SWA + 512
C_SIN2 = C_COS2 + S
C_POOL = C_SIN2 + S
C_END = C_POOL + 4 * S


def constants():
    c = np.zeros((P, C_END), np.float32)
    i = np.arange(P)
    c[i, C_IDENT + i] = 1
    half = HD // 2
    for m in range(P):
        first = m % HD < half
        c[m + half if first else m - half, C_ROT1 + m] = -1 if first else 1
    quarter = HD // 4
    for m in range(P):
        first = m % half < quarter
        c[m + quarter if first else m - quarter, C_ROT2 + m] = -1 if first else 1
    c[i % HD, C_DUP0 + i] = 1
    c[HD + i % HD, C_DUP1 + i] = 1
    c[:, C_HEADMEAN:C_HEADMEAN + P] = (i[:, None] // HD == i[None, :] // HD) / HD
    c[:, C_MEAN:C_MEAN + P] = 1.0 / D
    inv = THETA ** (-np.arange(half) / half)
    c[:, C_MISC] = inv[i % half]
    c[:, C_MISC + 1] = EPS
    c[:, C_IOTA:C_IOTA + N_EXP] = np.arange(N_EXP)
    q = np.arange(2)[None, :, None] * P + i[:, None, None]
    k = np.arange(S)[None, None, :]
    c[:, C_CAUSAL:C_CAUSAL + 512] = np.where(k <= q, 0, NEG).reshape(P, 512)
    c[:, C_SWA:C_SWA + 512] = np.where((k <= q) & (q - k < WINDOW), 0, NEG).reshape(P, 512)
    inv2 = (np.float32(THETA) ** (-np.arange(0, half, 2, dtype=np.float32) / half)).astype(np.float32)
    tok = np.arange(S)
    pos = np.where((i[:, None] % HD) < half, tok // GRID_W, tok % GRID_W).astype(np.float32)
    ang = (pos * inv2[i % quarter][:, None]).astype(np.float32).astype(np.float64)
    c[:, C_COS2:C_COS2 + S] = np.cos(ang)
    c[:, C_SIN2:C_SIN2 + S] = np.sin(ang)
    for g in range(4):
        w = 2 << g
        count = np.clip(tok + w // 2, 0, S) - np.clip(tok - w // 2, 0, S)
        c[:, C_POOL + g * S:C_POOL + (g + 1) * S] = 1.0 / count
    return c


def flat(tickets):
    for t in tickets:
        if t is None:
            continue
        if isinstance(t, list):
            yield from flat(t)
        else:
            yield t


class Lane:

    def __init__(self, sem):
        self.sem, self.count, self.steps, self.seen = sem, 0, [], {}

    def wait(self, *tickets):
        for sem, value in flat(tickets):
            if self.seen.get(id(sem), 0) < value:
                self.seen[id(sem)] = value
                self.steps.append(lambda e, sem=sem, value=value: e.wait_ge(sem, value))

    def do(self, issue, after=(), signal=True):
        self.wait(*after)
        if not signal:
            self.steps.append(issue)
            return None
        self.count += 1
        self.steps.append(lambda e: issue(e).then_inc(self.sem, 1))
        return self.sem, self.count

    def load(self, dst, src, mark, after=()):
        self.wait(*after)
        mark[1] += 16
        self.steps.append(lambda e: e.dma_start(dst, src).then_inc(mark[0], 16))
        return mark[0], mark[1]


class Ring:

    def __init__(self, n):
        self.n, self.at, self.free = n, 0, [[] for _ in range(n)]

    def take(self, k=1):
        self.at += (-self.at) % k
        first = self.at % self.n
        self.at += k
        tickets = []
        for i in range(first, first + k):
            assert self.free[i] is not None, "buffer still held"
            tickets += self.free[i]
            self.free[i] = None
        return first, tickets

    def give(self, first, tickets, k=1):
        for i in range(first, first + k):
            self.free[i] = list(tickets)


def build(nc, a, out):
    with ExitStack() as ctx:
        at = [-(-nc.sbuf_base // 64) * 64]

        def sb(name, shape, dt=F32, offset=None):
            size = 4 * int(np.prod(shape[1:]))
            if offset is None:
                offset = at[0]
                at[0] += -(-size // 64) * 64
                assert at[0] <= nc.sbuf_usable_end, (name, at[0], nc.sbuf_usable_end)
            return nc.alloc_sbuf_tensor_at(name, shape, dt, offset=offset), offset

        raw, _ = sb("raw", [P, RAW_SLOTS, UNIT])
        w_hi, _ = sb("w_hi", [P, SPLIT_SLOTS, DT, UC], F32R)
        w_lo, _ = sb("w_lo", [P, SPLIT_SLOTS, DT, UC], F32R)
        x, _ = sb("x", [P, DT, S2])
        h_hi2, big1 = sb("h_hi2", [P, DT, S2], F32R)
        h_lo2, _ = sb("h_lo2", [P, DT, S2], F32R)
        h_hi1, _ = sb("h_hi1", [P, DT, S], F32R, offset=big1)
        h_lo1, _ = sb("h_lo1", [P, DT, S], F32R, offset=big1 + 8192)
        gate_tanh, _ = sb("gate_tanh", [P, 16, S], F32, offset=big1 + 16384)
        u_hi2, big2 = sb("u_hi2", [P, DT, S2], F32R)
        u_lo2, _ = sb("u_lo2", [P, DT, S2], F32R)
        u_hi1, _ = sb("u_hi1", [P, DT, S], F32R, offset=big2)
        u_lo1, _ = sb("u_lo1", [P, DT, S], F32R, offset=big2 + 8192)
        qk, _ = sb("qk", [P, 16, S], F32, offset=big2 + 16384)
        q_att, _ = sb("q_att", [P, 8, S], F32, offset=big2 + 16384)
        k_att, _ = sb("k_att", [P, 4, S2], F32, offset=big2 + 24576)
        tokens_in, _ = sb("tokens_in", [P, 4, D], F32, offset=big2)
        v_tok, _ = sb("v_tok", [P, 1280])
        acc, _ = sb("acc", [P, 3, D])
        tmp, _ = sb("tmp", [P, 8, 512])
        rstd, _ = sb("rstd", [P, S2])
        cst, _ = sb("cst", [P, C_FIXED])
        phase_tab, _ = sb("phase_tab", [P, 1024])
        rope_tab, _ = sb("rope_tab", [P, 2, S])
        par, _ = sb("par", [P, 3, P])
        mod, _ = sb("mod", [P, 6, 48])
        gain, _ = sb("gain", [P, 12, DT])
        cond, _ = sb("cond", [P, 3, DT])
        cond_t, _ = sb("cond_t", [P, 3, DT])
        sink, _ = sb("sink", [P, 16])
        stats, _ = sb("stats", [P, 16, 12])
        w_route, _ = sb("w_route", [P, 2, DT, 20])
        b_route, _ = sb("b_route", [P, 2, 20])
        gates_t, _ = sb("gates_t", [16, S2])
        psum = ctx.enter_context(nc.psum_tensor("psum", [P, 8, 512], F32))

        def sem(name):
            return ctx.enter_context(nc.semaphore(name))

        pe, act, dve, pool, sp = (Lane(sem(n)) for n in ("s_pe", "s_act", "s_dve", "s_pool", "s_sp"))
        banks, bufs = Ring(8), Ring(8)
        marks = {}

        def mark(name):
            if name not in marks:
                marks[name] = [sem(name), 0]
            return marks[name]

        def mm(o, lhs, rhs, start, stop, after=(), signal=False):
            return pe.do(lambda e: e.matmul(o, lhs, rhs, start=start, stop=stop, skip_group_check=True),
                         after, signal)

        def tp(o, i, ident, after=(), signal=False):
            return pe.do(lambda e: e.transpose(o, i, ident), after, signal)

        def fn(o, i, func, after=(), bias=None, scale=1.0, accum=None):
            kw = {"scale": scale}
            if bias is not None:
                kw["bias"] = bias
            if accum is not None:
                kw["accum_out"] = accum
            return act.do(lambda e: e.activation(o, i, func, **kw), after)

        def tt(lane, o, i0, i1, op, after=()):
            return lane.do(lambda e: e.tensor_tensor(o, i0, i1, op), after)

        def ts(lane, o, i, s1, s2, op0, op1, after=()):
            if s2 is None:
                return lane.do(lambda e: e.tensor_scalar(o, i, s1, None, op0), after)
            return lane.do(lambda e: e.tensor_scalar(o, i, s1, s2, op0, op1), after)

        def stt(o, i0, s, i1, op0, op1, after=()):
            return dve.do(lambda e: e.scalar_tensor_tensor(out=o, in0=i0, scalar=s, in1=i1, op0=op0, op1=op1),
                          after)

        def reduce(o, i, op, after=()):
            return dve.do(lambda e: e.tensor_reduce(o, i, AX.X, op), after)

        def spread(ap, axis, shape):
            return ap.unsqueeze(axis).to_broadcast(shape)

        def plain(ap):
            return ap.bitcast(F32)

        def low(hi, lo, value_op, after):
            if isinstance(value_op, tuple):
                i0, s, op = value_op
                return stt(lo, i0, s, plain(hi), op, ALU.subtract, after)
            return tt(dve, lo, value_op, plain(hi), ALU.subtract, after)

        ident = cst[:, C_IDENT:C_IDENT + P]
        mean = cst[:, C_MEAN:C_MEAN + P]
        headmean = cst[:, C_HEADMEAN:C_HEADMEAN + P]
        eps = cst[:, C_MISC + 1:C_MISC + 2]

        got_cst = act.load(cst[:], a["consts"][:, 0:C_FIXED], mark("d_cst"))
        tok_mark = [mark(f"d_tok{i}") for i in range(4)]
        got_tok = []
        for i in range(4):
            src = a["x"][0] if i < 2 else a["ctx_2"][0]
            got_tok.append(act.load(tokens_in[:, i, :], src[(i % 2) * P:(i % 2 + 1) * P, :], tok_mark[i]))
        rows = tmp[:, 0, 0:3 * P].rearrange("p (r c) -> p r c", r=3)
        row_free = [bufs.take(1) for _ in range(2)]

        def param_rows(dst_row, block, arr, n):
            return pool.load(rows[dst_row:dst_row + n, block, :], arr.rearrange("(r c) -> r c", c=P), mark("d_par"))

        for layer in range(2):
            r = 64 * layer
            for block, names in ((0, ("rms_mix", "rms_mlp", "b_ada")), (1, ("norm1_g_2", "norm2_g_2", "b_mod_2"))):
                param_rows(r, block, a[names[0]][layer], 8)
                param_rows(r + 8, block, a[names[1]][layer], 8)
                param_rows(r + 16, block, a[names[2]][layer], 48)
        param_rows(0, 2, a["pool_b_2"][0].rearrange("g c -> (g c)"), 8)
        param_rows(8, 2, a["pool_ls_2"][0], 8)
        param_rows(16, 2, a["c"][0], 8)
        param_rows(24, 2, a["c_2"][0], 8)
        param_rows(32, 2, a["c_ctx_2"], 8)
        R_HEAD = 40
        for j, name in enumerate(("q_norm_swa", "k_norm_swa", "q_norm_moba", "k_norm_moba")):
            for half in range(2):
                pool.load(rows[R_HEAD + 2 * j:R_HEAD + 2 * j + 2, 2, half * HD:(half + 1) * HD], a[name],
                          mark("d_par"))
        for j, name in enumerate(("attn_qg_2", "attn_kg_2")):
            for half in range(2):
                got_rows = pool.load(rows[R_HEAD + 8 + j:R_HEAD + 9 + j, 2, half * HD:(half + 1) * HD], a[name],
                                     mark("d_par"))
        N_ROWS = (P, P, R_HEAD + 10)
        pos_i = tmp[:, 1, 0:S].bitcast(I32)
        got_pos = act.load(pos_i, a["positions"][0].partition_broadcast(P), mark("d_pos"))
        got_phase = act.load(phase_tab[:], a["consts"][:, C_CAUSAL:C_CAUSAL + 1024], mark("d_phase"))
        pool.load(sink[:], a["swa_sinks"].rearrange("l h -> (l h)").partition_broadcast(P), mark("d_small"))
        for layer in range(2):
            pool.load(w_route[:, layer, :, 0:4], a["moe_wrg_2"][layer].rearrange("(k p) c -> p k c", p=P),
                      mark("d_small"))
            pool.load(w_route[:, layer, :, 4:20], a["moe_wre_2"][layer].rearrange("(k p) c -> p k c", p=P),
                      mark("d_small"))
            pool.load(b_route[:, layer, 0:4], a["moe_brg_2"][layer].partition_broadcast(P), mark("d_small"))
            got_small = pool.load(b_route[:, layer, 4:20], a["moe_bre_2"][layer].partition_broadcast(P),
                                  mark("d_small"))

        def unit_of(w, k0, c0, k=DT):
            return w[k0 * P:(k0 + k) * P, c0:c0 + UC].rearrange("(k p) c -> p k c", p=P)

        plan = []

        def plan_gemm(name, w, k0, c0):
            plan.append(("gemm", name, [(0, DT, unit_of(w, k0, c0))]))

        mod_items = []
        for layer in range(4):
            for chunk in ((1, 0, 2, 4, 3, 5)):
                for pair in range(4):
                    mod_items.append(("mod", layer, chunk, pair))

        gemms = []
        for l in range(2):
            for j in range(4352 // UC):
                gemms.append(("in", [(0, DT, unit_of(a["w_in"][l], 0, j * UC))]))
            for j in range(4):
                gemms.append(("o", [(0, 4, unit_of(a["w_o_swa"][l], 0, j * UC, 4)),
                                    (4, 4, unit_of(a["w_o_moba"][l], 0, j * UC, 4))]))
            for j in range(4):
                gemms.append(("out", [(0, DT, unit_of(a["w_out"][l], 0, j * UC))]))
            for g in range(4):
                for j in range(4):
                    gemms.append(("up", [(0, DT, unit_of(a["w_up"][l], 0, g * D + j * UC))]))
                for j in range(4):
                    gemms.append(("down", [(0, DT, unit_of(a["w_down"][l], g * DT, j * UC))]))
        for l in range(2):
            if l == 0:
                gemms.append(("pool", [(0, DT, unit_of(a["pool_w_2"][0].rearrange("g c d -> (g c) d"), 0, 0))]))
            else:
                for j in range(6):
                    gemms.append(("qkv", [(0, DT, unit_of(a["attn_wqkv_2"][0], 0, j * UC))]))
                for j in range(4):
                    gemms.append(("wo", [(0, DT, unit_of(a["attn_wo_2"][0], 0, j * UC))]))
            w_dn = a["moe_wd_2"][l].rearrange("e f d -> (e f) d")
            for g in range(4):
                for e in range(4 * g, 4 * g + 4):
                    gemms.append(("eg", [(0, DT, unit_of(a["moe_wg_2"][l, e], 0, 0))]))
                    gemms.append(("eu", [(0, DT, unit_of(a["moe_wu_2"][l, e], 0, 0))]))
                for j in range(4):
                    gemms.append(("ed", [(0, DT, unit_of(w_dn, g * DT, j * UC))]))
        sent = 8
        plan += mod_items[:sent]
        for i, (name, parts) in enumerate(gemms):
            want = min(len(mod_items), sent if i < 0 else 8 + int(0.62 * (i + 1)))
            while sent < want:
                plan.append(mod_items[sent])
                sent += 1
            plan.append(("gemm", name, parts))
        assert sent == len(mod_items)

        raw_mark = [mark(f"d_raw{i}") for i in range(RAW_SLOTS)]
        raw_free = [[] for _ in range(RAW_SLOTS)]
        split_free = [[] for _ in range(SPLIT_SLOTS)]
        accs = Ring(3)
        fed = {"plan": 0, "gemm": 0, "used": 0}
        split_ready = {}
        mod_sources = [a["w_ada"][0], a["w_ada"][1], a["w_mod_2"][0], a["w_mod_2"][1]]
        cond_of = lambda layer, chunk: ([(0, layer)] if layer < 2 else
                                        [(1, layer)] + ([(2, layer + 2)] if layer == 2 or chunk < 2 else []))
        mod_acc, mod_ready, finals = {}, {}, []
        cond_ready = []

        def feed():
            item = plan[fed["plan"]]
            slot = fed["plan"] % RAW_SLOTS
            fed["plan"] += 1
            if item[0] == "gemm":
                flat_dst = raw[:, slot, :].rearrange("p (k c) -> p k c", c=UC)
                for k0, k, src in item[2]:
                    landed = sp.load(flat_dst[:, k0:k0 + k, :], src, raw_mark[slot], [raw_free[slot]])
                s = fed["gemm"] % SPLIT_SLOTS
                src = raw[:, slot, :]
                hi = w_hi[:, s].rearrange("p k c -> p (k c)")
                lo = w_lo[:, s].rearrange("p k c -> p (k c)")
                t_hi = fn(hi, src, ACT.Copy, [landed, split_free[s]])
                t_lo = low(hi, lo, src, [landed, t_hi, split_free[s]])
                raw_free[slot] = [t_hi, t_lo]
                split_ready[fed["gemm"]] = [t_hi, t_lo]
                fed["gemm"] += 1
                return
            _, layer, chunk, pair = item
            dst = raw[:, slot, :].rearrange("p (k c) -> p k c", c=D)
            src = mod_sources[layer][2 * pair * P:(2 * pair + 2) * P, chunk * D:(chunk + 1) * D]
            landed = sp.load(dst, src.rearrange("(k p) c -> p k c", p=P), raw_mark[slot], [raw_free[slot]])
            last = []
            for which, row in cond_of(layer, chunk):
                if pair == 0:
                    mod_acc[row] = list(accs.take()) + [None]
                buf, free, before = mod_acc[row]
                for k in range(2):
                    s = cond[:, which, 2 * pair + k:2 * pair + k + 1]
                    if pair == 0 and k == 0:
                        before = ts(dve, acc[:, buf, :], dst[:, k, :], s, None, ALU.mult, None,
                                    [landed, cond_ready, free])
                    else:
                        before = stt(acc[:, buf, :], dst[:, k, :], s, acc[:, buf, :], ALU.mult, ALU.add,
                                     [landed, before])
                mod_acc[row][2] = before
                last.append(before)
                if pair == 3:
                    finals.append((row, layer, chunk, buf, before))
            raw_free[slot] = last

        def finish_mods():
            while finals:
                row, layer, chunk, buf, summed = finals.pop(0)
                b, free = banks.take()
                for t in range(DT):
                    done = mm(psum[:, b, t:t + 1], acc[:, buf, t * P:(t + 1) * P], mean[:, 0:1], True, True,
                              [summed, free, got_cst], t == DT - 1)
                accs.give(buf, [done])
                col = mod[:, row, chunk * DT:(chunk + 1) * DT]
                base = 64 * (layer % 2)
                bias = par[:, layer // 2, base + 16 + chunk * DT:base + 16 + (chunk + 1) * DT]
                t = stt(col, psum[:, b, 0:DT], float(D), bias, ALU.mult, ALU.add, [done, par_ready])
                banks.give(b, [t])
                if chunk in (1, 4):
                    g = par[:, layer // 2, base + (chunk // 4) * 8:base + (chunk // 4) * 8 + 8]
                    t = stt(gain[:, 2 * row + chunk // 4, :], col, 1.0, g, ALU.add, ALU.mult, [t])
                mod_ready[row, chunk] = t

        def unit(name):
            g = fed["used"]
            assert gemms[g][0] == name, (gemms[g][0], name)
            while fed["gemm"] < min(g + SPLIT_SLOTS, len(gemms)):
                feed()
            finish_mods()
            fed["used"] += 1
            s = g % SPLIT_SLOTS
            return s, split_ready[g]

        def column(row, chunk, t):
            return mod[:, row, chunk * DT + t:chunk * DT + t + 1]

        def gain_col(row, chunk, t):
            return gain[:, 2 * row + chunk // 4, t:t + 1]

        def product(name, acts, n, ktiles=None, col0=0):
            s, ready = unit(name)
            k_banks = 2 * n // 512
            b, free = banks.take(k_banks)
            o = psum[:, b:b + k_banks, :].rearrange("p b c -> p (b c)").rearrange("p (m n) -> p m n", n=n)
            hi, lo, tickets = acts
            for m in range(2):
                ks = list(range(DT))
                for i, k in enumerate(ks):
                    wh = w_hi[:, s, k, m * P:(m + 1) * P]
                    wl = w_lo[:, s, k, m * P:(m + 1) * P]
                    xh, xl = hi[:, k, col0:col0 + n], lo[:, k, col0:col0 + n]
                    mm(o[:, m], wh, xh, i == 0, False, [ready[0], free, tickets[k]])
                    mm(o[:, m], wh, xl, False, False)
                    last = m == 1 and i == len(ks) - 1
                    done = mm(o[:, m], wl, xh, False, i == len(ks) - 1, [ready[1]], last)
            split_free[s] = [done]
            return b, k_banks, o, done

        par_ready = []
        for block in range(3):
            n = N_ROWS[block]
            b, free = banks.take()
            t = tp(psum[:, b, 0:n], rows[0:n, block, :], ident[0:n, 0:n], [got_rows, got_cst, free], True)
            t = fn(par[:, block, 0:n], psum[:, b, 0:n], ACT.Copy, [t])
            banks.give(b, [t])
            par_ready.append(t)
        bufs.give(row_free[0][0], [par_ready[-1]])
        cvec = par[:, 2, 16:40].rearrange("p (v t) -> p v t", v=3)
        t = fn(cond_t[:], cvec, ACT.Tanh, [par_ready], scale=0.5)
        t = stt(cond_t[:], cond_t[:], 1.0, cvec, ALU.add, ALU.mult, [t, par_ready])
        cond_ready = [ts(dve, cond[:], cond_t[:], 0.5, None, ALU.mult, None, [t])]

        x_ready = [[] for _ in range(DT)]
        for t in range(DT):
            b, free = banks.take()
            for i in range(4):
                done = tp(psum[:, b, i * P:(i + 1) * P], tokens_in[:, i, t * P:(t + 1) * P], ident,
                          [got_tok[i], free], i == 3)
            done = fn(x[:, t, :], psum[:, b, :], ACT.Copy, [done])
            banks.give(b, [done])
            x_ready[t] = [done]

        C1 = 6.28125
        C2 = float(np.float32(2 * np.pi - C1).view(np.uint32) & np.uint32(0xFFFFF000))
        C2 = float(np.array([int(C2)], np.uint32).view(np.float32)[0])
        C3 = float(2 * np.pi - C1 - C2)
        MAGIC = 1.5 * 2.0 ** 23
        LIMIT = 3.1415925
        pf, ang, turns = tmp[:, 2, 0:S], tmp[:, 3, 0:S], tmp[:, 4, 0:S]
        rope_bufs = [bufs.take() for _ in range(3)]
        t = dve.do(lambda e: e.tensor_copy(pf, pos_i), [got_pos])
        bufs.give(row_free[1][0], [t])
        t = ts(dve, ang, pf, cst[:, C_MISC:C_MISC + 1], None, ALU.mult, None, [t, got_cst])
        t = ts(dve, turns, ang, 1.0 / (2 * np.pi), None, ALU.mult, None, [t])
        t = ts(dve, turns, turns, MAGIC, None, ALU.add, None, [t])
        t = ts(dve, turns, turns, -MAGIC, None, ALU.add, None, [t])
        for c in (C1, C2, C3):
            t = stt(ang, turns, -c, ang, ALU.mult, ALU.add, [t])
        t = ts(dve, ang, ang, LIMIT, -LIMIT, ALU.min, ALU.max, [t])
        sin_t = fn(rope_tab[:, 1, :], ang, ACT.Sin, [t])
        t = ts(dve, pf, ang, float(np.pi / 2), None, ALU.add, None, [t])
        t = ts(dve, turns, pf, float(np.pi), -2 * float(np.pi), ALU.is_gt, ALU.mult, [t])
        t = tt(dve, pf, pf, turns, ALU.add, [t])
        t = ts(dve, pf, pf, LIMIT, -LIMIT, ALU.min, ALU.max, [t])
        rope_ready = fn(rope_tab[:, 0, :], pf, ACT.Sin, [t, sin_t])
        for b, _ in rope_bufs:
            bufs.give(b, [rope_ready, t])

        def rms_scale(n):
            b, free = banks.take()
            for t in range(DT):
                buf, bfree = bufs.take()
                sq = fn(tmp[:, buf, 0:n], x[:, t, 0:n], ACT.Square, [x_ready[t], bfree])
                done = mm(psum[:, b, 0:n], mean, tmp[:, buf, 0:n], t == 0, t == DT - 1, [sq, free, got_cst], True)
                bufs.give(buf, [done])
            r = fn(rstd[:, 0:n], psum[:, b, 0:n], ACT.Sqrt, [done, rstd_free], bias=eps)
            banks.give(b, [r])
            return dve.do(lambda e: e.reciprocal(rstd[:, 0:n], rstd[:, 0:n]), [r])

        rstd_free = []

        def modulate(rows_of_sets, chunk, hi, lo):
            n = S * len(rows_of_sets)
            r = rms_scale(n)
            tickets = []
            for t in range(DT):
                buf, bfree = bufs.take()
                his, los = [], []
                for i, row in enumerate(rows_of_sets):
                    c = slice(i * S, (i + 1) * S)
                    u = tmp[:, buf, c]
                    g = stt(u, x[:, t, c], gain_col(row, chunk + 1, t), rstd[:, c], ALU.mult, ALU.mult,
                            [r, x_ready[t], bfree, mod_ready[row, chunk + 1]])
                    sh = column(row, chunk, t)
                    his.append(fn(hi[:, t, c], u, ACT.Identity, [g, mod_ready[row, chunk]], bias=sh))
                    los.append(low(hi[:, t, c], lo[:, t, c], (u, sh, ALU.add), [his[-1], mod_ready[row, chunk]]))
                bufs.give(buf, his + los)
                tickets.append(his + los)
            rstd_free[:] = [g]
            return hi, lo, tickets

        def add_to_x(o, m0, done, chunk, rows_of_sets, b, k_banks):
            seen = []
            for m in range(2):
                t = m0 + m
                parts = []
                for i, row in enumerate(rows_of_sets):
                    c = slice(i * S, (i + 1) * S)
                    parts.append(stt(x[:, t, c], o[:, m, c], column(row, chunk, t), x[:, t, c], ALU.mult, ALU.add,
                                     [done, x_ready[t], mod_ready[row, chunk]]))
                x_ready[t] = parts
                seen += parts
            banks.give(b, seen, k_banks)

        def norm_rope(src, w, done, gain_ap, dest, rot, rope_w, after):
            b1, f1 = bufs.take()
            sq = fn(tmp[:, b1, 0:w], src, ACT.Square, [done, f1])
            pb, pfree = banks.take()
            ms = mm(psum[:, pb, 0:w], headmean, tmp[:, b1, 0:w], True, True, [sq, pfree], True)
            b2, f2 = bufs.take()
            r = fn(tmp[:, b2, 0:w], psum[:, pb, 0:w], ACT.Sqrt, [ms, f2], bias=eps)
            banks.give(pb, [r])
            r = dve.do(lambda e: e.reciprocal(tmp[:, b2, 0:w], tmp[:, b2, 0:w]), [r])
            n = stt(tmp[:, b1, 0:w], src, gain_ap, tmp[:, b2, 0:w], ALU.mult, ALU.mult, [r, ms, par_ready])
            pb, pfree = banks.take()
            turned = mm(psum[:, pb, 0:rope_w], rot, tmp[:, b1, 0:rope_w], True, True, [n, pfree], True)
            tiles = rope_w // S
            wide = lambda ap: ap.rearrange("p (m n) -> p m n", n=S)
            tab = lambda i: spread(rope_tab[:, i, :], 1, [P, tiles, S])
            s = tt(dve, wide(tmp[:, b2, 0:rope_w]), wide(psum[:, pb, 0:rope_w]), tab(1), ALU.mult,
                   [turned, rope_ready])
            banks.give(pb, [s])
            c = tt(pool, wide(tmp[:, b1, 0:rope_w]), wide(tmp[:, b1, 0:rope_w]), tab(0), ALU.mult,
                   [turned, rope_ready])
            q = tt(dve, dest[:, 0:rope_w], tmp[:, b1, 0:rope_w], tmp[:, b2, 0:rope_w], ALU.add, [s, c, after])
            ends = [q]
            if rope_w < w:
                ends.append(dve.do(lambda e: e.tensor_copy(dest[:, rope_w:w], tmp[:, b1, rope_w:w]), [n, after]))
            bufs.give(b1, ends)
            bufs.give(b2, ends)
            return ends, n

        def both_halves(src, w, ready, dests, after):
            out_t = []
            for j, dup in enumerate((C_DUP0, C_DUP1)):
                pb, pfree = banks.take()
                d = mm(psum[:, pb, 0:w], cst[:, dup:dup + P], src, True, True, [ready, pfree], True)
                out_t.append(fn(dests[j], psum[:, pb, 0:w], ACT.Copy, [d, after]))
                banks.give(pb, [out_t[-1]])
            return out_t

        def values_by_token(src, w, done, dest, after):
            b1, f1 = bufs.take()
            c = fn(tmp[:, b1, 0:w], src, ACT.Copy, [done, f1])
            pb, pfree = banks.take()
            for i in range(w // P):
                d = tp(psum[:, pb, i * P:(i + 1) * P], tmp[:, b1, i * P:(i + 1) * P], ident, [c, pfree],
                       i == w // P - 1)
            bufs.give(b1, [d])
            e = fn(dest, psum[:, pb, 0:w].rearrange("p (i c) -> p i c", c=P), ACT.Copy, [d, after])
            banks.give(pb, [e])
            return e, c

        def attend(heads, nk, fill):
            kt, nb = nk // P, nk // S
            held = {}

            def score(h):
                d = heads[h]
                b, free = banks.take(nb)
                o = psum[:, b:b + nb, :].rearrange("p b c -> p (b c)").rearrange("p (q k) -> p q k", k=nk)
                for qt in range(2):
                    t = mm(o[:, qt], d["q"][:, qt * P:(qt + 1) * P], d["k"], True, True, [free, d["ready"]],
                           qt == 1)
                pb, pfree = bufs.take(nb)
                p = tmp[:, pb:pb + nb, :].rearrange("p b c -> p (b c)").rearrange("p (q k) -> p q k", k=nk)
                st = stats[:, h, :]
                if d["mask"] is not None:
                    src = p
                    t = stt(p, o, SCALE, d["mask"], ALU.mult, ALU.add, [t, pfree, got_phase])
                    banks.give(b, [t], nb)
                    t = reduce(st[:, 0:2], p, ALU.max, [t])
                    after, scale, neg = [], 1.0, -1.0
                else:
                    src, scale, neg = o, SCALE, -SCALE
                    t = reduce(st[:, 0:2], o, ALU.max, [t])
                if d["sink"] is not None:
                    t = ts(dve, st[:, 2:4], st[:, 0:2], d["sink"], neg, ALU.max, ALU.mult, [t, got_small])
                else:
                    t = ts(dve, st[:, 2:4], st[:, 0:2], neg, None, ALU.mult, None, [t])
                for qt in range(2):
                    e = fn(p[:, qt], src[:, qt], ACT.Exp, [t, pfree], bias=st[:, 2 + qt:3 + qt], scale=scale,
                           accum=st[:, 4 + qt:5 + qt])
                if d["mask"] is None:
                    banks.give(b, [e], nb)
                if d["sink"] is not None:
                    e2 = fn(st[:, 6:8], st[:, 2:4], ACT.Exp, [t], bias=d["sink"])
                    e = tt(dve, st[:, 4:6], st[:, 4:6], st[:, 6:8], ALU.add, [e, e2])
                r = dve.do(lambda e_: e_.reciprocal(st[:, 8:10], st[:, 4:6]), [e])
                for qt in range(2):
                    n = ts(pool, p[:, qt], p[:, qt], st[:, 8 + qt:9 + qt], None, ALU.mult, None, [r, e])
                held[h] = [p, pb, n]

            def turn(h):
                p, pb, n = held[h]
                b, free = banks.take(nb)
                o = psum[:, b:b + nb, :].rearrange("p b c -> p (b c)").rearrange("p (k q) -> p k q", q=S)
                for i in range(kt):
                    for qt in range(2):
                        t = tp(o[:, i, qt * P:(qt + 1) * P], p[:, qt, i * P:(i + 1) * P], ident, [free, n],
                               i == kt - 1 and qt == 1)
                bufs.give(pb, [t], nb)
                tb, tfree = bufs.take(nb)
                pt = tmp[:, tb:tb + nb, :].rearrange("p b c -> p (b c)").rearrange("p (k q) -> p k q", q=S)
                c = fn(pt, o, ACT.Copy, [t, tfree])
                banks.give(b, [c], nb)
                held[h] = [pt, tb, c]

            def weigh(h):
                d = heads[h]
                pt, tb, c = held.pop(h)
                if h % 2 == 0:
                    held["o"] = banks.take()
                b, free = held["o"]
                base = HD * (h % 2)
                for i in range(kt):
                    t = mm(psum[base:base + HD, b, 0:S], d["v"](i), pt[:, i, :], i == 0, i == kt - 1,
                           [free, c, d["ready"]], i == kt - 1)
                bufs.give(tb, [t], nb)
                if h % 2:
                    j = d["tile"]
                    hi = fn(u_hi1[:, j, :], psum[:, b, 0:S], ACT.Copy, [t, o_free])
                    lo = low(u_hi1[:, j, :], u_lo1[:, j, :], psum[:, b, 0:S], [hi, o_free])
                    banks.give(b, [hi, lo])
                    o_ready[j] = [hi, lo]

            o_ready = [None] * DT
            for i in range(len(heads) + 2):
                if i < len(heads):
                    score(i)
                if 1 <= i <= len(heads):
                    turn(i - 1)
                if i >= 2:
                    weigh(i - 2)
                fill(i)
            return u_hi1, u_lo1, o_ready

        o_free = [x_ready[t] for t in range(DT)]
        small_gain = lambda row: par[:, 2, row:row + 1]

        last_readers = list(o_free)
        for l in range(2):
            if l == 0:
                while fed["plan"] < 8:
                    feed()
                finish_mods()
            h = modulate([l], 0, h_hi1, h_lo1)
            rot1 = cst[:, C_ROT1:C_ROT1 + P]
            flat2 = lambda o: o.rearrange("p m n -> p (m n)")
            qk_ready = [None] * 14
            tab_q = lambda j: qk[:, j:j + 2, :].rearrange("p m n -> p (m n)")
            for j in range(2):
                b, kb, o, done = product("in", h, S)
                t, n = norm_rope(flat2(o), 512, done, small_gain(R_HEAD + l), tab_q(2 * j), rot1, 512, last_readers)
                banks.give(b, [n])
                qk_ready[2 * j] = qk_ready[2 * j + 1] = t
            b, kb, o, done = product("in", h, S)
            kbuf, kfree = bufs.take()
            t, n = norm_rope(o[:, 0], S, done, small_gain(R_HEAD + 2 + l), tmp[:, kbuf, 0:S], rot1, S, kfree)
            qk_ready[4], qk_ready[5] = both_halves(tmp[:, kbuf, 0:S], S, t, [qk[:, 4, :], qk[:, 5, :]], last_readers)
            bufs.give(kbuf, [qk_ready[4], qk_ready[5]])
            va = v_tok[:, 0:256].rearrange("p (i c) -> p i c", c=P)
            va_ready, c = values_by_token(o[:, 1], S, done, va, last_readers)
            banks.give(b, [n, c])
            for part, first in (("q", 6), ("k", 10)):
                for j in range(2):
                    b, kb, o, done = product("in", h, S)
                    row = R_HEAD + (4 if part == "q" else 6) + l
                    t, n = norm_rope(flat2(o), 512, done, small_gain(row), tab_q(first + 2 * j), rot1, 512,
                                     last_readers)
                    banks.give(b, [n])
                    qk_ready[first + 2 * j] = qk_ready[first + 2 * j + 1] = t
            vb = v_tok[:, 256:1280].rearrange("p (i c) -> p i c", c=512)
            vb_ready = []
            for j in range(2):
                b, kb, o, done = product("in", h, S)
                cs = []
                for m in range(2):
                    f = (2 * j + m) * P
                    t, c = values_by_token(o[:, m], S, done, vb[:, :, f:f + P], last_readers)
                    vb_ready.append(t)
                    cs.append(c)
                banks.give(b, cs)

            mask = lambda i: phase_tab[:, 512 * i:512 * (i + 1)].rearrange("p (q k) -> p q k", k=S)
            heads = []
            for i in range(8):
                rows_ = slice(HD * (i % 2), HD * (i % 2) + HD)
                kv = i // 4
                heads.append(dict(q=qk[rows_, i // 2, :], k=qk[rows_, 4 + kv, :], tile=i // 2, mask=mask(1),
                                  v=lambda kt, kv=kv: va[:, kt, kv * HD:(kv + 1) * HD],
                                  sink=sink[:, 8 * l + i:8 * l + i + 1],
                                  ready=[qk_ready[i // 2], qk_ready[4 + kv], va_ready]))
            for i in range(8):
                rows_ = slice(HD * (i % 2), HD * (i % 2) + HD)
                heads.append(dict(q=qk[rows_, 6 + i // 2, :], k=qk[rows_, 10 + i // 2, :], tile=4 + i // 2,
                                  v=lambda kt, i=i: vb[:, kt, i * HD:(i + 1) * HD], mask=mask(0), sink=None,
                                  ready=[qk_ready[6 + i // 2], qk_ready[10 + i // 2], vb_ready]))
            gate_ready = []

            def fill(i):
                if i % 2 == 0 and len(gate_ready) < 8:
                    b, kb, o, done = product("in", h, S)
                    j = len(gate_ready)
                    t = fn(gate_tanh[:, 2 * j:2 * j + 2, :], o, ACT.Tanh, [done, h_free], scale=0.5)
                    banks.give(b, [t])
                    gate_ready.append(t)

            h_free = last_readers
            att = attend(heads, S, fill)
            assert len(gate_ready) == 8
            mixed_ready = [None] * DT
            for j in range(4):
                s, ready = unit("o")
                outs = []
                for part in range(2):
                    b, free = banks.take()
                    o = psum[:, b, :].rearrange("p (m n) -> p m n", n=S)
                    for m in range(2):
                        for i in range(4):
                            k = 4 * part + i
                            wh, wl = w_hi[:, s, k, m * P:(m + 1) * P], w_lo[:, s, k, m * P:(m + 1) * P]
                            xh, xl = att[0][:, k, :], att[1][:, k, :]
                            mm(o[:, m], wh, xh, i == 0, False, [ready[0], free, att[2][k]])
                            mm(o[:, m], wh, xl, False, False)
                            done = mm(o[:, m], wl, xh, False, i == 3, [ready[1]], m == 1 and i == 3)
                    outs.append((b, o, done))
                split_free[s] = [done]
                bb, bfree = bufs.take(2)
                ya = tmp[:, bb, :].rearrange("p (m n) -> p m n", n=S)
                yb = tmp[:, bb + 1, :].rearrange("p (m n) -> p m n", n=S)
                t = []
                for part, y in enumerate((ya, yb)):
                    b, o, done = outs[part]
                    g = gate_tanh[:, 8 * part + 2 * j:8 * part + 2 * j + 2, :]
                    t.append(stt(y, g, 1.0, o, ALU.add, ALU.mult, [done, gate_ready[4 * part + j], bfree]))
                    banks.give(b, [t[-1]])
                t = tt(pool, ya, ya, yb, ALU.add, [t])
                c = slice(2 * j, 2 * j + 2)
                hi = fn(h_hi1[:, c, :], ya, ACT.Copy, [t], scale=0.5)
                lo = low(h_hi1[:, c, :], h_lo1[:, c, :], (ya, 0.5, ALU.mult), [hi])
                bufs.give(bb, [hi, lo], 2)
                mixed_ready[2 * j] = mixed_ready[2 * j + 1] = [hi, lo]
            for j in range(4):
                b, kb, o, done = product("out", (h_hi1, h_lo1, mixed_ready), S)
                add_to_x(o, 2 * j, done, 2, [l], b, kb)

            h = modulate([l], 3, h_hi1, h_lo1)
            for g in range(4):
                u_ready = [None] * DT
                for j in range(4):
                    b, kb, o, done = product("up", h, S)
                    buf, bfree = bufs.take()
                    r = tmp[:, buf, :].rearrange("p (m n) -> p m n", n=S)
                    t = fn(r, o, ACT.Relu, [done, bfree])
                    t = stt(r, o, 0.0, r, ALU.max, ALU.mult, [t])
                    banks.give(b, [t])
                    c = slice(2 * j, 2 * j + 2)
                    hi = fn(u_hi1[:, c, :], r, ACT.Copy, [t, done])
                    lo = low(u_hi1[:, c, :], u_lo1[:, c, :], r, [hi])
                    bufs.give(buf, [hi, lo])
                    u_ready[2 * j] = u_ready[2 * j + 1] = [hi, lo]
                for j in range(4):
                    b, kb, o, done = product("down", (u_hi1, u_lo1, u_ready), S)
                    add_to_x(o, 2 * j, done, 5, [l], b, kb)
            last_readers = [done]
            o_free = [done]

        pool_tab = act.load(phase_tab[:], a["consts"][:, C_POOL:C_POOL + 1024], mark("d_phase"), [done])
        rope_load = act.load(rope_tab[:].rearrange("p a c -> p (a c)"), a["consts"][:, C_COS2:C_COS2 + 512],
                             mark("d_rope"), [done])

        def route(layer, n, h):
            T = n // P
            b, free = banks.take()
            lg_p = psum[:, b, 0:T * 20].rearrange("p (i c) -> p i c", c=20)
            for i in range(T):
                for k in range(DT):
                    for part in range(2):
                        t = mm(lg_p[:, i], plain(h[part][:, k, i * P:(i + 1) * P]), w_route[:, layer, k, :],
                               k == 0 and part == 0, k == DT - 1 and part == 1, [free, h[2][k], got_small],
                               i == T - 1 and k == DT - 1)
            buf, bfree = bufs.take()
            area = [0]

            def room(*shape):
                size = int(np.prod(shape))
                ap = tmp[:, buf, area[0]:area[0] + size]
                area[0] += size
                assert area[0] <= 512
                if len(shape) == 2:
                    return ap.rearrange("p (i c) -> p i c", c=shape[1])
                return ap

            N4, N16 = [P, T, 4], [P, T, N_EXP]
            lg = room(T, 20)
            t = tt(dve, lg, lg_p, spread(b_route[:, layer, :], 1, [P, T, 20]), ALU.add, [t, got_small, bfree])
            banks.give(b, [t])
            gl, el = lg[:, :, 0:4], lg[:, :, 4:20]
            iota4 = spread(cst[:, C_IOTA:C_IOTA + 4], 1, N4)
            iota16 = spread(cst[:, C_IOTA:C_IOTA + N_EXP], 1, N16)

            def first_of_max(v, wide, iota, t):
                m, d, at_, one, least = room(T), room(T, wide), room(T, wide), room(T, wide), room(T)
                shape = [P, T, wide]
                t = reduce(m, v, ALU.max, [t])
                td = tt(dve, d, v, spread(m, 2, shape), ALU.subtract, [t])
                t = ts(dve, one, d, 0.0, -64.0, ALU.is_ge, ALU.mult, [td])
                t = tt(dve, at_, one, iota, ALU.add, [t])
                t = reduce(least, at_, ALU.min, [t])
                t = tt(dve, one, at_, spread(least, 2, shape), ALU.is_equal, [t])
                return m, d, one, t, td

            _, d, group, t, td = first_of_max(gl, 4, iota4, t)
            eg, sg, gw = room(T, 4), room(T), room(T)
            e = fn(eg, d, ACT.Exp, [td])
            e = reduce(sg, eg, ALU.add, [e])
            gw_t = dve.do(lambda e_: e_.reciprocal(gw, sg), [e])
            pen = room(T, 4)
            t = ts(dve, pen, group, -1.0, 1e30, ALU.add, ALU.mult, [t])
            by_group = lambda ap: ap.rearrange("p i (g c) -> p i g c", c=4)
            inside = room(T, N_EXP)
            for i in range(T):
                ti = tt(dve, inside[:, i].rearrange("p (g c) -> p g c", c=4),
                        el[:, i].rearrange("p (g c) -> p g c", c=4), spread(pen[:, i], 2, [P, 4, 4]), ALU.add, [t])
            t = ti
            m1, _, one1, t, _ = first_of_max(inside, N_EXP, iota16, t)
            t = stt(inside, one1, -2e30, inside, ALU.mult, ALU.add, [t])
            area2, fr2 = bufs.take()
            first_buf = buf
            buf, area[0] = area2, 0
            t2 = [t, fr2]
            m2, _, one2, t, _ = first_of_max(inside, N_EXP, iota16, t2)
            dm, ex, den = room(T), room(T), room(T)
            td = tt(dve, dm, m2, m1, ALU.subtract, [t])
            e = fn(ex, dm, ACT.Exp, [td])
            td = ts(dve, den, ex, 1.0, None, ALU.add, None, [e])
            td = dve.do(lambda e_: e_.reciprocal(den, den), [td])
            td = tt(dve, den, den, gw, ALU.mult, [td, gw_t])
            t1 = tt(dve, one1, one1, spread(den, 2, N16), ALU.mult, [td, t])
            td = tt(dve, den, den, ex, ALU.mult, [td, t1])
            t2 = tt(dve, one2, one2, spread(den, 2, N16), ALU.mult, [td, t])
            t = tt(dve, one1, one1, one2, ALU.add, [t1, t2])
            b, free = banks.take()
            for i in range(T):
                d_ = tp(psum[0:N_EXP, b, i * P:(i + 1) * P], one1[:, i, :], ident, [t, free], i == T - 1)
            bufs.give(first_buf, [d_])
            bufs.give(area2, [d_])
            g = fn(gates_t[:, 0:n], psum[0:N_EXP, b, 0:n], ACT.Copy, [d_, done_all], scale=0.5)
            banks.give(b, [g])
            return g

        def moe(layer, rows_of_sets):
            sets = len(rows_of_sets)
            n = S * sets
            h_bufs = (h_hi1, h_lo1) if sets == 1 else (h_hi2, h_lo2)
            u_bufs = (u_hi1, u_lo1) if sets == 1 else (u_hi2, u_lo2)
            h = modulate(rows_of_sets, 3, *h_bufs)
            gates = route(layer, n, h)
            for g in range(4):
                u_ready = [None] * DT
                for i in range(4):
                    expert = 4 * g + i
                    ba, kb, oa, da = product("eg", h, n)
                    bb, _, ob, db = product("eu", h, n)
                    buf, bfree = bufs.take(sets)
                    u = tmp[:, buf:buf + sets, :].rearrange("p b c -> p (b c)").rearrange("p (m n) -> p m n", n=n)
                    t = fn(u, oa, ACT.Tanh, [da, bfree], scale=0.5)
                    t = stt(u, u, 1.0, oa, ALU.add, ALU.mult, [t])
                    banks.give(ba, [t], sets)
                    t = tt(dve, u, u, ob, ALU.mult, [t, db])
                    banks.give(bb, [t], sets)
                    pb, pfree = banks.take()
                    row = cst[0:N_EXP, C_IDENT + expert:C_IDENT + expert + 1].to_broadcast([N_EXP, P])
                    gd = mm(psum[:, pb, 0:n], row, gates_t[:, 0:n], True, True, [gates, pfree], True)
                    t = tt(dve, u, u, spread(psum[:, pb, 0:n], 1, [P, 2, n]), ALU.mult, [t, gd])
                    banks.give(pb, [t])
                    c = slice(2 * i, 2 * i + 2)
                    hi = fn(u_bufs[0][:, c, :], u, ACT.Copy, [t])
                    lo = low(u_bufs[0][:, c, :], u_bufs[1][:, c, :], u, [hi])
                    bufs.give(buf, [hi, lo], sets)
                    u_ready[2 * i] = u_ready[2 * i + 1] = [hi, lo]
                for j in range(4):
                    b, kb, o, done = product("ed", (*u_bufs, u_ready), n)
                    add_to_x(o, 2 * j, done, 5, rows_of_sets, b, kb)
            return done

        done_all = []
        sets = [2, 4]
        r = rms_scale(S2)
        pool_ready = []
        PAD = 8
        fw = S + 2 * PAD
        pscale, pbias = gain[:, 10, :], gain[:, 11, :]
        pool_cols = []
        for i, row in enumerate(sets):
            sc = cond_t[:, i, :]
            pool_cols.append(sc)
        pool_rows = {}

        for t in range(DT):
            g = t // 2
            hb, hfree = bufs.take(2)
            sbuf_, sfree = bufs.take(2)
            hp = tmp[:, hb:hb + 2, :].rearrange("p b c -> p (b c)")[:, 0:2 * fw].rearrange("p (s c) -> p s c", s=2)
            sw = tmp[:, sbuf_:sbuf_ + 2, :].rearrange("p b c -> p (b c)")[:, 0:2 * fw].rearrange("p (s c) -> p s c",
                                                                                              s=2)
            z = pool.do(lambda e, hp=hp: e.memset(hp, 0.0), [hfree])
            hs = []
            for i, row in enumerate(sets):
                c = slice(i * S, (i + 1) * S)
                v = hp[:, i, PAD:PAD + S]
                q = stt(v, x[:, t, c], gain_col(row, 1, t), rstd[:, c], ALU.mult, ALU.mult,
                        [r, x_ready[t], z, mod_ready[row, 1]])
                hs.append(fn(v, v, ACT.Identity, [q, mod_ready[row, 0]], bias=column(row, 0, t)))
            rstd_free[:] = [q]
            cur = tt(dve, sw[:, :, 1:fw], hp[:, :, 0:fw - 1], hp[:, :, 1:fw], ALU.add, [hs, sfree])
            lo_i, hi_i, half = 1, fw, 1
            src = sw
            spare, spfree = bufs.take(2)
            sv = tmp[:, spare:spare + 2, :].rearrange("p b c -> p (b c)")[:, 0:2 * fw].rearrange("p (s c) -> p s c",
                                                                                               s=2)
            dst = sv
            cur = [cur, spfree]
            for step in range(g):
                a0, a1 = lo_i + half, hi_i - half
                cur = tt(dve, dst[:, :, a0:a1], src[:, :, a0 - half:a1 - half], src[:, :, a0 + half:a1 + half],
                         ALU.add, [cur])
                lo_i, hi_i, half = a0, a1, 2 * half
                src, dst = dst, src
            rc = spread(phase_tab[:, g * S:(g + 1) * S], 1, [P, 2, S])
            cur = tt(dve, dst[:, :, PAD:PAD + S], src[:, :, PAD:PAD + S], rc, ALU.mult, [cur, pool_tab])
            cur = tt(dve, src[:, :, PAD:PAD + S], dst[:, :, PAD:PAD + S], hp[:, :, PAD:PAD + S], ALU.subtract, [cur])
            hi_ap = h_hi2[:, t, :].rearrange("p (s c) -> p s c", s=2)
            lo_ap = h_lo2[:, t, :].rearrange("p (s c) -> p s c", s=2)
            hi = fn(hi_ap, src[:, :, PAD:PAD + S], ACT.Copy, [cur, last_readers])
            lo = low(hi_ap, lo_ap, src[:, :, PAD:PAD + S], [hi])
            for bf in (hb, sbuf_, spare):
                bufs.give(bf, [hi, lo], 2)
            pool_ready.append([hi, lo])
        s, ready = unit("pool")
        while (2, 2) not in mod_ready or (4, 2) not in mod_ready:
            feed()
            finish_mods()
        for i, row in enumerate(sets):
            t1 = tt(dve, cond_t[:, i, :], mod[:, row, 2 * DT:3 * DT], par[:, 2, 8:16], ALU.mult,
                    [mod_ready[row, 2], cond_ready])
        scale_ready = [t1]
        for g in range(4):
            b, free = banks.take(2)
            o = psum[:, b:b + 2, :]
            for m in range(2):
                for i in range(2):
                    k = 2 * g + i
                    wh, wl = w_hi[:, s, k, m * P:(m + 1) * P], w_lo[:, s, k, m * P:(m + 1) * P]
                    xh, xl = h_hi2[:, k, :], h_lo2[:, k, :]
                    mm(o[:, m], wh, xh, i == 0, False, [ready[0], free, pool_ready[k]])
                    mm(o[:, m], wh, xl, False, False)
                    done = mm(o[:, m], wl, xh, False, i == 1, [ready[1]], m == 1 and i == 1)
            seen = []
            for m in range(2):
                t = 2 * g + m
                buf, bfree = bufs.take()
                u = tmp[:, buf, :]
                parts = []
                bias = par[:, 2, t:t + 1]
                for i in range(2):
                    c = slice(i * S, (i + 1) * S)
                    q = ts(dve, u[:, c], o[:, m, c], bias, cond_t[:, i, t:t + 1], ALU.add, ALU.mult,
                           [done, bfree, scale_ready])
                    seen.append(q)
                    parts.append(tt(dve, x[:, t, c], u[:, c], x[:, t, c], ALU.add, [q, x_ready[t]]))
                x_ready[t] = parts
                bufs.give(buf, parts)
            banks.give(b, seen, 2)
        split_free[s] = [done]
        done_all = [moe(0, sets)]

        h = modulate([3, 5], 0, h_hi2, h_lo2)
        rope_ready = rope_load
        rot2 = cst[:, C_ROT2:C_ROT2 + P]
        q_ready = [None] * 8
        for j in range(4):
            b, kb, o, done = product("qkv", h, S)
            t, n = norm_rope(o.rearrange("p m n -> p (m n)"), 512, done, small_gain(R_HEAD + 8),
                             q_att[:, 2 * j:2 * j + 2, :].rearrange("p m n -> p (m n)"), rot2, 512, [done])
            banks.give(b, [n])
            q_ready[2 * j] = q_ready[2 * j + 1] = t
        b, kb, o, done = product("qkv", h, S2)
        k_ready = []
        for m in range(2):
            kbuf, kfree = bufs.take()
            t, n = norm_rope(o[:, m], S2, done, small_gain(R_HEAD + 9), tmp[:, kbuf, :], rot2, S, kfree)
            banks.give(b + m, [n])
            ts_ = both_halves(tmp[:, kbuf, :], S2, t, [k_att[:, 2 * m, :], k_att[:, 2 * m + 1, :]], [done])
            bufs.give(kbuf, ts_)
            k_ready += ts_
        vv = v_tok[:, 0:1024].rearrange("p (i c) -> p i c", c=256)
        b, kb, o, done = product("qkv", h, S2)
        v_ready = []
        for m in range(2):
            t, c = values_by_token(o[:, m], S2, done, vv[:, :, m * P:(m + 1) * P], [])
            v_ready.append(t)
            banks.give(b + m, [c])
        heads = []
        for i in range(16):
            rows_ = slice(HD * (i % 2), HD * (i % 2) + HD)
            kv = i // 4
            heads.append(dict(q=q_att[rows_, i // 2, :], k=k_att[rows_, kv, :], tile=i // 2, mask=None, sink=None,
                              v=lambda kt, kv=kv: vv[:, kt, kv * HD:(kv + 1) * HD],
                              ready=[q_ready[i // 2], k_ready[kv], v_ready]))
        o_free = [done]
        att = attend(heads, S2, lambda i: None)
        for j in range(4):
            b, kb, o, done = product("wo", att, S)
            add_to_x(o, 2 * j, done, 2, [3], b, kb)
        moe(1, [3])
        assert fed["plan"] == len(plan) and fed["used"] == len(gemms)

        outs = []
        for i in range(2):
            buf, bfree = bufs.take(2)
            o_tok = tmp[:, buf:buf + 2, :].rearrange("p b c -> p (b c)")
            cs = []
            for half in range(2):
                b, free = banks.take()
                for t in range(4):
                    k = 4 * half + t
                    d = tp(psum[:, b, t * P:(t + 1) * P], x[:, k, i * P:(i + 1) * P], ident, [x_ready[k], free], t == 3)
                cs.append(fn(o_tok[:, 512 * half:512 * (half + 1)], psum[:, b, :], ACT.Copy, [d, bfree]))
                banks.give(b, [cs[-1]])
            outs.append(sp.load(out[0, i * P:(i + 1) * P, :], o_tok, mark(f"d_out{i}"), cs))
            bufs.give(buf, [outs[-1]], 2)
        sp.wait(*outs)

        block = ctx.enter_context(nc.Block())

        def run(lane):
            def body(engine):
                for step in lane.steps:
                    step(engine)
            return body

        block.sync(run(sp))
        block.tensor(run(pe))
        block.scalar(run(act))
        block.vector(run(dve))
        block.gpsimd(run(pool))


INPUTS = ["x", "c", "positions", "rms_mix", "rms_mlp", "w_ada", "b_ada", "w_in", "q_norm_swa", "k_norm_swa",
          "q_norm_moba", "k_norm_moba", "swa_sinks", "w_o_swa", "w_o_moba", "w_out", "w_up", "w_down", "c_2",
          "ctx_2", "c_ctx_2", "w_mod_2", "b_mod_2", "norm1_g_2", "norm2_g_2", "pool_w_2", "pool_b_2",
          "pool_ls_2", "attn_wqkv_2", "attn_qg_2", "attn_kg_2", "attn_wo_2", "moe_wrg_2", "moe_brg_2",
          "moe_wre_2", "moe_bre_2", "moe_wg_2", "moe_wu_2", "moe_wd_2"]


def kernel(**inputs):
    import concourse.bacc as bacc
    from concourse.bass_utils import run_bass_kernel_spmd

    nc = bacc.Bacc("TRN2", target_bir_lowering=False, num_devices=1, dynamic_dma_scratch_size=8192)
    arrays = {f"in_{name}": np.ascontiguousarray(inputs[name]) for name in INPUTS}
    arrays["in_consts"] = constants()
    aps = {}
    for name, arr in arrays.items():
        aps[name[3:]] = nc.dram_tensor(name, arr.shape, mybir.dt.from_np(arr.dtype), kind="ExternalInput").ap()
    out = nc.dram_tensor("out", (1, S, D), F32, kind="ExternalOutput").ap()
    build(nc, aps, out)
    result = run_bass_kernel_spmd(nc, [arrays], core_ids=[0])
    return result.results[0]["out"]
```

```python
from contextlib import ExitStack

import numpy as np
import concourse.bass as bass
from concourse import mybir

F32 = mybir.dt.float32
F32R = mybir.dt.float32r
I32 = mybir.dt.int32
ALU = mybir.AluOpType
ACT = mybir.ActivationFunctionType
AX = mybir.AxisListType

P = 128
D = 1024
DT = D // P
S = 256
S2 = 512
HD = 64
UC = 256
UNIT = DT * UC
RAW_SLOTS = 4
SPLIT_SLOTS = 3
NEG = -1e30
EPS = 1e-6
SCALE = HD ** -0.5
N_EXP = 16
WINDOW = 128
GRID_W = 64
THETA = 10000.0

C_IDENT, C_ROT1, C_ROT2, C_DUP0, C_DUP1, C_HEADMEAN, C_MEAN = (P * i for i in range(7))
C_MISC = 7 * P
C_IOTA = C_MISC + 2
C_FIXED = C_IOTA + N_EXP
C_CAUSAL = C_FIXED
C_SWA = C_CAUSAL + 512
C_COS2 = C_SWA + 512
C_SIN2 = C_COS2 + S
C_POOL = C_SIN2 + S
C_END = C_POOL + 4 * S


def constants():
    c = np.zeros((P, C_END), np.float32)
    i = np.arange(P)
    c[i, C_IDENT + i] = 1
    half = HD // 2
    for m in range(P):
        first = m % HD < half
        c[m + half if first else m - half, C_ROT1 + m] = -1 if first else 1
    quarter = HD // 4
    for m in range(P):
        first = m % half < quarter
        c[m + quarter if first else m - quarter, C_ROT2 + m] = -1 if first else 1
    c[i % HD, C_DUP0 + i] = 1
    c[HD + i % HD, C_DUP1 + i] = 1
    c[:, C_HEADMEAN:C_HEADMEAN + P] = (i[:, None] // HD == i[None, :] // HD) / HD
    c[:, C_MEAN:C_MEAN + P] = 1.0 / D
    inv = THETA ** (-np.arange(half) / half)
    c[:, C_MISC] = inv[i % half]
    c[:, C_MISC + 1] = EPS
    c[:, C_IOTA:C_IOTA + N_EXP] = np.arange(N_EXP)
    q = np.arange(2)[None, :, None] * P + i[:, None, None]
    k = np.arange(S)[None, None, :]
    c[:, C_CAUSAL:C_CAUSAL + 512] = np.where(k <= q, 0, NEG).reshape(P, 512)
    c[:, C_SWA:C_SWA + 512] = np.where((k <= q) & (q - k < WINDOW), 0, NEG).reshape(P, 512)
    inv2 = (np.float32(THETA) ** (-np.arange(0, half, 2, dtype=np.float32) / half)).astype(np.float32)
    tok = np.arange(S)
    pos = np.where((i[:, None] % HD) < half, tok // GRID_W, tok % GRID_W).astype(np.float32)
    ang = (pos * inv2[i % quarter][:, None]).astype(np.float32).astype(np.float64)
    c[:, C_COS2:C_COS2 + S] = np.cos(ang)
    c[:, C_SIN2:C_SIN2 + S] = np.sin(ang)
    for g in range(4):
        w = 2 << g
        count = np.clip(tok + w // 2, 0, S) - np.clip(tok - w // 2, 0, S)
        c[:, C_POOL + g * S:C_POOL + (g + 1) * S] = 1.0 / count
    return c


def flat(tickets):
    for t in tickets:
        if t is None:
            continue
        if isinstance(t, list):
            yield from flat(t)
        else:
            yield t


class Lane:

    def __init__(self, sem):
        self.sem, self.count, self.steps, self.seen = sem, 0, [], {}

    def wait(self, *tickets):
        for sem, value in flat(tickets):
            if self.seen.get(id(sem), 0) < value:
                self.seen[id(sem)] = value
                self.steps.append(lambda e, sem=sem, value=value: e.wait_ge(sem, value))

    def do(self, issue, after=(), signal=True):
        self.wait(*after)
        if not signal:
            self.steps.append(issue)
            return None
        self.count += 1
        self.steps.append(lambda e: issue(e).then_inc(self.sem, 1))
        return self.sem, self.count

    def load(self, dst, src, mark, after=()):
        self.wait(*after)
        mark[1] += 16
        self.steps.append(lambda e: e.dma_start(dst, src).then_inc(mark[0], 16))
        return mark[0], mark[1]


class Steps:

    def __init__(self):
        self.live, self.busy = [], []

    def start(self, gen):
        self.live.append(gen)
        self.advance(gen)

    def advance(self, gen):
        self.busy.append(gen)
        ended = next(gen, "end") == "end"
        self.busy.remove(gen)
        if ended:
            self.live.remove(gen)

    def tick(self):
        ready = [gen for gen in self.live if gen not in self.busy]
        assert ready, "nothing left to queue"
        for gen in ready:
            if gen in self.live and gen not in self.busy:
                self.advance(gen)

    def need(self, tickets, i):
        while tickets[i] is None:
            self.tick()
        return tickets[i]

    def finish(self):
        while self.live:
            self.tick()


class Ring:

    def __init__(self, n, tick):
        self.n, self.at, self.free, self.tick = n, 0, [[] for _ in range(n)], tick

    def take(self, k=1):
        while True:
            starts = [(self.at + i) % self.n for i in range(self.n)]
            for first in starts:
                if first % k == 0 and all(self.free[i] is not None for i in range(first, first + k)):
                    tickets = [t for i in range(first, first + k) for t in self.free[i]]
                    for i in range(first, first + k):
                        self.free[i] = None
                    self.at = (first + k) % self.n
                    return first, tickets
            self.tick()

    def give(self, first, tickets, k=1):
        for i in range(first, first + k):
            self.free[i] = list(tickets)


def build(nc, a, out):
    with ExitStack() as ctx:
        at = [-(-nc.sbuf_base // 64) * 64]

        def sb(name, shape, dt=F32, offset=None):
            size = 4 * int(np.prod(shape[1:]))
            if offset is None:
                offset = at[0]
                at[0] += -(-size // 64) * 64
                assert at[0] <= nc.sbuf_usable_end, (name, at[0], nc.sbuf_usable_end)
            return nc.alloc_sbuf_tensor_at(name, shape, dt, offset=offset), offset

        raw, _ = sb("raw", [P, RAW_SLOTS, UNIT])
        w_hi, _ = sb("w_hi", [P, SPLIT_SLOTS, DT, UC], F32R)
        w_lo, _ = sb("w_lo", [P, SPLIT_SLOTS, DT, UC], F32R)
        x, _ = sb("x", [P, DT, S2])
        h_hi2, big1 = sb("h_hi2", [P, DT, S2], F32R)
        h_lo2, _ = sb("h_lo2", [P, DT, S2], F32R)
        h_hi1, _ = sb("h_hi1", [P, DT, S], F32R, offset=big1)
        h_lo1, _ = sb("h_lo1", [P, DT, S], F32R, offset=big1 + 8192)
        att_room, _ = sb("att_room", [P, 8, D], F32, offset=big1)
        gate_tanh, _ = sb("gate_tanh", [P, 16, S], F32, offset=big1 + 16384)
        u_hi2, big2 = sb("u_hi2", [P, DT, S2], F32R)
        u_lo2, _ = sb("u_lo2", [P, DT, S2], F32R)
        u_hi1, _ = sb("u_hi1", [P, DT, S], F32R, offset=big2)
        u_lo1, _ = sb("u_lo1", [P, DT, S], F32R, offset=big2 + 8192)
        qk, _ = sb("qk", [P, 16, S], F32, offset=big2 + 16384)
        q_att, _ = sb("q_att", [P, 8, S], F32, offset=big2 + 16384)
        k_att, _ = sb("k_att", [P, 4, S2], F32, offset=big2 + 24576)
        pool_in, _ = sb("pool_in", [P, 15, 544], F32, offset=big2)
        tokens_in, _ = sb("tokens_in", [P, 4, D], F32, offset=big2)
        v_tok, _ = sb("v_tok", [P, 1280])
        acc, _ = sb("acc", [P, 3, D])
        tmp, _ = sb("tmp", [P, 8, 512])
        rstd, _ = sb("rstd", [P, S2])
        cst, _ = sb("cst", [P, C_FIXED])
        phase_tab, _ = sb("phase_tab", [P, 1024])
        rope_tab, _ = sb("rope_tab", [P, 2, S])
        par, _ = sb("par", [P, 3, P])
        mod, _ = sb("mod", [P, 6, 48])
        gain, _ = sb("gain", [P, 12, DT])
        cond, _ = sb("cond", [P, 3, DT])
        cond_t, _ = sb("cond_t", [P, 3, DT])
        sink, _ = sb("sink", [P, 16])
        stats, _ = sb("stats", [P, 16, 12])
        w_route, _ = sb("w_route", [P, 2, DT, 20])
        b_route, _ = sb("b_route", [P, 2, 20])
        gates_t, _ = sb("gates_t", [16, S2])
        psum = ctx.enter_context(nc.psum_tensor("psum", [P, 8, 512], F32))

        def sem(name):
            return ctx.enter_context(nc.semaphore(name))

        pe, act, dve, pool, sp = (Lane(sem(n)) for n in ("s_pe", "s_act", "s_dve", "s_pool", "s_sp"))
        steps = Steps()
        banks, bufs = Ring(8, steps.tick), Ring(8, steps.tick)
        marks = {}

        def mark(name):
            if name not in marks:
                marks[name] = [sem(name), 0]
            return marks[name]

        def mm(o, lhs, rhs, start, stop, after=(), signal=False):
            return pe.do(lambda e: e.matmul(o, lhs, rhs, start=start, stop=stop, skip_group_check=True),
                         after, signal)

        def tp(o, i, ident, after=(), signal=False):
            return pe.do(lambda e: e.transpose(o, i, ident), after, signal)

        def fn(o, i, func, after=(), bias=None, scale=1.0, accum=None):
            kw = {"scale": scale}
            if bias is not None:
                kw["bias"] = bias
            if accum is not None:
                kw["accum_out"] = accum
            return act.do(lambda e: e.activation(o, i, func, **kw), after)

        def tt(lane, o, i0, i1, op, after=()):
            return lane.do(lambda e: e.tensor_tensor(o, i0, i1, op), after)

        def ts(lane, o, i, s1, s2, op0, op1, after=()):
            if s2 is None:
                return lane.do(lambda e: e.tensor_scalar(o, i, s1, None, op0), after)
            return lane.do(lambda e: e.tensor_scalar(o, i, s1, s2, op0, op1), after)

        def stt(o, i0, s, i1, op0, op1, after=()):
            return dve.do(lambda e: e.scalar_tensor_tensor(out=o, in0=i0, scalar=s, in1=i1, op0=op0, op1=op1),
                          after)

        def reduce(o, i, op, after=()):
            return dve.do(lambda e: e.tensor_reduce(o, i, AX.X, op), after)

        def spread(ap, axis, shape):
            return ap.unsqueeze(axis).to_broadcast(shape)

        def plain(ap):
            return ap.bitcast(F32)

        def low(hi, lo, value_op, after):
            if isinstance(value_op, tuple):
                i0, s, op = value_op
                return stt(lo, i0, s, plain(hi), op, ALU.subtract, after)
            return tt(dve, lo, value_op, plain(hi), ALU.subtract, after)

        ident = cst[:, C_IDENT:C_IDENT + P]
        mean = cst[:, C_MEAN:C_MEAN + P]
        headmean = cst[:, C_HEADMEAN:C_HEADMEAN + P]
        eps = cst[:, C_MISC + 1:C_MISC + 2]

        got_cst = act.load(cst[:], a["consts"][:, 0:C_FIXED], mark("d_cst"))
        tok_mark = [mark(f"d_tok{i}") for i in range(4)]
        got_tok = []
        for i in range(4):
            src = a["x"][0] if i < 2 else a["ctx_2"][0]
            got_tok.append(act.load(tokens_in[:, i, :], src[(i % 2) * P:(i % 2 + 1) * P, :], tok_mark[i]))
        rows = tmp[:, 0, 0:3 * P].rearrange("p (r c) -> p r c", r=3)
        row_free = [bufs.take(1) for _ in range(2)]

        def param_rows(dst_row, block, arr, n):
            return sp.load(rows[dst_row:dst_row + n, block, :], arr.rearrange("(r c) -> r c", c=P),
                           mark(f"d_par{block}"))

        got_rows = [None] * 3
        param_rows(0, 2, a["pool_b_2"][0].rearrange("g c -> (g c)"), 8)
        param_rows(8, 2, a["pool_ls_2"][0], 8)
        param_rows(16, 2, a["c"][0], 8)
        param_rows(24, 2, a["c_2"][0], 8)
        param_rows(32, 2, a["c_ctx_2"], 8)
        R_HEAD = 40
        for j, name in enumerate(("q_norm_swa", "k_norm_swa", "q_norm_moba", "k_norm_moba")):
            for half in range(2):
                sp.load(rows[R_HEAD + 2 * j:R_HEAD + 2 * j + 2, 2, half * HD:(half + 1) * HD], a[name],
                        mark("d_par2"))
        for j, name in enumerate(("attn_qg_2", "attn_kg_2")):
            for half in range(2):
                got_rows[2] = sp.load(rows[R_HEAD + 8 + j:R_HEAD + 9 + j, 2, half * HD:(half + 1) * HD], a[name],
                                      mark("d_par2"))
        for layer in range(2):
            r = 64 * layer
            for block, names in ((0, ("rms_mix", "rms_mlp", "b_ada")), (1, ("norm1_g_2", "norm2_g_2", "b_mod_2"))):
                param_rows(r, block, a[names[0]][layer], 8)
                param_rows(r + 8, block, a[names[1]][layer], 8)
                got_rows[block] = param_rows(r + 16, block, a[names[2]][layer], 48)
        N_ROWS = (P, P, R_HEAD + 10)
        pos_i = tmp[:, 1, 0:S].bitcast(I32)
        got_pos = act.load(pos_i, a["positions"][0].partition_broadcast(P), mark("d_pos"))
        got_phase = act.load(phase_tab[:], a["consts"][:, C_CAUSAL:C_CAUSAL + 1024], mark("d_phase"))
        pool.load(sink[:], a["swa_sinks"].rearrange("l h -> (l h)").partition_broadcast(P), mark("d_small"))
        for layer in range(2):
            pool.load(w_route[:, layer, :, 0:4], a["moe_wrg_2"][layer].rearrange("(k p) c -> p k c", p=P),
                      mark("d_small"))
            pool.load(w_route[:, layer, :, 4:20], a["moe_wre_2"][layer].rearrange("(k p) c -> p k c", p=P),
                      mark("d_small"))
            pool.load(b_route[:, layer, 0:4], a["moe_brg_2"][layer].partition_broadcast(P), mark("d_small"))
            got_small = pool.load(b_route[:, layer, 4:20], a["moe_bre_2"][layer].partition_broadcast(P),
                                  mark("d_small"))

        def unit_of(w, k0, c0, k=DT):
            return w[k0 * P:(k0 + k) * P, c0:c0 + UC].rearrange("(k p) c -> p k c", p=P)

        plan = []

        def plan_gemm(name, w, k0, c0):
            plan.append(("gemm", name, [(0, DT, unit_of(w, k0, c0))]))

        mod_items = []
        for layer in range(4):
            for chunk in ((1, 0, 2, 4, 3, 5)):
                for pair in range(4):
                    mod_items.append(("mod", layer, chunk, pair))

        gemms = []
        for l in range(2):
            for j in range(4352 // UC):
                gemms.append(("in", [(0, DT, unit_of(a["w_in"][l], 0, j * UC))]))
            for j in range(4):
                gemms.append(("o", [(0, 4, unit_of(a["w_o_swa"][l], 0, j * UC, 4)),
                                    (4, 4, unit_of(a["w_o_moba"][l], 0, j * UC, 4))]))
            for j in range(4):
                gemms.append(("out", [(0, DT, unit_of(a["w_out"][l], 0, j * UC))]))
            for g in range(4):
                for j in range(4):
                    gemms.append(("up", [(0, DT, unit_of(a["w_up"][l], 0, g * D + j * UC))]))
                for j in range(4):
                    gemms.append(("down", [(0, DT, unit_of(a["w_down"][l], g * DT, j * UC))]))
        for l in range(2):
            if l == 0:
                gemms.append(("pool", [(0, DT, unit_of(a["pool_w_2"][0].rearrange("g c d -> (g c) d"), 0, 0))]))
            else:
                for j in range(6):
                    gemms.append(("qkv", [(0, DT, unit_of(a["attn_wqkv_2"][0], 0, j * UC))]))
                for j in range(4):
                    gemms.append(("wo", [(0, DT, unit_of(a["attn_wo_2"][0], 0, j * UC))]))
            w_dn = a["moe_wd_2"][l].rearrange("e f d -> (e f) d")
            for g in range(4):
                for e in range(4 * g, 4 * g + 4):
                    gemms.append(("eg", [(0, DT, unit_of(a["moe_wg_2"][l, e], 0, 0))]))
                    gemms.append(("eu", [(0, DT, unit_of(a["moe_wu_2"][l, e], 0, 0))]))
                for j in range(4):
                    gemms.append(("ed", [(0, DT, unit_of(w_dn, g * DT, j * UC))]))
        sent = 8
        plan += mod_items[:sent]
        for i, (name, parts) in enumerate(gemms):
            want = min(len(mod_items), 8 + int(0.56 * (i + 1)))
            while sent < want:
                plan.append(mod_items[sent])
                sent += 1
            plan.append(("gemm", name, parts))
        assert sent == len(mod_items)

        raw_mark = [mark(f"d_raw{i}") for i in range(RAW_SLOTS)]
        raw_free = [[] for _ in range(RAW_SLOTS)]
        split_free = [[] for _ in range(SPLIT_SLOTS)]
        accs = Ring(3, steps.tick)
        fed = {"plan": 0, "gemm": 0, "used": 0}
        split_ready = {}
        mod_sources = [a["w_ada"][0], a["w_ada"][1], a["w_mod_2"][0], a["w_mod_2"][1]]
        cond_of = lambda layer, chunk: ([(0, layer)] if layer < 2 else
                                        [(1, layer)] + ([(2, layer + 2)] if layer == 2 or chunk < 2 else []))
        mod_acc, mod_ready = {}, {}
        mod_lane, mod_turn = {}, [0]
        cond_ready = []

        lows = []

        def feed_low():
            g, slot, s, landed, t_hi = lows.pop(0)
            t_lo = low(w_hi[:, s].rearrange("p k c -> p (k c)"), w_lo[:, s].rearrange("p k c -> p (k c)"),
                       raw[:, slot, :], [landed, t_hi])
            raw_free[slot] = [t_hi, t_lo]
            split_ready[g] = [t_hi, t_lo]

        def feed():
            item = plan[fed["plan"]]
            slot = fed["plan"] % RAW_SLOTS
            if raw_free[slot] is None:
                feed_low()
            fed["plan"] += 1
            if item[0] == "gemm":
                flat_dst = raw[:, slot, :].rearrange("p (k c) -> p k c", c=UC)
                for k0, k, src in item[2]:
                    landed = sp.load(flat_dst[:, k0:k0 + k, :], src, raw_mark[slot], [raw_free[slot]])
                s = fed["gemm"] % SPLIT_SLOTS
                src = raw[:, slot, :]
                hi = w_hi[:, s].rearrange("p k c -> p (k c)")
                t_hi = fn(hi, src, ACT.Copy, [landed, split_free[s]])
                lows.append((fed["gemm"], slot, s, landed, t_hi))
                raw_free[slot] = None
                fed["gemm"] += 1
                if len(lows) > 1:
                    feed_low()
                return
            _, layer, chunk, pair = item
            dst = raw[:, slot, :].rearrange("p (k c) -> p k c", c=D)
            src = mod_sources[layer][2 * pair * P:(2 * pair + 2) * P, chunk * D:(chunk + 1) * D]
            landed = sp.load(dst, src.rearrange("(k p) c -> p k c", p=P), raw_mark[slot], [raw_free[slot]])
            last = []
            conds = cond_of(layer, chunk)
            for n_cond, (which, row) in enumerate(conds):
                if pair == 0:
                    mod_acc[row] = list(accs.take()) + [None]
                    mod_turn[0] += 1
                    mod_lane[row] = (mod_turn[0] > 2 and mod_turn[0] % 2) if len(conds) == 1 else n_cond
                buf, free, before = mod_acc[row]
                a_buf = acc[:, buf, :]
                for k in range(2):
                    s = cond[:, which, 2 * pair + k:2 * pair + k + 1]
                    first = pair == 0 and k == 0
                    if mod_lane[row] == 0:
                        if first:
                            before = ts(dve, a_buf, dst[:, k, :], s, None, ALU.mult, None,
                                        [landed, cond_ready, free])
                        else:
                            before = stt(a_buf, dst[:, k, :], s, a_buf, ALU.mult, ALU.add, [landed, before])
                    elif first:
                        before = fn(a_buf, dst[:, k, :], ACT.Copy, [landed, cond_ready, free], scale=s)
                    else:
                        t = fn(dst[:, k, :], dst[:, k, :], ACT.Copy, [landed, cond_ready, last], scale=s)
                        before = tt(pool, a_buf, a_buf, dst[:, k, :], ALU.add, [t, before])
                mod_acc[row][2] = before
                last = last + [before]
                if pair == 3:
                    steps.start(finish_mod(row, layer, chunk, buf, before))
            raw_free[slot] = last

        def finish_mod(row, layer, chunk, buf, summed):
            yield
            yield
            yield
            b, free = banks.take()
            for t in range(DT):
                done = mm(psum[:, b, t:t + 1], acc[:, buf, t * P:(t + 1) * P], mean[:, 0:1], True, True,
                          [summed, free, got_cst], t == DT - 1)
            accs.give(buf, [done])
            col = mod[:, row, chunk * DT:(chunk + 1) * DT]
            base = 64 * (layer % 2)
            bias = par[:, layer // 2, base + 16 + chunk * DT:base + 16 + (chunk + 1) * DT]
            t = stt(col, psum[:, b, 0:DT], float(D), bias, ALU.mult, ALU.add, [done, par_ready])
            banks.give(b, [t])
            if chunk in (1, 4):
                g = par[:, layer // 2, base + (chunk // 4) * 8:base + (chunk // 4) * 8 + 8]
                t = stt(gain[:, 2 * row + chunk // 4, :], col, 1.0, g, ALU.add, ALU.mult, [t])
            mod_ready[row, chunk] = t

        def need_mod(row, chunk):
            while (row, chunk) not in mod_ready:
                if not steps.live:
                    feed()
                else:
                    steps.tick()
            return mod_ready[row, chunk]

        def unit(name):
            g = fed["used"]
            assert gemms[g][0] == name, (gemms[g][0], name)
            while fed["gemm"] < min(g + SPLIT_SLOTS, len(gemms)):
                feed()
            while lows and lows[0][0] <= g + 1:
                feed_low()
            fed["used"] += 1
            s = g % SPLIT_SLOTS
            return s, split_ready[g]

        def column(row, chunk, t):
            return mod[:, row, chunk * DT + t:chunk * DT + t + 1]

        def gain_col(row, chunk, t):
            return gain[:, 2 * row + chunk // 4, t:t + 1]

        def product(name, acts, n, ktiles=None, col0=0):
            s, ready = unit(name)
            k_banks = 2 * n // 512
            b, free = banks.take(k_banks)
            o = psum[:, b:b + k_banks, :].rearrange("p b c -> p (b c)").rearrange("p (m n) -> p m n", n=n)
            hi, lo, tickets = acts
            for k in range(DT):
                steps.need(tickets, k)
                for m in range(2):
                    wh = w_hi[:, s, k, m * P:(m + 1) * P]
                    wl = w_lo[:, s, k, m * P:(m + 1) * P]
                    xh, xl = hi[:, k, col0:col0 + n], lo[:, k, col0:col0 + n]
                    mm(o[:, m], wh, xh, k == 0 and (m == 0 or k_banks == 2), False, [ready[0], free, tickets[k]])
                    mm(o[:, m], wh, xl, False, False)
                    last = m == 1 and k == DT - 1
                    done = mm(o[:, m], wl, xh, False, k == DT - 1, [ready[1]], last)
            split_free[s] = [done]
            if steps.live:
                steps.tick()
            return b, k_banks, o, done

        par_ready = []
        par_ready = [None] * 3
        for block in (2, 0, 1):
            n = N_ROWS[block]
            b, free = banks.take()
            t = tp(psum[:, b, 0:n], rows[0:n, block, :], ident[0:n, 0:n], [got_rows[block], got_cst, free], True)
            t = fn(par[:, block, 0:n], psum[:, b, 0:n], ACT.Copy, [t])
            banks.give(b, [t])
            par_ready[block] = t
            if block == 2:
                cvec = par[:, 2, 16:40].rearrange("p (v t) -> p v t", v=3)
                t = fn(cond_t[:], cvec, ACT.Tanh, [t], scale=0.5)
                t = stt(cond_t[:], cond_t[:], 1.0, cvec, ALU.add, ALU.mult, [t])
                cond_ready = [ts(dve, cond[:], cond_t[:], 0.5, None, ALU.mult, None, [t])]
        bufs.give(row_free[0][0], par_ready)

        x_ready = [[] for _ in range(DT)]
        for t in range(DT):
            b, free = banks.take()
            for i in range(4):
                done = tp(psum[:, b, i * P:(i + 1) * P], tokens_in[:, i, t * P:(t + 1) * P], ident,
                          [got_tok[i], free], i == 3)
            done = fn(x[:, t, :], psum[:, b, :], ACT.Copy, [done])
            banks.give(b, [done])
            x_ready[t] = [done]

        C1 = 6.28125
        C2 = float(np.float32(2 * np.pi - C1).view(np.uint32) & np.uint32(0xFFFFF000))
        C2 = float(np.array([int(C2)], np.uint32).view(np.float32)[0])
        C3 = float(2 * np.pi - C1 - C2)
        MAGIC = 1.5 * 2.0 ** 23
        LIMIT = 3.1415925
        pf, ang, turns = tmp[:, 2, 0:S], tmp[:, 3, 0:S], tmp[:, 4, 0:S]
        rope_bufs = [bufs.take() for _ in range(3)]
        t = dve.do(lambda e: e.tensor_copy(pf, pos_i), [got_pos])
        bufs.give(row_free[1][0], [t])
        t = ts(dve, ang, pf, cst[:, C_MISC:C_MISC + 1], None, ALU.mult, None, [t, got_cst])
        t = ts(dve, turns, ang, 1.0 / (2 * np.pi), None, ALU.mult, None, [t])
        t = ts(dve, turns, turns, MAGIC, None, ALU.add, None, [t])
        t = ts(dve, turns, turns, -MAGIC, None, ALU.add, None, [t])
        for c in (C1, C2, C3):
            t = stt(ang, turns, -c, ang, ALU.mult, ALU.add, [t])
        t = ts(dve, ang, ang, LIMIT, -LIMIT, ALU.min, ALU.max, [t])
        sin_t = fn(rope_tab[:, 1, :], ang, ACT.Sin, [t])
        t = ts(dve, pf, ang, float(np.pi / 2), None, ALU.add, None, [t])
        t = ts(dve, turns, pf, float(np.pi), -2 * float(np.pi), ALU.is_gt, ALU.mult, [t])
        t = tt(dve, pf, pf, turns, ALU.add, [t])
        t = ts(dve, pf, pf, LIMIT, -LIMIT, ALU.min, ALU.max, [t])
        rope_ready = fn(rope_tab[:, 0, :], pf, ACT.Sin, [t, sin_t])
        for b, _ in rope_bufs:
            bufs.give(b, [rope_ready, t])

        def rms_scale(n):
            b, free = banks.take()
            for t in range(DT):
                buf, bfree = bufs.take()
                sq = fn(tmp[:, buf, 0:n], x[:, t, 0:n], ACT.Square, [x_ready[t], bfree])
                done = mm(psum[:, b, 0:n], mean, tmp[:, buf, 0:n], t == 0, t == DT - 1, [sq, free, got_cst], True)
                bufs.give(buf, [done])
            r = fn(rstd[:, 0:n], psum[:, b, 0:n], ACT.Sqrt, [done, rstd_free], bias=eps)
            banks.give(b, [r])
            return dve.do(lambda e: e.reciprocal(rstd[:, 0:n], rstd[:, 0:n]), [r])

        rstd_free = []

        def modulate(rows_of_sets, chunk, hi, lo):
            n = S * len(rows_of_sets)
            for row in rows_of_sets:
                need_mod(row, chunk)
                need_mod(row, chunk + 1)
            r = rms_scale(n)
            tickets = [None] * DT

            def tile(t):
                buf, bfree = bufs.take()
                gs, his, los = [], [], []
                for i, row in enumerate(rows_of_sets):
                    c = slice(i * S, (i + 1) * S)
                    gs.append(stt(tmp[:, buf, c], x[:, t, c], gain_col(row, chunk + 1, t), rstd[:, c], ALU.mult,
                                  ALU.mult, [r, x_ready[t], bfree, mod_ready[row, chunk + 1]]))
                rstd_free[:] = gs
                for i, row in enumerate(rows_of_sets):
                    c = slice(i * S, (i + 1) * S)
                    his.append(fn(hi[:, t, c], tmp[:, buf, c], ACT.Identity, [gs[i], mod_ready[row, chunk]],
                                  bias=column(row, chunk, t)))
                yield
                yield
                for i, row in enumerate(rows_of_sets):
                    c = slice(i * S, (i + 1) * S)
                    los.append(low(hi[:, t, c], lo[:, t, c], (tmp[:, buf, c], column(row, chunk, t), ALU.add),
                                   [his[i], mod_ready[row, chunk]]))
                bufs.give(buf, his + los)
                tickets[t] = his + los

            for t in range(DT):
                steps.start(tile(t))
                steps.tick()
            return hi, lo, tickets

        def add_to_x(o, m0, done, chunk, rows_of_sets, b, k_banks):
            seen = []
            for m in range(2):
                t = m0 + m
                parts = []
                for i, row in enumerate(rows_of_sets):
                    c = slice(i * S, (i + 1) * S)
                    parts.append(stt(x[:, t, c], o[:, m, c], column(row, chunk, t), x[:, t, c], ALU.mult, ALU.add,
                                     [done, x_ready[t], need_mod(row, chunk)]))
                x_ready[t] = parts
                seen += parts
            banks.give(b, seen, k_banks)

        def norm_rope(src, w, done, gain_ap, dest, rot, rope_w, after, src_done, ready, i):
            b1, f1 = bufs.take()
            sq = fn(tmp[:, b1, 0:w], src, ACT.Square, [done, f1])
            yield
            pb, pfree = banks.take()
            ms = mm(psum[:, pb, 0:w], headmean, tmp[:, b1, 0:w], True, True, [sq, pfree], True)
            b2, f2 = bufs.take()
            r = fn(tmp[:, b2, 0:w], psum[:, pb, 0:w], ACT.Sqrt, [ms, f2], bias=eps)
            banks.give(pb, [r])
            r = dve.do(lambda e: e.reciprocal(tmp[:, b2, 0:w], tmp[:, b2, 0:w]), [r])
            n = stt(tmp[:, b1, 0:w], src, gain_ap, tmp[:, b2, 0:w], ALU.mult, ALU.mult, [r, ms, par_ready])
            src_done(n)
            yield
            pb, pfree = banks.take()
            turned = mm(psum[:, pb, 0:rope_w], rot, tmp[:, b1, 0:rope_w], True, True, [n, pfree], True)
            tiles = rope_w // S
            wide = lambda ap: ap.rearrange("p (m n) -> p m n", n=S)
            tab = lambda i: spread(rope_tab[:, i, :], 1, [P, tiles, S])
            c = tt(pool, wide(tmp[:, b1, 0:rope_w]), wide(tmp[:, b1, 0:rope_w]), tab(0), ALU.mult,
                   [turned, rope_ready])
            yield
            s = tt(dve, wide(tmp[:, b2, 0:rope_w]), wide(psum[:, pb, 0:rope_w]), tab(1), ALU.mult,
                   [turned, rope_ready])
            banks.give(pb, [s])
            q = tt(pool, dest[:, 0:rope_w], tmp[:, b1, 0:rope_w], tmp[:, b2, 0:rope_w], ALU.add, [s, c, after])
            ends = [q]
            if rope_w < w:
                ends.append(dve.do(lambda e: e.tensor_copy(dest[:, rope_w:w], tmp[:, b1, rope_w:w]), [n, after]))
            bufs.give(b1, ends)
            bufs.give(b2, ends)
            ready[i] = ends

        def keys_twice(src, w, done, gain_ap, rot, rope_w, src_done, dests, after, ready, i):
            kbuf, kfree = bufs.take()
            k, got = tmp[:, kbuf, 0:w], [None]
            yield from norm_rope(src, w, done, gain_ap, k, rot, rope_w, kfree, src_done, got, 0)
            yield
            for j, dup in enumerate((C_DUP0, C_DUP1)):
                pb, pfree = banks.take()
                d = mm(psum[:, pb, 0:w], cst[:, dup:dup + P], k, True, True, [got[0], pfree], True)
                ready[i + j] = fn(dests[j], psum[:, pb, 0:w], ACT.Copy, [d, after])
                banks.give(pb, [ready[i + j]])
            bufs.give(kbuf, [ready[i], ready[i + 1]])

        def values_by_token(src, w, done, dest, after, src_done, ready, i):
            b1, f1 = bufs.take()
            c = fn(tmp[:, b1, 0:w], src, ACT.Copy, [done, f1])
            src_done(c)
            yield
            pb, pfree = banks.take()
            for k in range(w // P):
                d = tp(psum[:, pb, k * P:(k + 1) * P], tmp[:, b1, k * P:(k + 1) * P], ident, [c, pfree],
                       k == w // P - 1)
            bufs.give(b1, [d])
            ready[i] = fn(dest, psum[:, pb, 0:w].rearrange("p (i c) -> p i c", c=P), ACT.Copy, [d, after])
            banks.give(pb, [ready[i]])

        def handed_back(b, times):
            got = []

            def back(ticket):
                got.append(ticket)
                if len(got) == times:
                    banks.give(b, got)
            return back

        def attend(heads, nk, fill, pring, pbuf, pk, skew=2):
            kt, nb = nk // P, nk // S
            held = {}

            def score(h):
                d = heads[h]
                b, free = banks.take(nb)
                o = psum[:, b:b + nb, :].rearrange("p b c -> p (b c)").rearrange("p (q k) -> p q k", k=nk)
                for qt in range(2):
                    t = mm(o[:, qt], d["q"][:, qt * P:(qt + 1) * P], d["k"], True, True, [free, d["ready"]],
                           qt == 1)
                pb, pfree = pring.take(pk)
                p = pbuf[:, pb:pb + pk, :].rearrange("p b c -> p (b c)").rearrange("p (q k) -> p q k", k=nk)
                st = stats[:, h, :]
                if d["mask"] is not None:
                    src = p
                    t = stt(p, o, SCALE, d["mask"], ALU.mult, ALU.add, [t, pfree, got_phase])
                    banks.give(b, [t], nb)
                    t = reduce(st[:, 0:2], p, ALU.max, [t])
                    after, scale, neg = [], 1.0, -1.0
                else:
                    src, scale, neg = o, SCALE, -SCALE
                    t = reduce(st[:, 0:2], o, ALU.max, [t])
                if d["sink"] is not None:
                    t = ts(dve, st[:, 2:4], st[:, 0:2], d["sink"], neg, ALU.max, ALU.mult, [t, got_small])
                else:
                    t = ts(dve, st[:, 2:4], st[:, 0:2], neg, None, ALU.mult, None, [t])
                for qt in range(2):
                    e = fn(p[:, qt], src[:, qt], ACT.Exp, [t, pfree], bias=st[:, 2 + qt:3 + qt], scale=scale,
                           accum=st[:, 4 + qt:5 + qt])
                if d["mask"] is None:
                    banks.give(b, [e], nb)
                if d["sink"] is not None:
                    e2 = fn(st[:, 6:8], st[:, 2:4], ACT.Exp, [t], bias=d["sink"])
                    e = tt(dve, st[:, 4:6], st[:, 4:6], st[:, 6:8], ALU.add, [e, e2])
                r = dve.do(lambda e_: e_.reciprocal(st[:, 8:10], st[:, 4:6]), [e])
                for qt in range(2):
                    n = ts(pool, p[:, qt], p[:, qt], st[:, 8 + qt:9 + qt], None, ALU.mult, None, [r, e])
                held[h] = [p, pb, n]

            def turn(h):
                p, pb, n = held[h]
                b, free = banks.take(nb)
                o = psum[:, b:b + nb, :].rearrange("p b c -> p (b c)").rearrange("p (k q) -> p k q", q=S)
                for i in range(kt):
                    for qt in range(2):
                        t = tp(o[:, i, qt * P:(qt + 1) * P], p[:, qt, i * P:(i + 1) * P], ident, [free, n],
                               i == kt - 1 and qt == 1)
                pring.give(pb, [t], pk)
                tb, tfree = pring.take(pk)
                pt = pbuf[:, tb:tb + pk, :].rearrange("p b c -> p (b c)").rearrange("p (k q) -> p k q", q=S)
                c = fn(pt, o, ACT.Copy, [t, tfree])
                banks.give(b, [c], nb)
                held[h] = [pt, tb, c]

            def weigh(h):
                d = heads[h]
                pt, tb, c = held.pop(h)
                if h % 2 == 0:
                    held["o"] = banks.take()
                b, free = held["o"]
                base = HD * (h % 2)
                for i in range(kt):
                    t = mm(psum[base:base + HD, b, 0:S], d["v"](i), pt[:, i, :], i == 0, i == kt - 1,
                           [free, c, d["ready"]], i == kt - 1)
                pring.give(tb, [t], pk)
                if h % 2:
                    j = d["tile"]
                    hi = fn(u_hi1[:, j, :], psum[:, b, 0:S], ACT.Copy, [t, o_free])
                    lo = low(u_hi1[:, j, :], u_lo1[:, j, :], psum[:, b, 0:S], [hi, o_free])
                    banks.give(b, [hi, lo])
                    o_ready[j] = [hi, lo]

            o_ready = [None] * DT
            for i in range(len(heads) + skew + 1):
                if i < len(heads):
                    score(i)
                if 0 <= i - skew < len(heads):
                    turn(i - skew)
                if i > skew:
                    weigh(i - skew - 1)
                fill(i)
            return u_hi1, u_lo1, o_ready

        o_free = [x_ready[t] for t in range(DT)]
        small_gain = lambda row: par[:, 2, row:row + 1]

        last_readers = list(o_free)
        for l in range(2):
            while fed["plan"] < 8:
                feed()
            need_mod(l, 0)
            need_mod(l, 1)
            h = modulate([l], 0, h_hi1, h_lo1)
            rot1 = cst[:, C_ROT1:C_ROT1 + P]
            flat2 = lambda o: o.rearrange("p m n -> p (m n)")
            qk_ready = [None] * 14
            tab_q = lambda j: qk[:, j:j + 2, :].rearrange("p m n -> p (m n)")
            va = v_tok[:, 0:256].rearrange("p (i c) -> p i c", c=P)
            vb = v_tok[:, 256:1280].rearrange("p (i c) -> p i c", c=512)
            va_ready, vb_ready = [None], [None] * 4

            def queries(first, row):
                b, kb, o, done = product("in", h, S)
                steps.start(norm_rope(flat2(o), 512, done, small_gain(row), tab_q(first), rot1, 512,
                                      last_readers, handed_back(b, 1), qk_ready, first))

            for j in range(2):
                queries(2 * j, R_HEAD + l)
            b, kb, o, done = product("in", h, S)
            back = handed_back(b, 2)
            steps.start(keys_twice(o[:, 0], S, done, small_gain(R_HEAD + 2 + l), rot1, S, back,
                                   [qk[:, 4, :], qk[:, 5, :]], last_readers, qk_ready, 4))
            steps.start(values_by_token(o[:, 1], S, done, va, last_readers, back, va_ready, 0))
            for j in range(2):
                queries(6 + 2 * j, R_HEAD + 4 + l)
            for j in range(2):
                queries(10 + 2 * j, R_HEAD + 6 + l)
            for j in range(2):
                b, kb, o, done = product("in", h, S)
                back = handed_back(b, 2)
                for m in range(2):
                    f = (2 * j + m) * P
                    steps.start(values_by_token(o[:, m], S, done, vb[:, :, f:f + P], last_readers, back,
                                                vb_ready, 2 * j + m))
            steps.finish()
            for t in (0, 2, 6, 8, 10, 12):
                qk_ready[t + 1] = qk_ready[t] if t != 4 else qk_ready[t + 1]

            mask = lambda i: phase_tab[:, 512 * i:512 * (i + 1)].rearrange("p (q k) -> p q k", k=S)
            heads = []
            for i in range(8):
                rows_ = slice(HD * (i % 2), HD * (i % 2) + HD)
                kv = i // 4
                heads.append(dict(q=qk[rows_, i // 2, :], k=qk[rows_, 4 + kv, :], tile=i // 2, mask=mask(1),
                                  v=lambda kt, kv=kv: va[:, kt, kv * HD:(kv + 1) * HD],
                                  sink=sink[:, 8 * l + i:8 * l + i + 1],
                                  ready=[qk_ready[i // 2], qk_ready[4 + kv], va_ready]))
            for i in range(8):
                rows_ = slice(HD * (i % 2), HD * (i % 2) + HD)
                heads.append(dict(q=qk[rows_, 6 + i // 2, :], k=qk[rows_, 10 + i // 2, :], tile=4 + i // 2,
                                  v=lambda kt, i=i: vb[:, kt, i * HD:(i + 1) * HD], mask=mask(0), sink=None,
                                  ready=[qk_ready[6 + i // 2], qk_ready[10 + i // 2], vb_ready]))
            gate_ready = []

            def fill(i):
                if i % 2 == 0 and len(gate_ready) < 8:
                    b, kb, o, done = product("in", h, S)
                    j = len(gate_ready)
                    t = fn(gate_tanh[:, 2 * j:2 * j + 2, :], o, ACT.Tanh, [done, h_free], scale=0.5)
                    banks.give(b, [t])
                    gate_ready.append(t)

            h_free = last_readers
            att = attend(heads, S, fill, bufs, tmp, 1)
            assert len(gate_ready) == 8
            mixed_ready = [None] * DT
            for j in range(4):
                s, ready = unit("o")
                outs = []
                for part in range(2):
                    b, free = banks.take()
                    o = psum[:, b, :].rearrange("p (m n) -> p m n", n=S)
                    for m in range(2):
                        for i in range(4):
                            k = 4 * part + i
                            wh, wl = w_hi[:, s, k, m * P:(m + 1) * P], w_lo[:, s, k, m * P:(m + 1) * P]
                            xh, xl = att[0][:, k, :], att[1][:, k, :]
                            mm(o[:, m], wh, xh, i == 0, False, [ready[0], free, att[2][k]])
                            mm(o[:, m], wh, xl, False, False)
                            done = mm(o[:, m], wl, xh, False, i == 3, [ready[1]], m == 1 and i == 3)
                    outs.append((b, o, done))
                split_free[s] = [done]
                bb, bfree = bufs.take(2)
                ya = tmp[:, bb, :].rearrange("p (m n) -> p m n", n=S)
                yb = tmp[:, bb + 1, :].rearrange("p (m n) -> p m n", n=S)
                t = []
                for part, y in enumerate((ya, yb)):
                    b, o, done = outs[part]
                    g = gate_tanh[:, 8 * part + 2 * j:8 * part + 2 * j + 2, :]
                    t.append(stt(y, g, 1.0, o, ALU.add, ALU.mult, [done, gate_ready[4 * part + j], bfree]))
                    banks.give(b, [t[-1]])
                t = tt(pool, ya, ya, yb, ALU.add, [t])
                c = slice(2 * j, 2 * j + 2)
                hi = fn(h_hi1[:, c, :], ya, ACT.Copy, [t], scale=0.5)
                lo = low(h_hi1[:, c, :], h_lo1[:, c, :], (ya, 0.5, ALU.mult), [hi])
                bufs.give(bb, [hi, lo], 2)
                mixed_ready[2 * j] = mixed_ready[2 * j + 1] = [hi, lo]
            for j in range(4):
                b, kb, o, done = product("out", (h_hi1, h_lo1, mixed_ready), S)
                add_to_x(o, 2 * j, done, 2, [l], b, kb)

            h = modulate([l], 3, h_hi1, h_lo1)

            def squared_relu(b, o, done, j, u_ready):
                buf, bfree = bufs.take()
                r = tmp[:, buf, :].rearrange("p (m n) -> p m n", n=S)
                t = fn(r, o, ACT.Relu, [done, bfree])
                yield
                t = stt(r, o, 0.0, r, ALU.max, ALU.mult, [t])
                banks.give(b, [t])
                c = slice(2 * j, 2 * j + 2)
                hi = fn(u_hi1[:, c, :], r, ACT.Copy, [t, done])
                yield
                lo = low(u_hi1[:, c, :], u_lo1[:, c, :], r, [hi])
                bufs.give(buf, [hi, lo])
                u_ready[2 * j] = u_ready[2 * j + 1] = [hi, lo]

            for g in range(4):
                u_ready = [None] * DT
                for j in range(4):
                    b, kb, o, done = product("up", h, S)
                    steps.start(squared_relu(b, o, done, j, u_ready))
                for j in range(4):
                    b, kb, o, done = product("down", (u_hi1, u_lo1, u_ready), S)
                    add_to_x(o, 2 * j, done, 5, [l], b, kb)
            last_readers = [done]
            o_free = [done]

        pool_tab = act.load(phase_tab[:], a["consts"][:, C_POOL:C_POOL + 1024], mark("d_phase"), [done])
        rope_load = act.load(rope_tab[:].rearrange("p a c -> p (a c)"), a["consts"][:, C_COS2:C_COS2 + 512],
                             mark("d_rope"), [done])

        def route(layer, n, h, gates):
            T = n // P
            b, free = banks.take()
            lg_p = psum[:, b, 0:T * 20].rearrange("p (i c) -> p i c", c=20)
            for i in range(T):
                for k in range(DT):
                    for part in range(2):
                        t = mm(lg_p[:, i], plain(h[part][:, k, i * P:(i + 1) * P]), w_route[:, layer, k, :],
                               k == 0 and part == 0, k == DT - 1 and part == 1, [free, h[2][k], got_small],
                               i == T - 1 and k == DT - 1)
            yield
            buf, bfree = bufs.take()
            area = [0]

            def room(*shape):
                size = int(np.prod(shape))
                ap = tmp[:, buf, area[0]:area[0] + size]
                area[0] += size
                assert area[0] <= 512
                if len(shape) == 2:
                    return ap.rearrange("p (i c) -> p i c", c=shape[1])
                return ap

            N4, N16 = [P, T, 4], [P, T, N_EXP]
            lg = room(T, 20)
            t = tt(dve, lg, lg_p, spread(b_route[:, layer, :], 1, [P, T, 20]), ALU.add, [t, got_small, bfree])
            banks.give(b, [t])
            gl, el = lg[:, :, 0:4], lg[:, :, 4:20]
            iota4 = spread(cst[:, C_IOTA:C_IOTA + 4], 1, N4)
            iota16 = spread(cst[:, C_IOTA:C_IOTA + N_EXP], 1, N16)

            def first_of_max(v, wide, iota, t):
                m, d, at_, one, least = room(T), room(T, wide), room(T, wide), room(T, wide), room(T)
                shape = [P, T, wide]
                t = reduce(m, v, ALU.max, [t])
                td = tt(dve, d, v, spread(m, 2, shape), ALU.subtract, [t])
                t = ts(dve, one, d, 0.0, -64.0, ALU.is_ge, ALU.mult, [td])
                t = tt(dve, at_, one, iota, ALU.add, [t])
                t = reduce(least, at_, ALU.min, [t])
                t = tt(dve, one, at_, spread(least, 2, shape), ALU.is_equal, [t])
                return m, d, one, t, td

            yield
            _, d, group, t, td = first_of_max(gl, 4, iota4, t)
            eg, sg, gw = room(T, 4), room(T), room(T)
            e = fn(eg, d, ACT.Exp, [td])
            e = reduce(sg, eg, ALU.add, [e])
            gw_t = dve.do(lambda e_: e_.reciprocal(gw, sg), [e])
            yield
            pen = room(T, 4)
            t = ts(dve, pen, group, -1.0, 1e30, ALU.add, ALU.mult, [t])
            by_group = lambda ap: ap.rearrange("p i (g c) -> p i g c", c=4)
            inside = room(T, N_EXP)
            for i in range(T):
                ti = tt(dve, inside[:, i].rearrange("p (g c) -> p g c", c=4),
                        el[:, i].rearrange("p (g c) -> p g c", c=4), spread(pen[:, i], 2, [P, 4, 4]), ALU.add, [t])
            t = ti
            yield
            m1, _, one1, t, _ = first_of_max(inside, N_EXP, iota16, t)
            t = stt(inside, one1, -2e30, inside, ALU.mult, ALU.add, [t])
            area2, fr2 = bufs.take()
            first_buf = buf
            buf, area[0] = area2, 0
            t2 = [t, fr2]
            yield
            m2, _, one2, t, _ = first_of_max(inside, N_EXP, iota16, t2)
            yield
            dm, ex, den = room(T), room(T), room(T)
            td = tt(dve, dm, m2, m1, ALU.subtract, [t])
            e = fn(ex, dm, ACT.Exp, [td])
            td = ts(dve, den, ex, 1.0, None, ALU.add, None, [e])
            td = dve.do(lambda e_: e_.reciprocal(den, den), [td])
            td = tt(dve, den, den, gw, ALU.mult, [td, gw_t])
            t1 = tt(dve, one1, one1, spread(den, 2, N16), ALU.mult, [td, t])
            td = tt(dve, den, den, ex, ALU.mult, [td, t1])
            t2 = tt(dve, one2, one2, spread(den, 2, N16), ALU.mult, [td, t])
            t = tt(dve, one1, one1, one2, ALU.add, [t1, t2])
            yield
            b, free = banks.take()
            for i in range(T):
                d_ = tp(psum[0:N_EXP, b, i * P:(i + 1) * P], one1[:, i, :], ident, [t, free], i == T - 1)
            bufs.give(first_buf, [d_])
            bufs.give(area2, [d_])
            g = fn(gates_t[:, 0:n], psum[0:N_EXP, b, 0:n], ACT.Copy, [d_, done_all], scale=0.5)
            banks.give(b, [g])
            gates[0] = g

        def moe(layer, rows_of_sets):
            sets = len(rows_of_sets)
            n = S * sets
            h_bufs = (h_hi1, h_lo1) if sets == 1 else (h_hi2, h_lo2)
            u_bufs = (u_hi1, u_lo1) if sets == 1 else (u_hi2, u_lo2)
            h = modulate(rows_of_sets, 3, *h_bufs)
            gates = [None]

            def gated(expert, i, ba, oa, da, bb, ob, db, u_ready):
                buf, bfree = bufs.take(sets)
                u = tmp[:, buf:buf + sets, :].rearrange("p b c -> p (b c)").rearrange("p (m n) -> p m n", n=n)
                t = fn(u, oa, ACT.Tanh, [da, bfree], scale=0.5)
                t = stt(u, u, 1.0, oa, ALU.add, ALU.mult, [t])
                banks.give(ba, [t], sets)
                t = tt(dve, u, u, ob, ALU.mult, [t, db])
                banks.give(bb, [t], sets)
                steps.need(gates, 0)
                pb, pfree = banks.take()
                row = cst[0:N_EXP, C_IDENT + expert:C_IDENT + expert + 1].to_broadcast([N_EXP, P])
                gd = mm(psum[:, pb, 0:n], row, gates_t[:, 0:n], True, True, [gates, pfree], True)
                t = tt(dve, u, u, spread(psum[:, pb, 0:n], 1, [P, 2, n]), ALU.mult, [t, gd])
                banks.give(pb, [t])
                c = slice(2 * i, 2 * i + 2)
                hi = fn(u_bufs[0][:, c, :], u, ACT.Copy, [t])
                yield
                lo = low(u_bufs[0][:, c, :], u_bufs[1][:, c, :], u, [hi])
                bufs.give(buf, [hi, lo], sets)
                u_ready[2 * i] = u_ready[2 * i + 1] = [hi, lo]

            for g in range(4):
                u_ready = [None] * DT
                for i in range(4):
                    expert = 4 * g + i
                    ba, kb, oa, da = product("eg", h, n)
                    if expert == 0:
                        steps.start(route(layer, n, h, gates))
                    bb, _, ob, db = product("eu", h, n)
                    steps.start(gated(expert, i, ba, oa, da, bb, ob, db, u_ready))
                for j in range(4):
                    b, kb, o, done = product("ed", (*u_bufs, u_ready), n)
                    add_to_x(o, 2 * j, done, 5, rows_of_sets, b, kb)
            return done

        done_all = []
        sets = [2, 4]
        for row in sets:
            need_mod(row, 0)
            need_mod(row, 1)
        r = rms_scale(S2)
        PAD = 8
        fw = S + 2 * PAD
        two = lambda ap: ap.rearrange("p (s c) -> p s c", s=2)
        taken = [bufs.take() for _ in range(8)]
        tmp_flat = tmp[:].rearrange("p b c -> p (b c)")
        spare = [two(pool_in[:, 8 + i, :]) for i in range(7)] + [two(tmp_flat[:, 544 * i:544 * (i + 1)])
                                                                 for i in range(7)]
        tmp_free = [f for _, f in taken]
        hp = [two(pool_in[:, t, :]) for t in range(DT)]
        sums, lane = [], [dve if t % 2 == 0 else pool for t in range(DT)]
        for t in range(DT):
            sums.append([spare.pop(), spare.pop() if t > 1 else None])
        z = pool.do(lambda e: e.memset(pool_in[:, 0:8, :], 0.0), [last_readers])
        cur = [None] * DT
        for t in range(DT):
            hs = []
            for i, row in enumerate(sets):
                c = slice(i * S, (i + 1) * S)
                v = hp[t][:, i, PAD:PAD + S]
                q = stt(v, x[:, t, c], gain_col(row, 1, t), rstd[:, c], ALU.mult, ALU.mult,
                        [r, x_ready[t], z, mod_ready[row, 1]])
                hs.append(fn(v, v, ACT.Identity, [q, mod_ready[row, 0]], bias=column(row, 0, t)))
            cur[t] = hs
        rstd_free[:] = [q]
        for t in range(DT):
            cur[t] = tt(lane[t], sums[t][0][:, :, 1:fw], hp[t][:, :, 0:fw - 1], hp[t][:, :, 1:fw], ALU.add,
                        [cur[t], tmp_free, last_readers])
        for step in range(3):
            half = 1 << step
            a0, a1 = 2 * half, fw - 2 * half + 1
            for t in range(2 * step + 2, DT):
                src, dst = sums[t]
                cur[t] = tt(lane[t], dst[:, :, a0:a1], src[:, :, a0 - half:a1 - half],
                            src[:, :, a0 + half:a1 + half], ALU.add, [cur[t]])
                sums[t] = [dst, src]
        inner = slice(PAD, PAD + S)
        for t in range(DT):
            rc = spread(phase_tab[:, (t // 2) * S:(t // 2 + 1) * S], 1, [P, 2, S])
            v = sums[t][0][:, :, inner]
            cur[t] = tt(lane[t], v, v, rc, ALU.mult, [cur[t], pool_tab])
        for t in range(DT):
            v = sums[t][0][:, :, inner]
            cur[t] = tt(lane[t], v, v, hp[t][:, :, inner], ALU.subtract, [cur[t]])
        pool_ready = []
        for t in range(DT):
            pool_ready.append([fn(two(h_hi2[:, t, :]), sums[t][0][:, :, inner], ACT.Copy, [cur[t], last_readers])])
        for t in range(DT):
            pool_ready[t].append(low(two(h_hi2[:, t, :]), two(h_lo2[:, t, :]), sums[t][0][:, :, inner],
                                     [pool_ready[t][0]]))
        for b, _ in taken:
            bufs.give(b, [pool_ready[t][n_] for t in range(DT) for n_ in range(2)])
        s, ready = unit("pool")
        need_mod(2, 2)
        need_mod(4, 2)
        for i, row in enumerate(sets):
            t1 = tt(dve, cond_t[:, i, :], mod[:, row, 2 * DT:3 * DT], par[:, 2, 8:16], ALU.mult,
                    [mod_ready[row, 2], cond_ready])
        scale_ready = [t1]
        for g in range(4):
            b, free = banks.take(2)
            o = psum[:, b:b + 2, :]
            for m in range(2):
                for i in range(2):
                    k = 2 * g + i
                    wh, wl = w_hi[:, s, k, m * P:(m + 1) * P], w_lo[:, s, k, m * P:(m + 1) * P]
                    xh, xl = h_hi2[:, k, :], h_lo2[:, k, :]
                    mm(o[:, m], wh, xh, i == 0, False, [ready[0], free, pool_ready[k]])
                    mm(o[:, m], wh, xl, False, False)
                    done = mm(o[:, m], wl, xh, False, i == 1, [ready[1]], m == 1 and i == 1)
            seen = []
            for m in range(2):
                t = 2 * g + m
                buf, bfree = bufs.take()
                u = tmp[:, buf, :]
                parts = []
                bias = par[:, 2, t:t + 1]
                for i in range(2):
                    c = slice(i * S, (i + 1) * S)
                    q = ts(dve, u[:, c], o[:, m, c], bias, cond_t[:, i, t:t + 1], ALU.add, ALU.mult,
                           [done, bfree, scale_ready])
                    seen.append(q)
                    parts.append(tt(dve, x[:, t, c], u[:, c], x[:, t, c], ALU.add, [q, x_ready[t]]))
                x_ready[t] = parts
                bufs.give(buf, parts)
            banks.give(b, seen, 2)
        split_free[s] = [done]
        done_all = [moe(0, sets)]

        h = modulate([3, 5], 0, h_hi2, h_lo2)
        rope_ready = rope_load
        rot2 = cst[:, C_ROT2:C_ROT2 + P]
        q_ready = [None] * 8
        back = None
        for j in range(4):
            b, kb, o, done = product("qkv", h, S)
            steps.start(norm_rope(o.rearrange("p m n -> p (m n)"), 512, done, small_gain(R_HEAD + 8),
                                  q_att[:, 2 * j:2 * j + 2, :].rearrange("p m n -> p (m n)"), rot2, 512, [done],
                                  handed_back(b, 1), q_ready, 2 * j))
        b, kb, o, done = product("qkv", h, S2)
        k_ready = [None] * 4
        for m in range(2):
            steps.start(keys_twice(o[:, m], S2, done, small_gain(R_HEAD + 9), rot2, S, handed_back(b + m, 1),
                                   [k_att[:, 2 * m, :], k_att[:, 2 * m + 1, :]], [done], k_ready, 2 * m))
        vv = v_tok[:, 0:1024].rearrange("p (i c) -> p i c", c=256)
        b, kb, o, done = product("qkv", h, S2)
        v_ready = [None] * 2
        for m in range(2):
            steps.start(values_by_token(o[:, m], S2, done, vv[:, :, m * P:(m + 1) * P], [], handed_back(b + m, 1),
                                        v_ready, m))
        steps.finish()
        for t in range(0, 8, 2):
            q_ready[t + 1] = q_ready[t]
        heads = []
        for i in range(16):
            rows_ = slice(HD * (i % 2), HD * (i % 2) + HD)
            kv = i // 4
            heads.append(dict(q=q_att[rows_, i // 2, :], k=k_att[rows_, kv, :], tile=i // 2, mask=None, sink=None,
                              v=lambda kt, kv=kv: vv[:, kt, kv * HD:(kv + 1) * HD],
                              ready=[q_ready[i // 2], k_ready[kv], v_ready]))
        o_free = [done]
        rooms = Ring(8, steps.tick)
        rooms.free = [[done] for _ in range(8)]
        att = attend(heads, S2, lambda i: None, rooms, att_room, 1)
        for j in range(4):
            b, kb, o, done = product("wo", att, S)
            add_to_x(o, 2 * j, done, 2, [3], b, kb)
        moe(1, [3])
        assert fed["plan"] == len(plan) and fed["used"] == len(gemms)

        outs = []
        for i in range(2):
            buf, bfree = bufs.take(2)
            o_tok = tmp[:, buf:buf + 2, :].rearrange("p b c -> p (b c)")
            cs = []
            for half in range(2):
                b, free = banks.take()
                for t in range(4):
                    k = 4 * half + t
                    d = tp(psum[:, b, t * P:(t + 1) * P], x[:, k, i * P:(i + 1) * P], ident, [x_ready[k], free], t == 3)
                cs.append(fn(o_tok[:, 512 * half:512 * (half + 1)], psum[:, b, :], ACT.Copy, [d, bfree]))
                banks.give(b, [cs[-1]])
            outs.append(sp.load(out[0, i * P:(i + 1) * P, :], o_tok, mark(f"d_out{i}"), cs))
            bufs.give(buf, [outs[-1]], 2)
        sp.wait(*outs)

        block = ctx.enter_context(nc.Block())

        def run(lane):
            def body(engine):
                for step in lane.steps:
                    step(engine)
            return body

        block.sync(run(sp))
        block.tensor(run(pe))
        block.scalar(run(act))
        block.vector(run(dve))
        block.gpsimd(run(pool))


INPUTS = ["x", "c", "positions", "rms_mix", "rms_mlp", "w_ada", "b_ada", "w_in", "q_norm_swa", "k_norm_swa",
          "q_norm_moba", "k_norm_moba", "swa_sinks", "w_o_swa", "w_o_moba", "w_out", "w_up", "w_down", "c_2",
          "ctx_2", "c_ctx_2", "w_mod_2", "b_mod_2", "norm1_g_2", "norm2_g_2", "pool_w_2", "pool_b_2",
          "pool_ls_2", "attn_wqkv_2", "attn_qg_2", "attn_kg_2", "attn_wo_2", "moe_wrg_2", "moe_brg_2",
          "moe_wre_2", "moe_bre_2", "moe_wg_2", "moe_wu_2", "moe_wd_2"]


def kernel(**inputs):
    import concourse.bacc as bacc
    from concourse.bass_utils import run_bass_kernel_spmd

    nc = bacc.Bacc("TRN2", target_bir_lowering=False, num_devices=1, dynamic_dma_scratch_size=8192)
    arrays = {f"in_{name}": np.ascontiguousarray(inputs[name]) for name in INPUTS}
    arrays["in_consts"] = constants()
    aps = {}
    for name, arr in arrays.items():
        aps[name[3:]] = nc.dram_tensor(name, arr.shape, mybir.dt.from_np(arr.dtype), kind="ExternalInput").ap()
    out = nc.dram_tensor("out", (1, S, D), F32, kind="ExternalOutput").ap()
    build(nc, aps, out)
    result = run_bass_kernel_spmd(nc, [arrays], core_ids=[0])
    return result.results[0]["out"]
```

```python
from contextlib import ExitStack

import numpy as np
import concourse.bass as bass
from concourse import mybir

F32 = mybir.dt.float32
F32R = mybir.dt.float32r
I32 = mybir.dt.int32
ALU = mybir.AluOpType
ACT = mybir.ActivationFunctionType
AX = mybir.AxisListType

P = 128
D = 1024
DT = D // P
S = 256
S2 = 512
HD = 64
UC = 256
UNIT = DT * UC
RAW_SLOTS = 4
SPLIT_SLOTS = 3
LAG = 1
ACCS = 3
NEG = -1e30
EPS = 1e-6
SCALE = HD ** -0.5
N_EXP = 16
WINDOW = 128
GRID_W = 64
THETA = 10000.0

C_IDENT, C_ROT1, C_ROT2, C_DUP0, C_DUP1, C_HEADMEAN, C_MEAN = (P * i for i in range(7))
C_MISC = 7 * P
C_IOTA = C_MISC + 3
C_FIXED = C_IOTA + N_EXP
MASK_W = P + S
C_CAUSAL = C_FIXED
C_SWA = C_CAUSAL + MASK_W
C_COS2 = C_SWA + MASK_W
C_SIN2 = C_COS2 + S
C_POOL = C_SIN2 + S
C_END = C_POOL + 4 * 2 * S


def constants():
    c = np.zeros((P, C_END), np.float32)
    i = np.arange(P)
    c[i, C_IDENT + i] = 1
    half = HD // 2
    for m in range(P):
        first = m % HD < half
        c[m + half if first else m - half, C_ROT1 + m] = -1 if first else 1
    quarter = HD // 4
    for m in range(P):
        first = m % half < quarter
        c[m + quarter if first else m - quarter, C_ROT2 + m] = -1 if first else 1
    c[i % HD, C_DUP0 + i] = 1
    c[HD + i % HD, C_DUP1 + i] = 1
    c[:, C_HEADMEAN:C_HEADMEAN + P] = (i[:, None] // HD == i[None, :] // HD) / HD
    c[:, C_MEAN:C_MEAN + P] = 1.0 / D
    inv = THETA ** (-np.arange(half) / half)
    c[:, C_MISC] = inv[i % half]
    c[:, C_MISC + 1] = EPS
    c[:, C_MISC + 2] = EPS / SCALE ** 2
    c[:, C_IOTA:C_IOTA + N_EXP] = np.arange(N_EXP)
    q = np.where(np.arange(MASK_W) < P, 0, P)[None, :] + i[:, None]
    k = np.where(np.arange(MASK_W) < P, np.arange(MASK_W), np.arange(MASK_W) - P)[None, :]
    c[:, C_CAUSAL:C_CAUSAL + MASK_W] = np.where(k <= q, 0, NEG)
    c[:, C_SWA:C_SWA + MASK_W] = np.where((k <= q) & (q - k < WINDOW), 0, NEG)
    inv2 = (np.float32(THETA) ** (-np.arange(0, half, 2, dtype=np.float32) / half)).astype(np.float32)
    tok = np.arange(S)
    pos = np.where((i[:, None] % HD) < half, tok // GRID_W, tok % GRID_W).astype(np.float32)
    ang = (pos * inv2[i % quarter][:, None]).astype(np.float32).astype(np.float64)
    c[:, C_COS2:C_COS2 + S] = np.cos(ang)
    c[:, C_SIN2:C_SIN2 + S] = np.sin(ang)
    for g in range(4):
        half_w = 1 << g
        first, past = np.clip(tok - half_w, 0, S), np.clip(tok + half_w, 0, S)
        for tile in range(2):
            source = tile * P + i[:, None]
            at = C_POOL + (2 * g + tile) * S
            c[:, at:at + S] = np.where((source >= first) & (source < past), 1.0 / (past - first), 0) - (source == tok)
    return c


def flat(tickets):
    for t in tickets:
        if t is None:
            continue
        if isinstance(t, list):
            yield from flat(t)
        else:
            yield t


class Lane:

    def __init__(self, sem):
        self.sem, self.count, self.steps, self.seen = sem, 0, [], {}

    def wait(self, *tickets):
        for sem, value in flat(tickets):
            if self.seen.get(id(sem), 0) < value:
                self.seen[id(sem)] = value
                self.steps.append(lambda e, sem=sem, value=value: e.wait_ge(sem, value))

    def do(self, issue, after=(), signal=True):
        self.wait(*after)
        if not signal:
            self.steps.append(issue)
            return None
        self.count += 1
        self.steps.append(lambda e: issue(e).then_inc(self.sem, 1))
        return self.sem, self.count

    def load(self, dst, src, mark, after=()):
        self.wait(*after)
        mark[1] += 16
        self.steps.append(lambda e: e.dma_start(dst, src).then_inc(mark[0], 16))
        return mark[0], mark[1]


class Steps:

    def __init__(self):
        self.live, self.busy, self.products, self.hurry = [], [], 0, False

    def start(self, gen):
        self.live.append(gen)
        self.advance(gen)

    def advance(self, gen):
        self.busy.append(gen)
        ended = next(gen, "end") == "end"
        self.busy.remove(gen)
        if ended:
            self.live.remove(gen)

    def tick(self):
        ready = [gen for gen in self.live if gen not in self.busy]
        assert ready, "nothing left to queue"
        for gen in ready:
            if gen in self.live and gen not in self.busy:
                self.advance(gen)

    def need(self, tickets, i):
        while tickets[i] is None:
            self.tick()
        return tickets[i]

    def finish(self):
        while self.live:
            self.tick()


class Ring:

    def __init__(self, n, tick):
        self.n, self.free, self.tick = n, [[] for _ in range(n)], tick
        self.given, self.count = list(range(n)), n

    def take(self, k=1):
        while True:
            runs = [range(first, first + k) for first in range(0, self.n - k + 1, k)]
            runs = [run for run in runs if all(self.free[i] is not None for i in run)]
            if runs:
                run = min(runs, key=lambda run: max(self.given[i] for i in run))
                tickets = [t for i in run for t in self.free[i]]
                for i in run:
                    self.free[i] = None
                return run[0], tickets
            self.tick()

    def give(self, first, tickets, k=1):
        self.count += 1
        for i in range(first, first + k):
            self.free[i], self.given[i] = list(tickets), self.count


def build(nc, a, out):
    with ExitStack() as ctx:
        at = [-(-nc.sbuf_base // 64) * 64]

        def sb(name, shape, dt=F32, offset=None):
            size = 4 * int(np.prod(shape[1:]))
            if offset is None:
                offset = at[0]
                at[0] += -(-size // 64) * 64
                assert at[0] <= nc.sbuf_usable_end, (name, at[0], nc.sbuf_usable_end)
            return nc.alloc_sbuf_tensor_at(name, shape, dt, offset=offset), offset

        raw, _ = sb("raw", [P, RAW_SLOTS, UNIT])
        w_hi, _ = sb("w_hi", [P, SPLIT_SLOTS, DT, UC], F32R)
        w_lo, _ = sb("w_lo", [P, SPLIT_SLOTS, DT, UC], F32R)
        x, _ = sb("x", [P, DT, S2])
        h_hi2, big1 = sb("h_hi2", [P, DT, S2], F32R)
        h_lo2, _ = sb("h_lo2", [P, DT, S2], F32R)
        h_hi1, _ = sb("h_hi1", [P, DT, S], F32R, offset=big1)
        h_lo1, _ = sb("h_lo1", [P, DT, S], F32R, offset=big1 + 8192)
        att_room, _ = sb("att_room", [P, 8, D], F32, offset=big1)
        gate_tanh, _ = sb("gate_tanh", [P, 16, S], F32, offset=big1 + 16384)
        u_hi2, big2 = sb("u_hi2", [P, DT, S2], F32R)
        u_lo2, _ = sb("u_lo2", [P, DT, S2], F32R)
        u_hi1, _ = sb("u_hi1", [P, DT, S], F32R, offset=big2)
        u_lo1, _ = sb("u_lo1", [P, DT, S], F32R, offset=big2 + 8192)
        u_hiB, _ = sb("u_hiB", [P, DT, S], F32R, offset=big2 + 16384)
        u_loB, _ = sb("u_loB", [P, DT, S], F32R, offset=big2 + 24576)
        qk, _ = sb("qk", [P, 16, S], F32, offset=big2 + 16384)
        q_att, _ = sb("q_att", [P, 8, S], F32, offset=big2 + 16384)
        k_att, _ = sb("k_att", [P, 4, S2], F32, offset=big2 + 24576)
        by_token, _ = sb("by_token", [P, 4, D], F32, offset=big2)
        window_tab, _ = sb("window_tab", [P, 4, 2, S], F32, offset=big2 + 16384)
        tokens_in, _ = sb("tokens_in", [P, 4, D], F32, offset=big2)
        v_tok, _ = sb("v_tok", [P, 1280])
        acc, _ = sb("acc", [P, ACCS, D])
        tmp, _ = sb("tmp", [P, 8, 512])
        rstd_col, _ = sb("rstd_col", [P, 4])
        cst, _ = sb("cst", [P, C_FIXED])
        masks, _ = sb("masks", [P, 2, MASK_W])
        rope_tab, _ = sb("rope_tab", [P, 2, S])
        par, _ = sb("par", [P, 4, P])
        mod, _ = sb("mod", [P, 6, 48])
        gain, _ = sb("gain", [P, 12, DT])
        cond, _ = sb("cond", [P, 3, DT])
        cond_t, _ = sb("cond_t", [P, 3, DT])
        sink, _ = sb("sink", [P, 16])
        stats, _ = sb("stats", [P, 16, 12])
        head_rstd, _ = sb("head_rstd", [P, 14, 8])
        w_route_hi, _ = sb("w_route_hi", [P, 2, DT * 20], F32R)
        w_route_lo, _ = sb("w_route_lo", [P, 2, DT * 20], F32R)
        b_route, _ = sb("b_route", [P, 2, 20])
        pick, _ = sb("pick", [N_EXP, N_EXP], F32R)
        gates_hi, _ = sb("gates_hi", [16, S2], F32R)
        gates_lo, _ = sb("gates_lo", [16, S2], F32R)
        psum = ctx.enter_context(nc.psum_tensor("psum", [P, 8, 512], F32))

        def sem(name):
            return ctx.enter_context(nc.semaphore(name))

        pe, act, dve, pool, sp = (Lane(sem(n)) for n in ("s_pe", "s_act", "s_dve", "s_pool", "s_sp"))
        steps = Steps()
        banks, bufs = Ring(8, steps.tick), Ring(8, steps.tick)
        marks = {}

        def mark(name):
            if name not in marks:
                marks[name] = [sem(name), 0]
            return marks[name]

        def mm(o, lhs, rhs, start, stop, after=(), signal=False):
            return pe.do(lambda e: e.matmul(o, lhs, rhs, start=start, stop=stop, skip_group_check=True),
                         after, signal)

        def tp(o, i, ident, after=(), signal=False):
            return pe.do(lambda e: e.transpose(o, i, ident), after, signal)

        def fn(o, i, func, after=(), bias=None, scale=1.0, accum=None):
            kw = {"scale": scale}
            if bias is not None:
                kw["bias"] = bias
            if accum is not None:
                kw["accum_out"] = accum
            return act.do(lambda e: e.activation(o, i, func, **kw), after)

        def tt(lane, o, i0, i1, op, after=()):
            return lane.do(lambda e: e.tensor_tensor(o, i0, i1, op), after)

        def ts(lane, o, i, s1, s2, op0, op1, after=()):
            if s2 is None:
                return lane.do(lambda e: e.tensor_scalar(o, i, s1, None, op0), after)
            return lane.do(lambda e: e.tensor_scalar(o, i, s1, s2, op0, op1), after)

        def stt(o, i0, s, i1, op0, op1, after=()):
            return dve.do(lambda e: e.scalar_tensor_tensor(out=o, in0=i0, scalar=s, in1=i1, op0=op0, op1=op1),
                          after)

        def reduce(o, i, op, after=()):
            return dve.do(lambda e: e.tensor_reduce(o, i, AX.X, op), after)

        def spread(ap, axis, shape):
            return ap.unsqueeze(axis).to_broadcast(shape)

        def plain(ap):
            return ap.bitcast(F32)

        def low(hi, lo, value_op, after):
            if isinstance(value_op, tuple):
                i0, s, op = value_op
                return stt(lo, i0, s, plain(hi), op, ALU.subtract, after)
            return tt(dve, lo, value_op, plain(hi), ALU.subtract, after)

        ident = cst[:, C_IDENT:C_IDENT + P]
        mean = cst[:, C_MEAN:C_MEAN + P]
        headmean = cst[:, C_HEADMEAN:C_HEADMEAN + P]
        eps = cst[:, C_MISC + 1:C_MISC + 2]
        eps_scaled = cst[:, C_MISC + 2:C_MISC + 3]

        rows = tmp[:, 0, :].rearrange("p (r c) -> p r c", r=4)
        row_buf = bufs.take()[0]
        got_rows = [None] * 4

        def param_rows(lane, dst_row, block, arr, n):
            got_rows[block] = lane.load(rows[dst_row:dst_row + n, block, :], arr.rearrange("(r c) -> r c", c=P),
                                        mark(f"d_par{block}"))

        def tokens(lane, i, after=()):
            src = a["x"][0] if i < 2 else a["ctx_2"][0]
            got_tok.append(lane.load(tokens_in[:, i, :], src[(i % 2) * P:(i % 2 + 1) * P, :], mark(f"d_tok{i}"),
                                     after))

        param_rows(sp, 0, 2, a["c"][0], 8)
        param_rows(sp, 8, 2, a["c_2"][0], 8)
        param_rows(sp, 16, 2, a["c_ctx_2"], 8)
        got_tok = []
        got_ident = act.load(cst[:, 0:P], a["consts"][:, 0:P], mark("d_ident"))
        tokens(act, 0)
        tokens(act, 1)
        got_cst = pool.load(cst[:, P:C_FIXED], a["consts"][:, P:C_FIXED], mark("d_cst"))
        pos_buf = bufs.take()[0]
        pos_i = tmp[:, pos_buf, 0:S].bitcast(I32)

        def modulation_rows(lane, block):
            names = (("rms_mix", "rms_mlp", "b_ada"), ("norm1_g_2", "norm2_g_2", "b_mod_2"))[block]
            for layer in range(2):
                for i, (name, n) in enumerate(zip(names, (8, 8, 48))):
                    param_rows(lane, 64 * layer + 8 * i, block, a[name][layer], n)

        R_POOL_B, R_POOL_LS = 10, 18
        got_pos = pool.load(pos_i, a["positions"][0].partition_broadcast(P), mark("d_pos"))
        modulation_rows(pool, 1)
        for half in range(2):
            for j, name in enumerate(("q_norm_swa", "k_norm_swa", "q_norm_moba", "k_norm_moba")):
                pool.load(rows[2 * j:2 * j + 2, 3, half * HD:(half + 1) * HD], a[name], mark("d_par3"))
            for j, name in enumerate(("attn_qg_2", "attn_kg_2")):
                pool.load(rows[8 + j:9 + j, 3, half * HD:(half + 1) * HD], a[name], mark("d_par3"))
        param_rows(pool, R_POOL_B, 3, a["pool_b_2"][0].rearrange("g c -> (g c)"), 8)
        param_rows(pool, R_POOL_LS, 3, a["pool_ls_2"][0], 8)
        N_ROWS = (P, P, 24, R_POOL_LS + 8)
        pool.load(sink[:], a["swa_sinks"].rearrange("l h -> (l h)").partition_broadcast(P), mark("d_small"))
        route_buf = bufs.take()[0]
        w_route = tmp[:, route_buf, 0:2 * DT * 20].rearrange("p (l k c) -> p l k c", l=2, c=20)
        for layer in range(2):
            pool.load(w_route[:, layer, :, 0:4], a["moe_wrg_2"][layer].rearrange("(k p) c -> p k c", p=P),
                      mark("d_small"))
            pool.load(w_route[:, layer, :, 4:20], a["moe_wre_2"][layer].rearrange("(k p) c -> p k c", p=P),
                      mark("d_small"))
            pool.load(b_route[:, layer, 0:4], a["moe_brg_2"][layer].partition_broadcast(P), mark("d_small"))
            got_small = pool.load(b_route[:, layer, 4:20], a["moe_bre_2"][layer].partition_broadcast(P),
                                  mark("d_small"))

        def unit_of(w, k0, c0, k=DT):
            return w[k0 * P:(k0 + k) * P, c0:c0 + UC].rearrange("(k p) c -> p k c", p=P)

        plan = []

        mod_items = []
        for layer in range(4):
            for chunk in ((1, 0, 2, 4, 3, 5)):
                for pair in range(4):
                    mod_items.append(("mod", layer, chunk, pair))

        def mlp_order():
            yield "up", 0, 0
            for g in range(4):
                for j in range(1, 4):
                    yield "up", g, j
                if g < 3:
                    yield "up", g + 1, 0
                else:
                    yield "down", 2, 3
                for j in range(3 if g == 2 else 4):
                    yield "down", g, j

        QKV_UNITS = (512 + 2 * 128 + 3 * 512) // UC
        gemms = []
        for l in range(2):
            for j in range(4352 // UC):
                gemms.append(("in", [(0, DT, unit_of(a["w_in"][l], 0, j * UC))]))
            for j in range(4):
                gemms.append(("o", [(0, 4, unit_of(a["w_o_swa"][l], 0, j * UC, 4)),
                                    (4, 4, unit_of(a["w_o_moba"][l], 0, j * UC, 4))]))
            for j in range(4):
                gemms.append(("out", [(0, DT, unit_of(a["w_out"][l], 0, j * UC))]))
            for what, g, j in mlp_order():
                src = unit_of(a["w_up"][l], 0, g * D + j * UC) if what == "up" else \
                    unit_of(a["w_down"][l], g * DT, j * UC)
                gemms.append((what, [(0, DT, src)]))
        gemms_per_layer = len(gemms) // 2
        for l in range(2):
            if l == 0:
                gemms.append(("pool", [(0, DT, unit_of(a["pool_w_2"][0].rearrange("g c d -> (g c) d"), 0, 0))]))
            else:
                for j in (4, 5, 0, 1, 2, 3):
                    gemms.append(("qkv", [(0, DT, unit_of(a["attn_wqkv_2"][0], 0, j * UC))]))
                for j in range(4):
                    gemms.append(("wo", [(0, DT, unit_of(a["attn_wo_2"][0], 0, j * UC))]))
            w_dn = a["moe_wd_2"][l].rearrange("e f d -> (e f) d")
            for g in range(4):
                for e in range(4 * g, 4 * g + 4):
                    gemms.append(("eg", [(0, DT, unit_of(a["moe_wg_2"][l, e], 0, 0))]))
                    gemms.append(("eu", [(0, DT, unit_of(a["moe_wu_2"][l, e], 0, 0))]))
                for j in range(4):
                    gemms.append(("ed", [(0, DT, unit_of(w_dn, g * DT, j * UC))]))

        def mod_pace(i):
            first_block = i < 2 * gemms_per_layer
            if first_block and i % gemms_per_layer < QKV_UNITS:
                return 0
            return 0.58 if first_block and i >= 30 else 0.8

        sent = 8
        due = sent
        plan += mod_items[:6]
        for i, (name, parts) in enumerate(gemms):
            due += mod_pace(i)
            want = min(len(mod_items), int(due))
            while sent < want:
                plan.append(mod_items[sent])
                sent += 1
            plan.append(("gemm", name, parts))
            if i == 0:
                plan += mod_items[6:sent]
        assert sent == len(mod_items)

        raw_mark = [mark(f"d_raw{i}") for i in range(RAW_SLOTS)]
        raw_free = [[] for _ in range(RAW_SLOTS)]
        split_free = [[] for _ in range(SPLIT_SLOTS)]
        closing = []

        def close_oldest():
            steps.hurry = True
            steps.advance(closing[0])
            steps.hurry = False

        accs = Ring(ACCS, close_oldest)
        fed = {"plan": 0, "gemm": 0, "used": 0}
        split_ready = {}
        mod_sources = [a["w_ada"][0], a["w_ada"][1], a["w_mod_2"][0], a["w_mod_2"][1]]
        cond_of = lambda layer, chunk: ([(0, layer)] if layer < 2 else
                                        [(1, layer)] + ([(2, layer + 2)] if layer == 2 or chunk < 2 else []))
        mod_acc, mod_ready = {}, {}
        mod_lane, mod_turn = {}, [0]
        cond_ready = []

        lows = []

        def feed_low(lane=None):
            g, slot, s, landed, t_hi = lows.pop(0)
            t_lo = []
            for half in range(2):
                k = slice(half * DT // 2, (half + 1) * DT // 2)
                part = slice(half * UNIT // 2, (half + 1) * UNIT // 2)
                t_lo.append(tt(lane or dve, w_lo[:, s, k].rearrange("p k c -> p (k c)"), raw[:, slot, part],
                               plain(w_hi[:, s, k].rearrange("p k c -> p (k c)")), ALU.subtract, [landed, t_hi]))
            raw_free[slot] = [t_hi, *t_lo]
            split_ready[g] = [t_hi, *t_lo]

        def feed():
            item = plan[fed["plan"]]
            slot = fed["plan"] % RAW_SLOTS
            if raw_free[slot] is None:
                feed_low()
            fed["plan"] += 1
            if item[0] == "gemm":
                flat_dst = raw[:, slot, :].rearrange("p (k c) -> p k c", c=UC)
                for k0, k, src in item[2]:
                    landed = sp.load(flat_dst[:, k0:k0 + k, :], src, raw_mark[slot], [raw_free[slot]])
                s = fed["gemm"] % SPLIT_SLOTS
                src = raw[:, slot, :]
                hi = w_hi[:, s].rearrange("p k c -> p (k c)")
                t_hi = fn(hi, src, ACT.Copy, [landed, split_free[s]])
                lows.append((fed["gemm"], slot, s, landed, t_hi))
                raw_free[slot] = None
                fed["gemm"] += 1
                if len(lows) > 1:
                    feed_low()
                return
            _, layer, chunk, pair = item
            dst = raw[:, slot, :].rearrange("p (k c) -> p k c", c=D)
            src = mod_sources[layer][2 * pair * P:(2 * pair + 2) * P, chunk * D:(chunk + 1) * D]
            landed = sp.load(dst, src.rearrange("(k p) c -> p k c", p=P), raw_mark[slot], [raw_free[slot]])
            last = []
            conds = cond_of(layer, chunk)
            for n_cond, (which, row) in enumerate(conds):
                if pair == 0:
                    mod_acc[row] = list(accs.take()) + [None]
                    mod_turn[0] += 1
                    mod_lane[row] = (mod_turn[0] > 2 and mod_turn[0] % 2) if len(conds) == 1 else n_cond
                buf, free, before = mod_acc[row]
                a_buf = acc[:, buf, :]
                for k in range(2):
                    s = cond[:, which, 2 * pair + k:2 * pair + k + 1]
                    first = pair == 0 and k == 0
                    if mod_lane[row] == 0:
                        if first:
                            before = ts(dve, a_buf, dst[:, k, :], s, None, ALU.mult, None,
                                        [landed, cond_ready, free])
                        else:
                            before = stt(a_buf, dst[:, k, :], s, a_buf, ALU.mult, ALU.add, [landed, before])
                    elif first:
                        before = fn(a_buf, dst[:, k, :], ACT.Copy, [landed, cond_ready, free], scale=s)
                    else:
                        t = fn(dst[:, k, :], dst[:, k, :], ACT.Copy, [landed, cond_ready, last], scale=s)
                        before = tt(pool, a_buf, a_buf, dst[:, k, :], ALU.add, [t, before])
                mod_acc[row][2] = before
                last = last + [before]
                if pair == 3:
                    closing.append(finish_mod(row, layer, chunk, buf, before))
                    steps.start(closing[-1])
            raw_free[slot] = last

        def finish_mod(row, layer, chunk, buf, summed):
            later = steps.products + 3
            while not steps.hurry and steps.products < later:
                yield
            closing.pop(0)
            b, free = banks.take()
            for t in range(DT):
                done = mm(psum[:, b, t:t + 1], acc[:, buf, t * P:(t + 1) * P], mean[:, 0:1], True, True,
                          [summed, free, got_cst], t == DT - 1)
            accs.give(buf, [done])
            yield
            col = mod[:, row, chunk * DT:(chunk + 1) * DT]
            base = 64 * (layer % 2)
            bias = par[:, layer // 2, base + 16 + chunk * DT:base + 16 + (chunk + 1) * DT]
            t = stt(col, psum[:, b, 0:DT], float(D), bias, ALU.mult, ALU.add, [done, par_ready])
            banks.give(b, [t])
            if chunk in (1, 4):
                g = par[:, layer // 2, base + (chunk // 4) * 8:base + (chunk // 4) * 8 + 8]
                t = stt(gain[:, 2 * row + chunk // 4, :], col, 1.0, g, ALU.add, ALU.mult, [t])
            mod_ready[row, chunk] = t

        def need_mod(row, chunk):
            while (row, chunk) not in mod_ready:
                if not steps.live:
                    feed()
                else:
                    steps.hurry = True
                    steps.tick()
                    steps.hurry = False
            return mod_ready[row, chunk]

        def unit(name):
            g = fed["used"]
            assert gemms[g][0] == name, (gemms[g][0], name)
            while fed["gemm"] < min(g + SPLIT_SLOTS, len(gemms)):
                feed()
            while lows and lows[0][0] <= g + 1:
                feed_low()
            fed["used"] += 1
            s = g % SPLIT_SLOTS
            return s, split_ready[g]

        def column(row, chunk, t):
            return mod[:, row, chunk * DT + t:chunk * DT + t + 1]

        def gain_col(row, chunk, t):
            return gain[:, 2 * row + chunk // 4, t:t + 1]

        def product(name, acts, n):
            s, ready = unit(name)
            k_banks = 2 * n // 512
            b, free = banks.take(k_banks)
            o = psum[:, b:b + k_banks, :].rearrange("p b c -> p (b c)").rearrange("p (m n) -> p m n", n=n)
            hi, lo, tickets = acts
            for i in range(DT + LAG):
                if i < DT:
                    steps.need(tickets, i)
                    for m in range(2):
                        mm(o[:, m], w_hi[:, s, i, m * P:(m + 1) * P], hi[:, i, 0:n], i == 0 and (m == 0 or k_banks == 2),
                           False, [ready[0], free, tickets[i][0]])
                if i >= LAG:
                    k = i - LAG
                    for m in range(2):
                        mm(o[:, m], w_hi[:, s, k, m * P:(m + 1) * P], lo[:, k, 0:n], False, False, [tickets[k][1]])
                        done = mm(o[:, m], w_lo[:, s, k, m * P:(m + 1) * P], hi[:, k, 0:n], False, k == DT - 1,
                                  [ready[1 + k // 4]], m == 1 and k == DT - 1)
            split_free[s] = [done]
            steps.products += 1
            if steps.live:
                steps.tick()
            return b, k_banks, o, done

        par_ready = [None] * 4

        def param_columns(block):
            n = N_ROWS[block]
            b, free = banks.take()
            t = tp(psum[:, b, 0:n], rows[0:n, block, :], ident[0:n, 0:n], [got_rows[block], got_ident, free], True)
            par_ready[block] = fn(par[:, block, 0:n], psum[:, b, 0:n], ACT.Copy, [t])
            banks.give(b, [par_ready[block]])

        param_columns(2)
        cvec = par[:, 2, 0:24].rearrange("p (v t) -> p v t", v=3)
        t = fn(cond_t[:], cvec, ACT.Tanh, [par_ready[2]], scale=0.5)
        t = stt(cond_t[:], cond_t[:], 1.0, cvec, ALU.add, ALU.mult, [t])
        cond_ready = [ts(dve, cond[:], cond_t[:], 0.5, None, ALU.mult, None, [t])]
        modulation_rows(act, 0)
        for _ in range(6):
            feed()

        def features(set_, t):
            b, free = banks.take()
            for i in range(2):
                done = tp(psum[:, b, i * P:(i + 1) * P], tokens_in[:, 2 * set_ + i, t * P:(t + 1) * P], ident,
                          [got_tok[2 * set_ + i], got_ident, free], i == 1)
            done = fn(x[:, t, set_ * S:(set_ + 1) * S], psum[:, b, 0:S], ACT.Copy, [done])
            banks.give(b, [done])
            return [done]

        x_ready = [features(0, t) for t in range(DT)]
        def sums_of_squares(n, paired=True):
            b, free = banks.take()
            return dict(n=n, b=b, free=free, queued=0, paired=paired)

        def add_squares(sums, t):
            n, b = sums["n"], sums["b"]
            sq = []
            for i in range(2):
                buf, bfree = bufs.take()
                sq.append((buf, fn(tmp[:, buf, 0:n], x[:, t + i, 0:n], ACT.Square,
                                   [x_ready[t + i], context_ready[t + i], bfree])))
            if t < DT - 2 and sums["paired"]:
                (b0, t0), (b1, t1) = sq
                t0 = tt(pool, tmp[:, b0, 0:n], tmp[:, b0, 0:n], tmp[:, b1, 0:n], ALU.add, [t0, t1])
                bufs.give(b1, [t0])
                sq = [(b0, t0)]
            yield
            for buf, landed in sq:
                for i in range(n // P):
                    done = mm(psum[:, b, i:i + 1], tmp[:, buf, i * P:(i + 1) * P], mean[:, 0:1],
                              sums["queued"] == 0 and i == 0, False, [landed, sums["free"], got_cst],
                              i == n // P - 1)
                bufs.give(buf, [done])
                sums["queued"] += 2 // len(sq)
            sums["done"] = done

        def rms_scale(n, sums=None):
            if sums is None:
                sums = sums_of_squares(n, paired=False)
                for t in range(0, DT, 2):
                    steps.start(add_squares(sums, t))
            while sums["queued"] < DT:
                steps.tick()
            b, done, tiles = sums["b"], sums["done"], n // P
            r = fn(rstd_col[:, 0:tiles], psum[:, b, 0:tiles], ACT.Sqrt, [done, rstd_seen], bias=eps)
            banks.give(b, [r])
            r = dve.do(lambda e: e.reciprocal(rstd_col[:, 0:tiles], rstd_col[:, 0:tiles]), [r])
            b, free = banks.take()
            for i in range(tiles):
                r = mm(psum[:, b, i * P:(i + 1) * P], rstd_col[:, i:i + 1].to_broadcast([P, P]), ident, i == 0,
                       True, [r, free], i == tiles - 1)
            rstd_seen[:] = [r]
            for _ in range(len(closing)):
                close_oldest()
            return b, r

        context_ready = [[]] * DT
        rstd_seen = []

        def modulate(rows_of_sets, chunk, hi, lo, sums=None, scale=None):
            n = S * len(rows_of_sets)
            rb, r = scale or rms_scale(n, sums)
            rstd = psum[:, rb, :]
            for row in rows_of_sets:
                need_mod(row, chunk + 1)
            tickets = [None] * DT

            def tile(t):
                buf, bfree = bufs.take()
                gs, his, los = [], [], []
                for i, row in enumerate(rows_of_sets):
                    c = slice(i * S, (i + 1) * S)
                    gs.append(stt(tmp[:, buf, c], x[:, t, c], gain_col(row, chunk + 1, t), rstd[:, c], ALU.mult,
                                  ALU.mult, [r, x_ready[t], bfree, mod_ready[row, chunk + 1]]))
                if t == DT - 1:
                    banks.give(rb, gs)
                while any((row, chunk) not in mod_ready for row in rows_of_sets):
                    yield
                for i, row in enumerate(rows_of_sets):
                    c = slice(i * S, (i + 1) * S)
                    his.append(fn(hi[:, t, c], tmp[:, buf, c], ACT.Identity, [gs[i], mod_ready[row, chunk]],
                                  bias=column(row, chunk, t)))
                if t % 2 if n == S else t in (2, 5):
                    for i, row in enumerate(rows_of_sets):
                        c = slice(i * S, (i + 1) * S)
                        v = ts(pool, tmp[:, buf, c], tmp[:, buf, c], column(row, chunk, t), None, ALU.add, None,
                               [gs[i], his[i], mod_ready[row, chunk]])
                        los.append(tt(pool, lo[:, t, c], tmp[:, buf, c], plain(hi[:, t, c]), ALU.subtract, [v]))
                    bufs.give(buf, his + los)
                    tickets[t] = [his, los]
                    return
                yield
                yield
                for i, row in enumerate(rows_of_sets):
                    c = slice(i * S, (i + 1) * S)
                    los.append(low(hi[:, t, c], lo[:, t, c], (tmp[:, buf, c], column(row, chunk, t), ALU.add),
                                   [his[i], mod_ready[row, chunk]]))
                bufs.give(buf, his + los)
                tickets[t] = [his, los]

            for t in range(DT):
                steps.start(tile(t))
                steps.tick()
            for row in rows_of_sets:
                need_mod(row, chunk)
            for t in range(DT):
                steps.need(tickets, t)
            return hi, lo, tickets

        def add_to_x(o, m0, done, chunk, rows_of_sets, b, k_banks, sums=None):
            seen = []
            for m in range(2):
                t = m0 + m
                parts = []
                for i, row in enumerate(rows_of_sets):
                    c = slice(i * S, (i + 1) * S)
                    parts.append(stt(x[:, t, c], o[:, m, c], column(row, chunk, t), x[:, t, c], ALU.mult, ALU.add,
                                     [done, x_ready[t], need_mod(row, chunk)]))
                x_ready[t] = parts
                seen += parts
            banks.give(b, seen, k_banks)
            if sums:
                steps.start(add_squares(sums, m0))

        def norm_rope(src, w, done, gain_ap, dest, rot, rope_w, after, src_done, ready, i, key):
            b1, f1 = bufs.take()
            sq = fn(tmp[:, b1, 0:w], src, ACT.Square, [done, f1])
            if not key:
                b2, f2 = bufs.take()
                n = fn(tmp[:, b2, 0:w], src, ACT.Copy, [done, f2, par_ready], scale=gain_ap)
                src_done(n)
            yield
            pb, pfree = banks.take()
            if key:
                ms = mm(psum[:, pb, 0:w], headmean, tmp[:, b1, 0:w], True, True, [sq, pfree], True)
                b2, f2 = bufs.take()
                r = fn(tmp[:, b2, 0:w], psum[:, pb, 0:w], ACT.Sqrt, [ms, f2], bias=eps)
                banks.give(pb, [r])
                r = dve.do(lambda e: e.reciprocal(tmp[:, b2, 0:w], tmp[:, b2, 0:w]), [r])
                n = stt(tmp[:, b2, 0:w], src, gain_ap, tmp[:, b2, 0:w], ALU.mult, ALU.mult, [r, par_ready])
                src_done(n)
                yield
            else:
                chunks = w // P
                for c in range(chunks):
                    ms = mm(psum[:, pb, 2 * c:2 * c + 2], tmp[:, b1, c * P:(c + 1) * P], headmean[:, 0:P:HD],
                            c == 0, True, [sq, pfree], c == chunks - 1)
                r_col = head_rstd[:, i, 0:2 * chunks]
                r = fn(r_col, psum[:, pb, 0:2 * chunks], ACT.Sqrt, [ms], bias=eps_scaled, scale=SCALE ** -2)
                banks.give(pb, [r])
                r = dve.do(lambda e: e.reciprocal(r_col, r_col), [r])
            squares, normed = b1, b2
            pb, pfree = banks.take()
            turned = mm(psum[:, pb, 0:rope_w], rot, tmp[:, normed, 0:rope_w], True, True, [n, pfree], True)
            tiles = rope_w // S
            wide = lambda ap: ap.rearrange("p (m n) -> p m n", n=S)
            tab = lambda k: spread(rope_tab[:, k, :], 1, [P, tiles, S])
            half = wide(tmp[:, normed, 0:rope_w])
            c = tt(pool, half, half, tab(0), ALU.mult, [turned, rope_ready])
            yield
            s = tt(dve, wide(tmp[:, squares, 0:rope_w]), wide(psum[:, pb, 0:rope_w]), tab(1), ALU.mult,
                   [turned, ms, rope_ready])
            banks.give(pb, [s])
            q = tt(pool, dest[:, 0:rope_w], tmp[:, normed, 0:rope_w], tmp[:, squares, 0:rope_w], ALU.add,
                   [s, c, after])
            ends = [q, r]
            if rope_w < w:
                ends.append(dve.do(lambda e: e.tensor_copy(dest[:, rope_w:w], tmp[:, normed, rope_w:w]), [n, after]))
            bufs.give(normed, ends)
            bufs.give(squares, ends)
            ready[i] = ends

        def keys_twice(src, w, done, gain_ap, rot, rope_w, src_done, dests, after, ready, i):
            kbuf, kfree = bufs.take()
            k = tmp[:, kbuf, 0:w]
            got = {}
            yield from norm_rope(src, w, done, gain_ap, k, rot, rope_w, kfree, src_done, got, i, True)
            yield
            for j, dup in enumerate((C_DUP0, C_DUP1)):
                pb, pfree = banks.take()
                d = mm(psum[:, pb, 0:w], cst[:, dup:dup + P], k, True, True, [got[i], pfree], True)
                ready[i + j] = fn(dests[j], psum[:, pb, 0:w], ACT.Copy, [d, after])
                banks.give(pb, [ready[i + j]])
            bufs.give(kbuf, [ready[i], ready[i + 1]])

        def values_by_token(src, w, done, dest, after, src_done, ready, i):
            b1, f1 = bufs.take()
            c = fn(tmp[:, b1, 0:w], src, ACT.Copy, [done, f1])
            src_done(c)
            yield
            pb, pfree = banks.take()
            for k in range(w // P):
                d = tp(psum[:, pb, k * P:(k + 1) * P], tmp[:, b1, k * P:(k + 1) * P], ident, [c, pfree],
                       k == w // P - 1)
            bufs.give(b1, [d])
            ready[i] = fn(dest, psum[:, pb, 0:w].rearrange("p (i c) -> p i c", c=P), ACT.Copy, [d, after])
            banks.give(pb, [ready[i]])

        def handed_back(b, times):
            got = []

            def back(ticket):
                got.append(ticket)
                if len(got) == times:
                    banks.give(b, got)
            return back

        def head_rows(first, head):
            tile = head // 2
            at_ = 4 * (tile % 2) + head % 2
            return head_rstd[:, first + tile // 2 * 2, at_:at_ + 3:2]

        def attend(heads, nk, fill, pring, pbuf, pk, causal):
            kt, nb = nk // P, nk // S
            keys = [P if causal else nk, nk]
            spans = [slice(0, keys[0]), slice(keys[0], keys[0] + keys[1])]
            blocks = [(qt, i) for i in range(kt) for qt in range(2) if i * P < keys[qt]]
            total = keys[0] + keys[1]
            held = {}
            flat_banks = lambda b: psum[:, b:b + nb, :].rearrange("p b c -> p (b c)")
            flat_bufs = lambda b: pbuf[:, b:b + pk, :].rearrange("p b c -> p (b c)")

            def score(h):
                d = heads[h]
                ready = [steps.need(*which) for which in d["ready"][:2]]
                b, free = banks.take(nb)
                o = flat_banks(b)
                for qt in range(2):
                    t = mm(o[:, spans[qt]], d["q"][:, qt * P:(qt + 1) * P], d["k"][:, 0:keys[qt]], True, True,
                           [free, ready], qt == 1)
                pb, pfree = pring.take(pk)
                p = flat_bufs(pb)
                st = stats[:, h, :]
                if d["mask"] is not None:
                    src = p
                    for qt in range(2):
                        m = stt(p[:, spans[qt]], o[:, spans[qt]], d["row_scale"][:, qt:qt + 1],
                                d["mask"][:, spans[qt]], ALU.mult, ALU.add, [t, pfree, got_masks])
                    t = m
                    banks.give(b, [t], nb)
                    pfree = []
                else:
                    src = o
                if causal:
                    for qt in range(2):
                        m = reduce(st[:, qt:qt + 1], src[:, spans[qt]], ALU.max, [t])
                    t = m
                else:
                    t = reduce(st[:, 0:2], src[:, 0:total].rearrange("p (q k) -> p q k", q=2), ALU.max, [t])
                if d["sink"] is not None:
                    t = ts(dve, st[:, 2:4], st[:, 0:2], d["sink"], -1.0, ALU.max, ALU.mult, [t, got_small])
                elif d["mask"] is not None:
                    t = ts(dve, st[:, 2:4], st[:, 0:2], -1.0, None, ALU.mult, None, [t])
                else:
                    t = stt(st[:, 2:4], st[:, 0:2], -1.0, d["row_scale"], ALU.mult, ALU.mult, [t])
                held[h] = [p, pb, t, b, src, pfree]

            def exponentials(h):
                d = heads[h]
                p, pb, t, b, src, pfree = held[h]
                st = stats[:, h, :]
                for qt in range(2):
                    scale = 1.0 if d["mask"] is not None else d["row_scale"][:, qt:qt + 1]
                    e = fn(p[:, spans[qt]], src[:, spans[qt]], ACT.Exp, [t, pfree], bias=st[:, 2 + qt:3 + qt],
                           scale=scale, accum=st[:, 4 + qt:5 + qt])
                if d["mask"] is None:
                    banks.give(b, [e], nb)
                if d["sink"] is not None:
                    e = fn(st[:, 6:8], st[:, 2:4], ACT.Exp, [t], bias=d["sink"])
                held[h] = [p, pb, e]

            def normalise(h):
                d = heads[h]
                p, pb, e = held[h]
                st = stats[:, h, :]
                if d["sink"] is not None:
                    e = tt(dve, st[:, 4:6], st[:, 4:6], st[:, 6:8], ALU.add, [e])
                r = dve.do(lambda e_: e_.reciprocal(st[:, 8:10], st[:, 4:6]), [e])
                for qt in range(2):
                    n = ts(pool, p[:, spans[qt]], p[:, spans[qt]], st[:, 8 + qt:9 + qt], None, ALU.mult, None,
                           [r, e])
                held[h] = [p, pb, n]

            def turn(h):
                p, pb, n = held[h]
                b, free = banks.take(nb)
                o = flat_banks(b)
                for j, (qt, i) in enumerate(blocks):
                    first = spans[qt].start + i * P
                    t = tp(o[:, j * P:(j + 1) * P], p[:, first:first + P], ident, [free, n], j == len(blocks) - 1)
                pring.give(pb, [t], pk)
                tb, tfree = pring.take(pk)
                pt = flat_bufs(tb)
                c = fn(pt[:, 0:total], o[:, 0:total], ACT.Copy, [t, tfree])
                banks.give(b, [c], nb)
                held[h] = [pt, tb, c]

            def weigh(h):
                d = heads[h]
                pt, tb, c = held.pop(h)
                ready = steps.need(*d["ready"][2])
                if h % 2 == 0:
                    held["o"] = banks.take()
                b, free = held["o"]
                base, at_ = HD * (h % 2), 0
                for i in range(kt):
                    q0 = i * P if causal else 0
                    t = mm(psum[base:base + HD, b, q0:S], d["v"](i), pt[:, at_:at_ + S - q0], i == 0, i == kt - 1,
                           [free, c, ready], i == kt - 1)
                    at_ += S - q0
                pring.give(tb, [t], pk)
                if h % 2:
                    steps.start(split_output(d["tile"], b, t))

            def split_output(j, b, t):
                hi = fn(u_hi1[:, j, :], psum[:, b, 0:S], ACT.Copy, [t, o_free])
                yield
                lo = low(u_hi1[:, j, :], u_lo1[:, j, :], psum[:, b, 0:S], [hi, o_free])
                banks.give(b, [hi, lo])
                o_ready[j] = [hi, lo]

            o_ready = [None] * DT
            n = len(heads)
            for i in range(n + 5):
                if i < n:
                    score(i)
                if 0 <= i - 3 < n:
                    turn(i - 3)
                if i < n:
                    exponentials(i)
                if 0 <= i - 5 < n:
                    weigh(i - 5)
                fill(i)
                if i < n:
                    normalise(i)
                if steps.live:
                    steps.tick()
            return u_hi1, u_lo1, o_ready

        def rotary_tables():
            C1 = 6.28125
            C2 = float(np.float32(2 * np.pi - C1).view(np.uint32) & np.uint32(0xFFFFF000))
            C2 = float(np.array([int(C2)], np.uint32).view(np.float32)[0])
            C3 = float(2 * np.pi - C1 - C2)
            MAGIC = 1.5 * 2.0 ** 23
            LIMIT = 3.1415925
            rope_bufs, rope_frees = zip(*(bufs.take() for _ in range(3)))
            pf, ang, turns = (tmp[:, b, 0:S] for b in rope_bufs)
            t = dve.do(lambda e: e.tensor_copy(pf, pos_i), [got_pos, *rope_frees])
            bufs.give(pos_buf, [t])
            t = ts(dve, ang, pf, cst[:, C_MISC:C_MISC + 1], None, ALU.mult, None, [t, got_cst])
            t = ts(dve, turns, ang, 1.0 / (2 * np.pi), None, ALU.mult, None, [t])
            t = ts(dve, turns, turns, MAGIC, None, ALU.add, None, [t])
            t = ts(dve, turns, turns, -MAGIC, None, ALU.add, None, [t])
            for c in (C1, C2, C3):
                t = stt(ang, turns, -c, ang, ALU.mult, ALU.add, [t])
            t = ts(dve, ang, ang, LIMIT, -LIMIT, ALU.min, ALU.max, [t])
            sin_t = fn(rope_tab[:, 1, :], ang, ACT.Sin, [t])
            t = ts(dve, pf, ang, float(np.pi / 2), None, ALU.add, None, [t])
            t = ts(dve, turns, pf, float(np.pi), -2 * float(np.pi), ALU.is_gt, ALU.mult, [t])
            t = tt(dve, pf, pf, turns, ALU.add, [t])
            t = ts(dve, pf, pf, LIMIT, -LIMIT, ALU.min, ALU.max, [t])
            rope_ready = fn(rope_tab[:, 0, :], pf, ACT.Sin, [t, sin_t])
            for b in rope_bufs:
                bufs.give(b, [rope_ready, t])
            return rope_ready

        small_gain = lambda row: par[:, 3, row:row + 1]
        sums, scale = None, rms_scale(S)
        param_columns(0)
        while fed["plan"] < 9:
            feed()
            if lows:
                feed_low(pool)
        for block in (1, 3):
            param_columns(block)
        bufs.give(row_buf, par_ready)
        behind = mod_acc[0][2]
        tokens(pool, 2, [behind])
        tokens(pool, 3)
        got_masks = pool.load(masks[:].rearrange("p a c -> p (a c)"), a["consts"][:, C_CAUSAL:C_CAUSAL + 2 * MASK_W],
                              mark("d_masks"))
        for l in range(2):
            h = modulate([l], 0, h_hi1, h_lo1, sums, scale)
            scale = None
            if l == 0:
                last_readers = []
            rot1 = cst[:, C_ROT1:C_ROT1 + P]
            flat2 = lambda o: o.rearrange("p m n -> p (m n)")
            qk_ready = [None] * 14
            tab_q = lambda j: qk[:, j:j + 2, :].rearrange("p m n -> p (m n)")
            va = v_tok[:, 0:256].rearrange("p (i c) -> p i c", c=P)
            vb = v_tok[:, 256:1280].rearrange("p (i c) -> p i c", c=512)
            va_ready, vb_ready = [None], [None] * 4

            def queries(first, row):
                b, kb, o, done = product("in", h, S)
                steps.start(norm_rope(flat2(o), 512, done, small_gain(row), tab_q(first), rot1, 512,
                                      last_readers, handed_back(b, 1), qk_ready, first, first >= 10))

            queries(0, l)
            if l == 0:
                rope_ready = rotary_tables()
                w_flat = tmp[:, route_buf, 0:2 * DT * 20]
                flat_route = lambda ap: ap.rearrange("p l c -> p (l c)")
                t = fn(flat_route(w_route_hi[:]), w_flat, ACT.Copy, [got_small])
                pick_ready = fn(pick[:], ident[0:N_EXP, 0:N_EXP], ACT.Copy, [got_ident])
                route_split = [t, low(flat_route(w_route_hi[:]), flat_route(w_route_lo[:]), w_flat, [got_small, t])]
                bufs.give(route_buf, route_split)
            queries(2, l)
            if l == 0:
                o_free = context_ready = [features(1, t) for t in range(DT)]
            b, kb, o, done = product("in", h, S)
            back = handed_back(b, 2)
            steps.start(keys_twice(o[:, 0], S, done, small_gain(2 + l), rot1, S, back,
                                   [qk[:, 4, :], qk[:, 5, :]], last_readers, qk_ready, 4))
            steps.start(values_by_token(o[:, 1], S, done, va, last_readers, back, va_ready, 0))
            for j in range(2):
                queries(6 + 2 * j, 4 + l)
            for j in range(2):
                queries(10 + 2 * j, 6 + l)
            for j in range(2):
                b, kb, o, done = product("in", h, S)
                back = handed_back(b, 2)
                for m in range(2):
                    f = (2 * j + m) * P
                    steps.start(values_by_token(o[:, m], S, done, vb[:, :, f:f + P], last_readers, back,
                                                vb_ready, 2 * j + m))

            heads = []
            for i in range(8):
                rows_ = slice(HD * (i % 2), HD * (i % 2) + HD)
                kv = i // 4
                heads.append(dict(q=qk[rows_, i // 2, :], k=qk[rows_, 4 + kv, :], tile=i // 2, mask=masks[:, 1, :],
                                  v=lambda kt, kv=kv: va[:, kt, kv * HD:(kv + 1) * HD],
                                  sink=sink[:, 8 * l + i:8 * l + i + 1],
                                  row_scale=head_rows(0, i),
                                  ready=[(qk_ready, i // 4 * 2), (qk_ready, 4 + kv), (va_ready, 0)]))
            for i in range(8):
                rows_ = slice(HD * (i % 2), HD * (i % 2) + HD)
                heads.append(dict(q=qk[rows_, 6 + i // 2, :], k=qk[rows_, 10 + i // 2, :], tile=4 + i // 2,
                                  v=lambda kt, i=i: vb[:, kt, i * HD:(i + 1) * HD], mask=masks[:, 0, :], sink=None,
                                  row_scale=head_rows(6, i),
                                  ready=[(qk_ready, 6 + i // 4 * 2), (qk_ready, 10 + i // 4 * 2),
                                         (vb_ready, i // 2)]))
            gate_ready = []

            def fill(i):
                if i in (0, 2, 4, 6, 8, 11, 14, 17):
                    b, kb, o, done = product("in", h, S)
                    j = len(gate_ready)
                    t = fn(gate_tanh[:, 2 * j:2 * j + 2, :], o, ACT.Tanh, [done, h_free], scale=0.5)
                    banks.give(b, [t])
                    gate_ready.append(t)

            h_free = last_readers
            att = attend(heads, S, fill, bufs, tmp, 1, True)
            assert len(gate_ready) == 8
            mixed_ready = [None] * DT

            def mix(j, outs):
                bb, bfree = bufs.take(2)
                ya = tmp[:, bb, :].rearrange("p (m n) -> p m n", n=S)
                yb = tmp[:, bb + 1, :].rearrange("p (m n) -> p m n", n=S)
                t = []
                for part, y in enumerate((ya, yb)):
                    b, o, done = outs[part]
                    g = gate_tanh[:, 8 * part + 2 * j:8 * part + 2 * j + 2, :]
                    t.append(stt(y, g, 1.0, o, ALU.add, ALU.mult, [done, gate_ready[4 * part + j], bfree]))
                    banks.give(b, [t[-1]])
                t = tt(dve, ya, ya, yb, ALU.add, [t])
                c = slice(2 * j, 2 * j + 2)
                hi = fn(h_hi1[:, c, :], ya, ACT.Copy, [t], scale=0.5)
                yield
                lo = low(h_hi1[:, c, :], h_lo1[:, c, :], (ya, 0.5, ALU.mult), [hi])
                bufs.give(bb, [hi, lo], 2)
                mixed_ready[2 * j] = mixed_ready[2 * j + 1] = [hi, lo]

            for j in range(4):
                s, ready = unit("o")
                outs = []
                for part in range(2):
                    b, free = banks.take()
                    o = psum[:, b, :].rearrange("p (m n) -> p m n", n=S)
                    for m in range(2):
                        for i in range(4):
                            k = 4 * part + i
                            steps.need(att[2], k)
                            wh, wl = w_hi[:, s, k, m * P:(m + 1) * P], w_lo[:, s, k, m * P:(m + 1) * P]
                            xh, xl = att[0][:, k, :], att[1][:, k, :]
                            mm(o[:, m], wh, xh, i == 0, False, [ready[0], free, att[2][k]])
                            mm(o[:, m], wh, xl, False, False)
                            done = mm(o[:, m], wl, xh, False, i == 3, [ready[1 + part]], m == 1 and i == 3)
                    outs.append((b, o, done))
                split_free[s] = [done]
                steps.start(mix(j, outs))
                steps.products += 1
                steps.tick()
            sums = sums_of_squares(S)
            for j in range(4):
                b, kb, o, done = product("out", (h_hi1, h_lo1, mixed_ready), S)
                add_to_x(o, 2 * j, done, 2, [l], b, kb, sums)

            h = modulate([l], 3, h_hi1, h_lo1, sums)

            def squared_relu(b, o, done, g, j, u_ready):
                u_hi, u_lo = u_parts[g % 2]
                buf, bfree = bufs.take()
                r = tmp[:, buf, :].rearrange("p (m n) -> p m n", n=S)
                t = fn(r, o, ACT.Relu, [done, bfree])
                yield
                t = stt(r, o, 0.0, r, ALU.max, ALU.mult, [t])
                banks.give(b, [t])
                c = slice(2 * j, 2 * j + 2)
                hi = fn(u_hi[:, c, :], r, ACT.Copy, [t, done])
                yield
                lo = low(u_hi[:, c, :], u_lo[:, c, :], r, [hi])
                bufs.give(buf, [hi, lo])
                u_ready[2 * j] = u_ready[2 * j + 1] = [hi, lo]

            u_parts = ((u_hiB, u_loB), (u_hi1, u_lo1))
            u_ready = [[None] * DT for _ in range(4)]
            for what, g, j in mlp_order():
                if what == "up":
                    b, kb, o, done = product("up", h, S)
                    steps.start(squared_relu(b, o, done, g, j, u_ready[g]))
                else:
                    b, kb, o, done = product("down", (*u_parts[g % 2], u_ready[g]), S)
                    if (g, j) == (3, 0):
                        sums = sums_of_squares(S if l == 0 else S2)
                    add_to_x(o, 2 * j, done, 5, [l], b, kb, sums if g == 3 else None)
                    if l == 1 and (g, j) == (2, 3):
                        got_window = pool.load(window_tab[:].rearrange("p g i n -> p (g i n)"),
                                               a["consts"][:, C_POOL:C_POOL + 2048], mark("d_window"), [done])
                        rope_load = pool.load(rope_tab[:].rearrange("p a c -> p (a c)"),
                                              a["consts"][:, C_COS2:C_COS2 + 512], mark("d_rope"), [done])
            last_readers = [done]
            o_free = [done]

        def route(layer, n, h, gates):
            T = n // P
            b, free = banks.take()
            for k in range(DT):
                for part in range(4):
                    w = (w_route_hi, w_route_lo)[part // 2][:, layer, k * 20:(k + 1) * 20]
                    t = mm(psum[0:20, b, 0:n], w, h[part % 2][:, k, :], k == 0 and part == 0,
                           k == DT - 1 and part == 3, [free, h[2][k], route_split], k == DT - 1 and part == 3)
            buf, bfree = bufs.take()
            t = fn(tmp[0:20, buf, 0:n], psum[0:20, b, 0:n], ACT.Copy, [t, bfree])
            banks.give(b, [t])
            by_expert = buf
            yield
            b, free = banks.take()
            lg_p = psum[:, b, 0:T * 20].rearrange("p (i c) -> p i c", c=20)
            for i in range(T):
                t_ = tp(lg_p[:, i], tmp[0:20, by_expert, i * P:(i + 1) * P], ident[0:20, 0:20], [t, free], i == T - 1)
            t = t_
            bufs.give(by_expert, [t])
            yield
            buf, bfree = bufs.take()
            area = [0]

            def room(*shape):
                size = int(np.prod(shape))
                ap = tmp[:, buf, area[0]:area[0] + size]
                area[0] += size
                assert area[0] <= 512
                if len(shape) == 2:
                    return ap.rearrange("p (i c) -> p i c", c=shape[1])
                return ap

            N4, N16 = [P, T, 4], [P, T, N_EXP]
            lg = room(T, 20)
            t = tt(dve, lg, lg_p, spread(b_route[:, layer, :], 1, [P, T, 20]), ALU.add, [t, got_small, bfree])
            banks.give(b, [t])
            gl, el = lg[:, :, 0:4], lg[:, :, 4:20]
            iota4 = spread(cst[:, C_IOTA:C_IOTA + 4], 1, N4)
            iota16 = spread(cst[:, C_IOTA:C_IOTA + N_EXP], 1, N16)

            def first_of_max(v, wide, iota, t):
                m, d, at_, one, least = room(T), room(T, wide), room(T, wide), room(T, wide), room(T)
                shape = [P, T, wide]
                t = reduce(m, v, ALU.max, [t])
                td = tt(dve, d, v, spread(m, 2, shape), ALU.subtract, [t])
                t = ts(dve, one, d, 0.0, -64.0, ALU.is_ge, ALU.mult, [td])
                t = tt(dve, at_, one, iota, ALU.add, [t])
                t = reduce(least, at_, ALU.min, [t])
                t = tt(dve, one, at_, spread(least, 2, shape), ALU.is_equal, [t])
                return m, d, one, t, td

            _, d, group, t, td = first_of_max(gl, 4, iota4, t)
            eg, sg, gw = room(T, 4), room(T), room(T)
            e = fn(eg, d, ACT.Exp, [td])
            e = reduce(sg, eg, ALU.add, [e])
            gw_t = dve.do(lambda e_: e_.reciprocal(gw, sg), [e])
            pen = room(T, 4)
            t = ts(dve, pen, group, -1.0, 1e30, ALU.add, ALU.mult, [t])
            by_group = lambda ap: ap.rearrange("p i (g c) -> p i g c", c=4)
            inside = room(T, N_EXP)
            for i in range(T):
                ti = tt(dve, inside[:, i].rearrange("p (g c) -> p g c", c=4),
                        el[:, i].rearrange("p (g c) -> p g c", c=4), spread(pen[:, i], 2, [P, 4, 4]), ALU.add, [t])
            t = ti
            m1, _, one1, t, _ = first_of_max(inside, N_EXP, iota16, t)
            t = stt(inside, one1, -2e30, inside, ALU.mult, ALU.add, [t])
            area2, fr2 = bufs.take()
            first_buf = buf
            buf, area[0] = area2, 0
            t2 = [t, fr2]
            m2, _, one2, t, _ = first_of_max(inside, N_EXP, iota16, t2)
            dm, ex, den = room(T), room(T), room(T)
            td = tt(dve, dm, m2, m1, ALU.subtract, [t])
            e = fn(ex, dm, ACT.Exp, [td])
            td = ts(dve, den, ex, 1.0, None, ALU.add, None, [e])
            td = dve.do(lambda e_: e_.reciprocal(den, den), [td])
            td = tt(dve, den, den, gw, ALU.mult, [td, gw_t])
            t1 = tt(dve, one1, one1, spread(den, 2, N16), ALU.mult, [td, t])
            td = tt(dve, den, den, ex, ALU.mult, [td, t1])
            t2 = tt(dve, one2, one2, spread(den, 2, N16), ALU.mult, [td, t])
            t = tt(dve, one1, one1, one2, ALU.add, [t1, t2])
            yield
            b, free = banks.take()
            for i in range(T):
                d_ = tp(psum[0:N_EXP, b, i * P:(i + 1) * P], one1[:, i, :], ident, [t, free], i == T - 1)
            bufs.give(first_buf, [d_])
            bufs.give(area2, [d_])
            buf, bfree = bufs.take()
            half = tmp[0:N_EXP, buf, 0:n]
            g = fn(half, psum[0:N_EXP, b, 0:n], ACT.Copy, [d_, bfree], scale=0.5)
            banks.give(b, [g])
            g = fn(gates_hi[:, 0:n], half, ACT.Copy, [g, done_all])
            g = [g, low(gates_hi[:, 0:n], gates_lo[:, 0:n], half, [g, done_all])]
            bufs.give(buf, g)
            yield
            gates[0] = g

        outs = []

        def store(half):
            for i in range(2):
                buf, bfree = bufs.take()
                b, free = banks.take()
                for t in range(4):
                    k = 4 * half + t
                    d = tp(psum[:, b, t * P:(t + 1) * P], x[:, k, i * P:(i + 1) * P], ident, [x_ready[k], free],
                           t == 3)
                c = fn(tmp[:, buf, :], psum[:, b, :], ACT.Copy, [d, bfree])
                banks.give(b, [c])
                outs.append(sp.load(out[0, i * P:(i + 1) * P, 512 * half:512 * (half + 1)], tmp[:, buf, :],
                                    mark(f"d_out{2 * half + i}"), [c]))
                bufs.give(buf, [outs[-1]])

        def moe(layer, rows_of_sets, sums, next_tokens):
            sets = len(rows_of_sets)
            n = S * sets
            h_bufs = (h_hi1, h_lo1) if sets == 1 else (h_hi2, h_lo2)
            u_bufs = (u_hi1, u_lo1) if sets == 1 else (u_hi2, u_lo2)
            h = modulate(rows_of_sets, 3, *h_bufs, sums)
            sums = None
            gates = [None]

            def gated(expert, i, ba, oa, da, bb, ob, db, u_ready):
                buf, bfree = bufs.take(sets)
                u = tmp[:, buf:buf + sets, :].rearrange("p b c -> p (b c)").rearrange("p (m n) -> p m n", n=n)
                t = fn(u, oa, ACT.Tanh, [da, bfree], scale=0.5)
                t = stt(u, u, 1.0, oa, ALU.add, ALU.mult, [t])
                banks.give(ba, [t], sets)
                t = tt(dve, u, u, ob, ALU.mult, [t, db])
                banks.give(bb, [t], sets)
                while gates[0] is None:
                    yield
                pb, pfree = banks.take()
                row = pick[:, expert:expert + 1].to_broadcast([N_EXP, P])
                mm(psum[:, pb, 0:n], row, gates_hi[:, 0:n], True, False, [gates, pfree, pick_ready])
                gd = mm(psum[:, pb, 0:n], row, gates_lo[:, 0:n], False, True, [], True)
                t = tt(dve, u, u, spread(psum[:, pb, 0:n], 1, [P, 2, n]), ALU.mult, [t, gd])
                banks.give(pb, [t])
                c = slice(2 * i, 2 * i + 2)
                hi = fn(u_bufs[0][:, c, :], u, ACT.Copy, [t])
                yield
                lo = low(u_bufs[0][:, c, :], u_bufs[1][:, c, :], u, [hi])
                bufs.give(buf, [hi, lo], sets)
                u_ready[2 * i] = u_ready[2 * i + 1] = [hi, lo]

            for g in range(4):
                u_ready = [None] * DT
                for i in range(4):
                    expert = 4 * g + i
                    ba, kb, oa, da = product("eg", h, n)
                    if expert == 0:
                        steps.start(route(layer, n, h, gates))
                    bb, _, ob, db = product("eu", h, n)
                    steps.start(gated(expert, i, ba, oa, da, bb, ob, db, u_ready))
                for j in range(4):
                    b, kb, o, done = product("ed", (*u_bufs, u_ready), n)
                    if (g, j) == (3, 0) and next_tokens:
                        sums = sums_of_squares(next_tokens)
                    add_to_x(o, 2 * j, done, 5, rows_of_sets, b, kb, sums)
                    if not next_tokens and g == 3 and j > 1:
                        store(j - 2)
            return [done], sums

        done_all = []
        sets = [2, 4]
        for t in range(DT):
            x_ready[t] = x_ready[t] + context_ready[t]
        h = modulate(sets, 0, h_hi2, h_lo2, sums)
        need_mod(2, 2)
        need_mod(4, 2)
        for i, row in enumerate(sets):
            scale_ready = tt(dve, cond_t[:, i, :], mod[:, row, 2 * DT:3 * DT], par[:, 3, R_POOL_LS:R_POOL_LS + DT], ALU.mult,
                             [mod_ready[row, 2], cond_ready])
        s, ready = unit("pool")
        turned = []
        for pair in range(2):
            for i in range(4):
                b, free = banks.take()
                for g in range(2):
                    for k in range(4 * pair + 2 * g, 4 * pair + 2 * g + 2):
                        steps.need(h[2], k)
                        o = psum[:, b, g * UC:(g + 1) * UC]
                        hh, hl = (part[:, k, i * P:(i + 1) * P] for part in h[:2])
                        mm(o, hh, w_hi[:, s, k, :], g == 0 and k % 2 == 0, False, [ready[0], free, h[2][k]])
                        mm(o, hl, w_hi[:, s, k, :], False, False)
                        done = mm(o, hh, w_lo[:, s, k, :], False, k % 2 == 1, [ready[1 + k // 4]], g == 1 and k % 2 == 1)
                dst = by_token[:, i, 2 * pair * UC:2 * (pair + 1) * UC]
                if i % 2:
                    t = dve.do(lambda e, dst=dst, b=b: e.tensor_copy(dst, psum[:, b, :]), [done, last_readers])
                else:
                    t = fn(dst, psum[:, b, :], ACT.Copy, [done, last_readers])
                banks.give(b, [t])
                turned.append(t)
        split_free[s] = [done]
        sums = sums_of_squares(S2, paired=False)
        REACH = 1 << 3
        for t in range(DT):
            b, free = banks.take()
            for i in range(4):
                set_, tile_ = i // 2, i % 2
                n0, n1 = (0, P + REACH) if tile_ == 0 else (P - REACH, S)
                done = mm(psum[:, b, set_ * S + n0:set_ * S + n1], by_token[:, i, t * P:(t + 1) * P],
                          window_tab[:, t // 2, tile_, n0:n1], i == 0, tile_ == 1,
                          [free, turned[4 * (t // 4) + i], got_window], i == 3)
            buf, bfree = bufs.take()
            parts, seen = [], []
            for i in range(2):
                c = slice(i * S, (i + 1) * S)
                q = ts(dve, tmp[:, buf, c], psum[:, b, c], par[:, 3, R_POOL_B + t:R_POOL_B + t + 1], cond_t[:, i, t:t + 1], ALU.add,
                       ALU.mult, [done, bfree, scale_ready])
                seen.append(q)
                parts.append(tt(dve, x[:, t, c], tmp[:, buf, c], x[:, t, c], ALU.add, [q, x_ready[t]]))
            x_ready[t] = parts
            bufs.give(buf, parts)
            banks.give(b, seen)
            if t % 2:
                steps.start(add_squares(sums, t - 1))
        done_all, sums = moe(0, sets, sums, S2)

        h = modulate([3, 5], 0, h_hi2, h_lo2, sums)
        rope_ready = rope_load
        rot2 = cst[:, C_ROT2:C_ROT2 + P]
        q_ready = [None] * 8
        b, kb, o, done = product("qkv", h, S2)
        k_ready = [None] * 12
        for m in range(2):
            steps.start(keys_twice(o[:, m], S2, done, small_gain(9), rot2, S, handed_back(b + m, 1),
                                   [k_att[:, 2 * m, :], k_att[:, 2 * m + 1, :]], [done], k_ready, 8 + 2 * m))
        vv = v_tok[:, 0:1024].rearrange("p (i c) -> p i c", c=256)
        b, kb, o, done = product("qkv", h, S2)
        v_ready = [None] * 2
        for m in range(2):
            steps.start(values_by_token(o[:, m], S2, done, vv[:, :, m * P:(m + 1) * P], [], handed_back(b + m, 1),
                                        v_ready, m))
        for j in range(4):
            b, kb, o, done = product("qkv", h, S)
            steps.start(norm_rope(o.rearrange("p m n -> p (m n)"), 512, done, small_gain(8),
                                  q_att[:, 2 * j:2 * j + 2, :].rearrange("p m n -> p (m n)"), rot2, 512, [done],
                                  handed_back(b, 1), q_ready, 2 * j, False))
        heads = []
        for i in range(16):
            rows_ = slice(HD * (i % 2), HD * (i % 2) + HD)
            kv = i // 4
            heads.append(dict(q=q_att[rows_, i // 2, :], k=k_att[rows_, kv, :], tile=i // 2, mask=None, sink=None,
                              v=lambda kt, kv=kv: vv[:, kt, kv * HD:(kv + 1) * HD],
                              row_scale=head_rows(0, i), ready=[(q_ready, i // 4 * 2), (k_ready, 8 + kv), (v_ready, kv // 2)]))
        o_free = [done]
        rooms = Ring(8, steps.tick)
        rooms.free = [[done] for _ in range(8)]
        att = attend(heads, S2, lambda i: None, rooms, att_room, 1, False)
        sums = sums_of_squares(S)
        for j in range(4):
            b, kb, o, done = product("wo", att, S)
            add_to_x(o, 2 * j, done, 2, [3], b, kb, sums)
        moe(1, [3], sums, None)
        assert fed["plan"] == len(plan) and fed["used"] == len(gemms)

        sp.wait(*outs)

        block = ctx.enter_context(nc.Block())

        def run(lane):
            def body(engine):
                for step in lane.steps:
                    step(engine)
            return body

        block.sync(run(sp))
        block.tensor(run(pe))
        block.scalar(run(act))
        block.vector(run(dve))
        block.gpsimd(run(pool))


INPUTS = ["x", "c", "positions", "rms_mix", "rms_mlp", "w_ada", "b_ada", "w_in", "q_norm_swa", "k_norm_swa",
          "q_norm_moba", "k_norm_moba", "swa_sinks", "w_o_swa", "w_o_moba", "w_out", "w_up", "w_down", "c_2",
          "ctx_2", "c_ctx_2", "w_mod_2", "b_mod_2", "norm1_g_2", "norm2_g_2", "pool_w_2", "pool_b_2",
          "pool_ls_2", "attn_wqkv_2", "attn_qg_2", "attn_kg_2", "attn_wo_2", "moe_wrg_2", "moe_brg_2",
          "moe_wre_2", "moe_bre_2", "moe_wg_2", "moe_wu_2", "moe_wd_2"]


def kernel(**inputs):
    import concourse.bacc as bacc
    from concourse.bass_utils import run_bass_kernel_spmd

    nc = bacc.Bacc("TRN2", target_bir_lowering=False, num_devices=1, dynamic_dma_scratch_size=8192)
    arrays = {f"in_{name}": np.ascontiguousarray(inputs[name]) for name in INPUTS}
    arrays["in_consts"] = constants()
    aps = {}
    for name, arr in arrays.items():
        aps[name[3:]] = nc.dram_tensor(name, arr.shape, mybir.dt.from_np(arr.dtype), kind="ExternalInput").ap()
    out = nc.dram_tensor("out", (1, S, D), F32, kind="ExternalOutput").ap()
    build(nc, aps, out)
    result = run_bass_kernel_spmd(nc, [arrays], core_ids=[0])
    return result.results[0]["out"]
```
